# Optimizing a Trainium2 kernel written in Bass

```python
import math
import jax, jax.numpy as jnp
from jax import lax
import numpy as np

D_MODEL = 1024
BATCH = 1
SEQ = 1024
DEPTH = 1

MEM_LEN = 256
CONV_CH = D_MODEL // 4
CONV_K = 3
DIFF_HEADS = 4
DIFF_QK_DIM = D_MODEL // 16
DIFF_V_DIM = 2 * DIFF_QK_DIM
MEM_HEADS = 4
MEM_HEAD_DIM = D_MODEL // 16
DIFF_QK_TOTAL = DIFF_HEADS * 2 * DIFF_QK_DIM
DIFF_V_TOTAL = DIFF_HEADS * DIFF_V_DIM
MEM_TOTAL = MEM_HEADS * MEM_HEAD_DIM
IN_WIDTH = 3 * CONV_CH + 2 * DIFF_QK_TOTAL + DIFF_V_TOTAL + MEM_TOTAL
MIX_WIDTH = CONV_CH + DIFF_V_TOTAL + MEM_TOTAL
IN_SPLITS = (CONV_CH, 2 * CONV_CH, 3 * CONV_CH,
             3 * CONV_CH + DIFF_QK_TOTAL,
             3 * CONV_CH + 2 * DIFF_QK_TOTAL,
             3 * CONV_CH + 2 * DIFF_QK_TOTAL + DIFF_V_TOTAL)
N_BUCKETS = 32
MAX_DISTANCE = 128
Q_BLOCK = 128
N_EXPERTS = 32
TOP_K = 4
D_EXPERT = D_MODEL
SWIGLU_ALPHA = 1.702
SWIGLU_LIMIT = 7.0
EXPERT_BLOCK = 128
EPS = 1e-5
NEG = -1e30

kernel_name = "hymba_conv_diffattn_mem_moe_block"

def rmsnorm(x, g):
    xf = x.astype(jnp.float32)
    y = xf * lax.rsqrt(jnp.mean(xf * xf, axis=-1, keepdims=True) + EPS)
    return (y * g.astype(jnp.float32)).astype(x.dtype)

def causal_short_conv(u, w):
    rhs = w[:, None, :].astype(u.dtype)
    return lax.conv_general_dilated(
        u, rhs, window_strides=(1,), padding=[(CONV_K - 1, 0)],
        dimension_numbers=("NWC", "WIO", "NWC"), feature_group_count=u.shape[-1])

def t5_bucket(n):
    max_exact = N_BUCKETS // 2
    nf = jnp.maximum(n, 1).astype(jnp.float32)
    large = max_exact + (jnp.log(nf / max_exact) / math.log(MAX_DISTANCE / max_exact)
                         * (N_BUCKETS - max_exact)).astype(jnp.int32)
    large = jnp.minimum(large, N_BUCKETS - 1)
    return jnp.where(n < max_exact, n, large)

def diff_attention(q, k, v, lam, rel_bias):
    S = q.shape[1]
    scale = DIFF_QK_DIM ** -0.5
    outs = []
    for i in range(S // Q_BLOCK):
        q0 = i * Q_BLOCK
        kv_len = q0 + Q_BLOCK
        qb = q[:, q0:kv_len]
        kb = k[:, :kv_len]
        vb = v[:, :kv_len]
        s = jnp.einsum("bqhcd,bkhcd->bhcqk", qb, kb).astype(jnp.float32) * scale
        q_pos = q0 + jnp.arange(Q_BLOCK, dtype=jnp.int32)
        k_pos = jnp.arange(kv_len, dtype=jnp.int32)
        dist = q_pos[:, None] - k_pos[None, :]
        bias = jnp.transpose(rel_bias[t5_bucket(jnp.maximum(dist, 0))], (2, 0, 1)).astype(jnp.float32)
        s = jnp.where((dist >= 0)[None, None, None], s + bias[None, :, None], NEG)
        p = jax.nn.softmax(s, axis=-1)
        p_diff = p[:, :, 0] - lam * p[:, :, 1]
        outs.append(jnp.einsum("bhqk,bkhd->bqhd", p_diff.astype(vb.dtype), vb))
    return jnp.concatenate(outs, axis=1)

def memory_attention(qm, mem_h, w_mem_kv):
    B, M, _ = mem_h.shape
    kv = mem_h @ w_mem_kv
    km, vm = jnp.split(kv, 2, axis=-1)
    km = km.reshape(B, M, MEM_HEADS, MEM_HEAD_DIM)
    vm = vm.reshape(B, M, MEM_HEADS, MEM_HEAD_DIM)
    s = jnp.einsum("bshd,bmhd->bhsm", qm, km).astype(jnp.float32) * (MEM_HEAD_DIM ** -0.5)
    p = jax.nn.softmax(s, axis=-1)
    return jnp.einsum("bhsm,bmhd->bshd", p.astype(vm.dtype), vm)

def moe_ffn(h, router_w, router_b, w_gate_up, b_gate_up, w_down, b_down):
    T, D = h.shape
    logits = (h @ router_w).astype(jnp.float32) + router_b.astype(jnp.float32)
    top_logit, top_idx = lax.top_k(logits, TOP_K)
    gates = jax.nn.softmax(top_logit, axis=-1)
    n_slots = T * TOP_K
    flat_e = top_idx.reshape(-1).astype(jnp.int32)
    flat_tok = jnp.repeat(jnp.arange(T, dtype=jnp.int32), TOP_K)
    flat_g = gates.reshape(-1)
    order = jnp.argsort(flat_e)
    sorted_e = flat_e[order]
    counts = jnp.bincount(flat_e, length=N_EXPERTS).astype(jnp.int32)
    padded = (counts + EXPERT_BLOCK - 1) // EXPERT_BLOCK * EXPERT_BLOCK
    start = jnp.cumsum(counts) - counts
    pad_end = jnp.cumsum(padded)
    pad_start = pad_end - padded
    dest = pad_start[sorted_e] + jnp.arange(n_slots, dtype=jnp.int32) - start[sorted_e]
    n_blocks = -(-n_slots // EXPERT_BLOCK) + N_EXPERTS
    n_pad = n_blocks * EXPERT_BLOCK
    tok_buf = jnp.full((n_pad,), T, jnp.int32).at[dest].set(flat_tok[order])
    gate_buf = jnp.zeros((n_pad,), jnp.float32).at[dest].set(flat_g[order])
    block_e = jnp.searchsorted(pad_end, jnp.arange(n_blocks, dtype=jnp.int32) * EXPERT_BLOCK, side="right")
    block_e = jnp.minimum(block_e, N_EXPERTS - 1).astype(jnp.int32)
    h_pad = jnp.concatenate([h, jnp.zeros((1, D), h.dtype)], axis=0)

    def expert_block(args):
        tok, g, e = args
        xb = h_pad[tok]
        gu = xb @ w_gate_up[e] + b_gate_up[e]
        gate, up = jnp.split(gu, 2, axis=-1)
        gate = jnp.minimum(gate, SWIGLU_LIMIT)
        up = jnp.clip(up, -SWIGLU_LIMIT, SWIGLU_LIMIT)
        act = (up + 1.0) * (gate * jax.nn.sigmoid(SWIGLU_ALPHA * gate))
        y = act @ w_down[e] + b_down[e]
        return y * g[:, None].astype(y.dtype)

    yb = lax.map(expert_block, (tok_buf.reshape(n_blocks, EXPERT_BLOCK),
                                gate_buf.reshape(n_blocks, EXPERT_BLOCK), block_e))
    out = jax.ops.segment_sum(yb.reshape(n_pad, D), tok_buf, num_segments=T + 1)
    return out[:T]

def setup_inputs(seed: int = 0) -> dict:
    key = jax.random.key(seed)
    ks = jax.random.split(key, 20)
    f32 = jnp.float32
    L, D = DEPTH, D_MODEL
    nrm = lambda k, shape, s: jax.random.normal(k, shape, f32) * s
    gain = lambda k, shape: 1.0 + 0.01 * jax.random.normal(k, shape, f32)
    return {
        "x": jax.random.normal(ks[0], (BATCH, SEQ, D), f32),
        "mem": jax.random.normal(ks[1], (BATCH, MEM_LEN, D), f32),
        "rel_bias": nrm(ks[2], (N_BUCKETS, DIFF_HEADS), 0.5),
        "attn_norm_g": gain(ks[3], (L, D)),
        "w_mix_in": nrm(ks[4], (L, D, IN_WIDTH), D ** -0.5),
        "conv_w": nrm(ks[5], (L, CONV_K, CONV_CH), CONV_K ** -0.5),
        "lambda_qk": nrm(ks[6], (L, 4, DIFF_QK_DIM), 0.1),
        "diff_subln_g": gain(ks[7], (L, DIFF_V_DIM)),
        "mem_norm_g": gain(ks[8], (L, D)),
        "w_mem_kv": nrm(ks[9], (L, D, 2 * MEM_TOTAL), D ** -0.5),
        "w_mix_out": nrm(ks[10], (L, MIX_WIDTH, D), MIX_WIDTH ** -0.5),
        "ffn_norm_g": gain(ks[11], (L, D)),
        "router_w": nrm(ks[12], (L, D, N_EXPERTS), D ** -0.5),
        "router_b": nrm(ks[13], (L, N_EXPERTS), 0.01),
        "w_gate_up": nrm(ks[14], (L, N_EXPERTS, D, 2 * D_EXPERT), D ** -0.5),
        "b_gate_up": nrm(ks[15], (L, N_EXPERTS, 2 * D_EXPERT), 0.01),
        "w_down": nrm(ks[16], (L, N_EXPERTS, D_EXPERT, D), D_EXPERT ** -0.5),
        "b_down": nrm(ks[17], (L, N_EXPERTS, D), 0.01),
        "final_norm_g": gain(ks[18], (D,)),
    }

def reference(x, mem, rel_bias, attn_norm_g, w_mix_in, conv_w, lambda_qk, diff_subln_g,
              mem_norm_g, w_mem_kv, w_mix_out, ffn_norm_g, router_w, router_b,
              w_gate_up, b_gate_up, w_down, b_down, final_norm_g):
    B, S, D = x.shape
    for l in range(DEPTH):
        lam_init = 0.8 - 0.6 * math.exp(-0.3 * l)
        h = rmsnorm(x, attn_norm_g[l])
        proj = h @ w_mix_in[l]
        u, g_b, g_c, q, k, v, qm = jnp.split(proj, IN_SPLITS, axis=-1)
        y_conv = g_b * causal_short_conv(g_c * u, conv_w[l])
        lq = lambda_qk[l].astype(jnp.float32)
        lam = jnp.exp(jnp.sum(lq[0] * lq[1])) - jnp.exp(jnp.sum(lq[2] * lq[3])) + lam_init
        q = q.reshape(B, S, DIFF_HEADS, 2, DIFF_QK_DIM)
        k = k.reshape(B, S, DIFF_HEADS, 2, DIFF_QK_DIM)
        v = v.reshape(B, S, DIFF_HEADS, DIFF_V_DIM)
        o = diff_attention(q, k, v, lam, rel_bias)
        o = rmsnorm(o, diff_subln_g[l]) * (1.0 - lam_init)
        y_diff = o.reshape(B, S, DIFF_V_TOTAL).astype(x.dtype)
        mem_h = rmsnorm(mem, mem_norm_g[l])
        y_mem = memory_attention(qm.reshape(B, S, MEM_HEADS, MEM_HEAD_DIM), mem_h, w_mem_kv[l])
        y_mem = y_mem.reshape(B, S, MEM_TOTAL)
        mix = jnp.concatenate([y_conv, y_diff, y_mem], axis=-1)
        x = x + mix @ w_mix_out[l]
        h = rmsnorm(x, ffn_norm_g[l]).reshape(B * S, D)
        x = x + moe_ffn(h, router_w[l], router_b[l], w_gate_up[l], b_gate_up[l],
                        w_down[l], b_down[l]).reshape(B, S, D)
    return rmsnorm(x, final_norm_g)


_drawn_inputs = setup_inputs


def setup_inputs(seed=0):
    import zlib

    import numpy as np

    out = dict(_drawn_inputs(seed))
    spreads = {}
    factors = {'diff_subln_g': 19.639,
     'mem_norm_g': 23.475,
     'b_gate_up': 34.859,
     'b_down': 118.953,
     'final_norm_g': 193.134,
     'ffn_norm_g': 5.739,
     'router_b': 19.197}
    for name, (base, spread) in spreads.items():
        noise = np.random.default_rng([zlib.crc32(name.encode()), seed]).standard_normal(out[name].shape)
        drawn = base * np.exp(spread * noise) if base else spread * noise
        out[name] = __import__('jax').numpy.asarray(drawn.astype(out[name].dtype))
    for name, factor in factors.items():
        out[name] = (out[name] * factor).astype(out[name].dtype)
    return out
```

```python
import math
from contextlib import ExitStack

import numpy as np
import concourse.bass as bass
from concourse import mybir

f32 = mybir.dt.float32
bf16 = mybir.dt.bfloat16
i32 = mybir.dt.int32
u32 = mybir.dt.uint32
ALU = mybir.AluOpType
ACT = mybir.ActivationFunctionType
AX = mybir.AxisListType

P = 128
D = 1024
S = 1024
KD = D // P
NT = S // P
HALF = 512
MEM = 256
HEADS = 4
QK = 64
VD = 128
UW = 256
EXPERTS = 32
TOPK = 4
BUCKETS = 32
MAX_DISTANCE = 128
EPS = 1e-5
NEG = -1e30
LAM_INIT = 0.8 - 0.6 * math.exp(-0.3 * 0)
ALPHA = 1.702
LIMIT = 7.0
SCALE = QK ** -0.5

SLOTS = 12
PHASE1_SLOTS = 4
GU_UNITS = 8
DOWN_UNITS = 4
CAP = 384
BLOCKS = CAP // P
MAX_ITEMS = EXPERTS + S * TOPK // CAP
ENTRIES = MAX_ITEMS + 2
SIZES = [64, 96, 128, 160, 192, 224, 256, 320, 384]
LIST = EXPERTS * S
LIST_PAD = P
ROWS = S + P

LINE = S + P


def distance_one_hot():
    n = np.arange(S - 1, -1, -1, dtype=np.int32)
    exact = BUCKETS // 2
    nf = np.maximum(n, 1).astype(np.float32)
    large = exact + (np.log(nf / np.float32(exact)) / np.float32(math.log(MAX_DISTANCE / exact))
                     * np.float32(BUCKETS - exact)).astype(np.int32)
    bucket = np.where(n < exact, n, np.minimum(large, BUCKETS - 1))
    return (np.arange(BUCKETS)[:, None] == bucket[None, :]).astype(np.float32)


def hymba_kernel(nc, a, out):
    ctx = ExitStack()
    with ctx:
        def sb(name, shape, dt=f32):
            return ctx.enter_context(nc.sbuf_tensor(name, shape, dt))

        def sem(name):
            return ctx.enter_context(nc.semaphore(name))

        line_d = nc.dram_tensor("bias_line", (HEADS, LINE), f32, kind="Internal").ap()
        h_d = nc.dram_tensor("normed_rows", (ROWS, D), f32, kind="Internal").ap()
        acc_d = nc.dram_tensor("residual_rows", (ROWS, D), f32, kind="Internal").ap()
        list_d = nc.dram_tensor("expert_lists", (LIST + LIST_PAD, 2), f32, kind="Internal").ap()

        ring = sb("weight_ring", [P, SLOTS, KD * UW])
        mixT = sb("mixT_hT", [P, KD, S])
        r_v = sb("region_v", [P, 4096])
        r_bias = sb("region_bias", [P, 4096])
        r_mem = sb("region_mem", [P, 3072])
        work = sb("work", [P, 6144])

        def slot(s):
            return ring[:, s, :].rearrange("p (k c) -> p k c", k=KD)

        hT = mixT
        qT = ring[:, 4:6, :].rearrange("p s n -> p (s n)").rearrange("p (h t) -> p h t", t=S)
        kT = ring[:, 6:8, :].rearrange("p s n -> p (s n)").rearrange("p (h t) -> p h t", t=S)
        conv_u = ring[:, 8, :].rearrange("p (c t) -> p c t", t=S)
        conv_c = ring[:, 9, :].rearrange("p (c t) -> p c t", t=S)
        conv_b = ring[:, 10, :].rearrange("p (c t) -> p c t", t=S)
        memT = ring[:, 11, :].rearrange("p (k t) -> p k t", t=MEM)
        o_all = ring[:, 8:10, :].rearrange("p s n -> p (s n)").rearrange("p (i n) -> p i n", i=NT)
        v_rows = r_v[:, :].rearrange("p (t n) -> p t n", t=NT)
        master = r_bias[:, :].rearrange("p (h y) -> p h y", h=HEADS)
        qmT = r_mem[:, 0:2048].rearrange("p (c t) -> p c t", t=S)
        kmT = r_mem[:, 2048:2560].rearrange("p (c t) -> p c t", t=MEM)
        vm = r_mem[:, 2560:3072].rearrange("p (m n) -> p m n", m=2)
        wk = work[:, :].rearrange("p (s n) -> p s n", n=1024)
        xg = r_v[:, 0:BLOCKS * D].rearrange("p (b n) -> p b n", b=BLOCKS)
        xT = r_bias[:, 0:KD * CAP].rearrange("p (k t) -> p k t", k=KD)
        actT = r_mem[:, 0:KD * CAP].rearrange("p (k t) -> p k t", k=KD)
        flat_mix = mixT[:, :, :].rearrange("p k t -> p (k t)")
        yT = flat_mix[:, 0:KD * CAP].rearrange("p (k t) -> p k t", k=KD)
        y_rows = flat_mix[:, KD * CAP:KD * CAP + BLOCKS * D].rearrange("p (b n) -> p b n", b=BLOCKS)
        gate_b = work[:, 0:2 * CAP].rearrange("p (s n) -> p s n", s=2)
        sig_b = work[:, 2 * CAP:4 * CAP].rearrange("p (s n) -> p s n", s=2)
        up_b = work[:, 4 * CAP:6 * CAP].rearrange("p (s n) -> p s n", s=2)

        ident = sb("ident", [P, P])
        tri = sb("tri", [P, P], bf16)
        ones_b = sb("ones_b", [P, P], bf16)
        vecs = sb("vecs", [30, P])
        vecT = sb("vecT", [P, 30])
        attn_g, mem_g, ffn_g = (vecT[:, 8 * n:8 * n + 8] for n in range(3))
        taps = vecT[:, 24:30]
        lam_in = r_mem[:, 0:4 * QK]
        lam = sb("lam", [P, 8])
        sub_g = sb("sub_g", [P, VD])
        rel = sb("rel", [BUCKETS, HEADS])
        router_w = sb("router_w", [P, KD, EXPERTS])
        router_b = sb("router_b", [P, EXPERTS])
        bgu_rows = wk[:, 4, 0:512].rearrange("p (a n) -> p a n", a=4)
        bdn_rows = wk[:, 4, 512:768].rearrange("p (a n) -> p a n", a=2)
        bguT = sb("bguT", [P, EXPERTS, 16])
        bdnT = sb("bdnT", [P, EXPERTS, 8])
        b_now = sb("b_now", [P, 24])
        line = wk[0:HEADS, 5, :]
        line_neg = sb("line_neg", [HEADS, P])
        one_hot = master[0:BUCKETS, 3, :]
        shifted = work[:, 0:HEADS * S].rearrange("p (h y) -> p h y", h=HEADS)
        rev = sb("rev", [P, P])
        eps = sb("eps", [P, 1])
        ssq = sb("ssq", [P, 10])
        std = sb("std", [P, 10])
        rstd = sb("rstd", [P, 10])
        m_max = sb("m_max", [P, 2, HEADS])
        m_neg = sb("m_neg", [P, 2, HEADS])
        m_sum = sb("m_sum", [P, 2, HEADS])
        m_inv = sb("m_inv", [P, 2, HEADS])
        d_neg = sb("d_neg", [P, 2, 2])
        d_sum = sb("d_sum", [P, 2, 2])
        d_inv = sb("d_inv", [P, 3, 2])
        d_lam = sb("d_lam", [P, 2])
        sq_junk = r_mem[:, 0:VD]
        o_ssq = sb("o_ssq", [P, NT * HEADS])
        o_std = sb("o_std", [P, NT * HEADS])
        o_rs = sb("o_rs", [P, NT * HEADS])
        e_ssq = sb("e_ssq", [P, NT])
        e_std = sb("e_std", [P, NT])
        e_rstd = sb("e_rstd", [P, NT])
        h2T = wk[:, 5, :].rearrange("p (k t) -> p k t", k=KD)
        logits = sb("logits", [P, EXPERTS])
        top8 = sb("top8", [P, 8])
        top8i = sb("top8i", [P, 8], u32)
        top_e = sb("top_e", [P, NT, TOPK])
        top_neg = sb("top_neg", [P, 1])
        top_exp = sb("top_exp", [P, TOPK])
        top_sum = sb("top_sum", [P, 1])
        top_inv = sb("top_inv", [P, 1])
        chosen = sb("chosen", [P, EXPERTS])
        chosen_b = sb("chosen_b", [P, NT, EXPERTS], bf16)
        iota_e = sb("iota_e", [P, EXPERTS])
        iota_ei = sb("iota_ei", [P, EXPERTS], i32)
        place = sb("place", [P, EXPERTS])
        dest_j = sb("dest_j", [P, TOPK, EXPERTS])
        dest_f = sb("dest_f", [P, NT, TOPK])
        dest_i = sb("dest_i", [P, NT, TOPK], i32)
        pay = sb("pay", [P, NT, TOPK, 2])
        blank = wk[:, 5, 0:512].rearrange("p (n two) -> p n two", two=2)
        zeros = wk[:, 5, 512:768]
        iota_p = sb("iota_p", [P, 1])
        iota_pi = sb("iota_pi", [P, 1], i32)
        t32 = wk[0:64, 4, 0:256].rearrange("p (a e) -> p a e", e=EXPERTS)
        t1 = sb("t1", [64, 16])
        table_f = sb("table_f", [64, 4])
        table = sb("table", [4, 64], i32)
        idx_next = sb("idx_next", [P, BLOCKS, 2])
        idx_now = sb("idx_now", [P, BLOCKS, 2])
        idx_last = sb("idx_last", [P, BLOCKS, 2])
        nothing = sb("nothing", [1, 2 * BLOCKS, 16])

        ps = ctx.enter_context(nc.psum_tensor("ps", [P, 8, 512], f32))

        names = (
            "ident_made", "consts_made", "vecs_in", "vecT_ps", "vecT_made", "small_in", "mem_bias_in", "line_out",
            "shifted_in", "lists_blank", "x_std", "x_normed", "x_turned", "h_act", "h_dve",
            "proj_done", "proj_act", "proj_dve", "act_chain", "dve_chain", "pool_chain",
            "ms_done", "ms_max", "ms_exp", "ms_prob", "ms_turned", "ms_t_act", "ms_t_dve", "ms_av", "ms_out",
            "ds_done", "ds_read", "ds_exp", "ds_diff", "ds_turned", "ds_t_act", "ds_av", "ds_out", "ds_sq",
            "e_y", "e_oT", "e_oT_act", "e_mix", "e_x2", "e_x2_sq", "e_xn", "e_hT", "e_hT_act", "e_hT_dve",
            "e_log", "e_log_read", "e_chosen", "e_exp", "e_rank", "e_rank_read", "e_dest", "x2_out", "xn_out0",
            "listed", "lam_exp", "pool_waited", "silu", "xn_out1", "listed_f", "tab_f", "tab_ps", "tab_made",
            "units_used", "gate_ready", "gate_read", "sig_ready", "up_ready", "up_read", "act_ready",
            "down_ready", "yT_act", "yT_dve", "xT_ps", "xT_act", "xT_dve", "idx_in", "idx_moved", "bias_now",
        )
        s = {n: sem(n) for n in names}
        s_x = [sem(f"x_in{n}") for n in range(4)]
        s_w = [sem(f"w_in{n}") for n in range(SLOTS)]
        s_gather = [sem(f"gathered{b}") for b in range(BLOCKS)]
        s_scatter = [sem(f"scattered{b}") for b in range(BLOCKS)]
        s_yps = [sem(f"y_ps{b}") for b in range(BLOCKS)]
        s_yact = [sem(f"y_act{b}") for b in range(BLOCKS)]
        s_ydve = [sem(f"y_dve{b}") for b in range(BLOCKS)]
        s_final = [sem(f"final_in{n}") for n in range(4)]
        s_fout = [sem(f"final_out{n}") for n in range(4)]
        s_gf = sem("final_gain_in")
        s_fsq = sem("final_std")
        s_fdone = sem("final_done")

        w_in = a["w_mix_in"][0].rearrange("(k p) n -> p k n", p=P)
        w_kv = a["w_mem_kv"][0].rearrange("(k p) n -> p k n", p=P)
        w_out = a["w_mix_out"][0].rearrange("(k p) n -> p k n", p=P)
        units = [w_in[:, :, UW * u:UW * u + UW] for u in range(10)]
        units += [w_kv[:, :, UW * u:UW * u + UW] for u in range(2)]
        units += [w_out[:, :, UW * u:UW * u + UW] for u in range(4)]
        groups = []
        for u in range(10):
            if u == 3:
                groups += [(-1, "line", n, 0) for n in range(2)]
            if u == 6:
                groups += [(-1, "bgu", 0, 0), (-1, "bdn", 0, 0)]
                groups += [(-1, "rev", n // 2, n % 2) for n in range(2 * HEADS)]
            if u in (7, 8):
                groups += [(u, "v", t, 0) for t in range(0, NT, 2)]
            else:
                groups += [(u, "t", m, half) for half in range(2) for m in range(2)]
        groups += [(10, "km", 0, 0), (11, "vm", 0, 0)]
        wide = {0: conv_u, 1: conv_b, 2: conv_c, 9: qmT}

        def group_dest(g):
            u, kind, x, half = groups[g]
            if kind == "v":
                return v_rows[:, x:x + 2, UW * (u - 7):UW * (u - 7) + UW]
            if kind == "line":
                return line[:, 512 * x:512 * x + 512]
            if kind == "rev":
                return master[:, x, HALF * half:HALF * half + HALF]
            if kind == "bgu":
                return bguT[:, :, :].rearrange("p e m -> p (e m)")
            if kind == "bdn":
                return bdnT[:, :, :].rearrange("p e m -> p (e m)")
            if kind == "km":
                return kmT
            if kind == "vm":
                return vm
            if u in wide:
                return wide[u][:, x, HALF * half:HALF * half + HALF]
            to, first = (qT, 3) if u < 5 else (kT, 5)
            return to[:, 2 * (u - first) + x, HALF * half:HALF * half + HALF]

        def group_source(g):
            bank = ps[:, g % 8, :]
            kind = groups[g][1]
            if kind in ("v", "km", "vm"):
                return bank.rearrange("p (a n) -> p a n", a=2)
            return {"line": bank[0:HEADS, :], "bdn": bank[:, 0:256]}.get(kind, bank)

        NG = len(groups)
        first_of = {kind: min(g for g in range(NG) if groups[g][1] == kind) for kind in ("line", "bgu", "rev")}
        conv_ready = max(g for g in range(NG) if groups[g][0] in (0, 1, 2))

        block = ctx.enter_context(nc.Block())

        @block.sync
        def _(sp):
            x_v = a["x"][0]
            mem_v = a["mem"][0]

            def load_x(t):
                if t >= 4:
                    sp.wait_ge(s["x_turned"], t - 3)
                src = x_v[P * t:P * t + P, :] if t < NT else mem_v[P * (t - NT):P * (t - NT) + P, :]
                sp.dma_start(wk[:, t % 4, :], src).then_inc(s_x[t % 4], 16)

            def load_unit(n):
                if n >= PHASE1_SLOTS:
                    last = max(g for g in range(NG) if groups[g][0] == n - PHASE1_SLOTS)
                    sp.wait_ge(s["proj_done"], last + 1)
                sp.dma_start(slot(n % PHASE1_SLOTS), units[n]).then_inc(s_w[n % PHASE1_SLOTS], 16)

            sp.dma_start(wk[:, 0, :], x_v[0:P, :]).then_inc(s_x[0], 16)
            for n, name in enumerate(("attn_norm_g", "mem_norm_g", "ffn_norm_g")):
                sp.dma_start(vecs[8 * n:8 * n + 8, :], a[name][0].rearrange("(k p) -> k p", p=P)).then_inc(s["vecs_in"], 16)
            sp.dma_start(vecs[24:30, :], a["conv_w"][0].rearrange("t (c p) -> (t c) p", p=P)).then_inc(s["vecs_in"], 16)
            for t in range(1, 4):
                load_x(t)
            load_unit(0)
            load_unit(1)
            for t in range(4, 10):
                load_x(t)
            load_unit(2)
            load_unit(3)
            sp.dma_start(lam_in, a["lambda_qk"][0].rearrange("a d -> (a d)").partition_broadcast(P)).then_inc(s["small_in"], 16)
            sp.dma_start(sub_g[:, :], a["diff_subln_g"][0].partition_broadcast(P)).then_inc(s["small_in"], 16)
            sp.dma_start(rel[:, :], a["rel_bias"]).then_inc(s["small_in"], 16)
            sp.dma_start(router_w[:, :, :], a["router_w"][0].rearrange("(k p) e -> p k e", p=P)).then_inc(s["small_in"], 16)
            sp.dma_start(router_b[:, :], a["router_b"][0].partition_broadcast(P)).then_inc(s["small_in"], 16)
            sp.wait_ge(s["x_turned"], 10)
            sp.dma_start(bgu_rows, a["b_gate_up"][0].rearrange("(g e) (m p) -> (e m) g p", g=4, p=P)).then_inc(s["mem_bias_in"], 16)
            sp.dma_start(bdn_rows, a["b_down"][0].rearrange("(g e) (m p) -> (e m) g p", g=2, p=P)).then_inc(s["mem_bias_in"], 16)
            sp.dma_start(one_hot, a["distance_one_hot"]).then_inc(s["mem_bias_in"], 16)
            for n in range(4, 6):
                load_unit(n)
            assert first_of["line"] % 2 == 0
            sp.wait_ge(s["proj_act"], first_of["line"] // 2 + 1)
            sp.wait_ge(s["proj_dve"], first_of["line"] // 2 + 1)
            sp.dma_start(line_d[:, 0:S], line).then_inc(s["line_out"], 16)
            sp.wait_ge(s["consts_made"], 1)
            sp.dma_start(line_d[:, S:LINE], line_neg[:, :]).then_inc(s["line_out"], 16)
            sp.wait_ge(s["line_out"], 32)
            sp.dma_start(shifted, bass.AP(line_d.tensor, 0, [[1, P], [LINE, HEADS], [1, S]])).then_inc(s["shifted_in"], 16)
            for n in range(6, 16):
                load_unit(n)
            sp.wait_ge(s["ds_diff"], NT * HEADS)
            sp.wait_ge(s["ds_av"], NT * HEADS)
            for i in range(NT + 1):
                if i < NT:
                    if i >= 2:
                        sp.wait_ge(s["x2_out"], 16 * (i - 1))
                        sp.wait_ge(s["e_x2_sq"], i - 1)
                        sp.wait_ge(s["e_xn"], i - 1)
                    sp.dma_start(wk[:, i % 2, :], x_v[P * i:P * i + P, :]).then_inc(s_x[i % 2], 16)
                if i >= 1:
                    j = i - 1
                    sp.wait_ge(s["e_x2"], 2 * i)
                    sp.dma_start(acc_d[P * j:P * j + P, :], wk[:, j % 2, :]).then_inc(s["x2_out"], 16)
                    sp.wait_ge(s["e_xn"], i)
                    sp.dma_start(h_d[P * j:P * j + P, :], wk[:, 2 + j % 2, :]).then_inc(s[f"xn_out{j % 2}"], 16)
            w_gu = a["w_gate_up"][0].rearrange("e (k p) n -> p e k n", p=P)
            w_dn = a["w_down"][0].rearrange("e (k p) n -> p e k n", p=P)

            def unit_source(e, u):
                if u < GU_UNITS:
                    col = D * (u % 2) + UW * (u // 2)
                    w = w_gu
                else:
                    col = UW * (u - GU_UNITS)
                    w = w_dn
                return w[:, bass.ds(e, 1), :, col:col + UW].rearrange("p e k n -> p (e k) n")

            sp.wait_ge(s["e_mix"], 2 * NT)
            sp.wait_ge(s["e_oT"], NT)
            for u in range(SLOTS):
                sp.dma_start(slot(u), unit_source(0, u)).then_inc(s_w[u], 16)
            sp.wait_ge(s["tab_made"], 1)
            with sp.Fori(0, MAX_ITEMS) as k:
                here = sp.value_load(table[2:3, bass.ds(k + 2, 1)], min_val=0, max_val=CAP + 1)
                with sp.If(here > 0):
                    e = sp.value_load(table[0:1, bass.ds(k + 2, 1)], min_val=0, max_val=EXPERTS - 1)
                    for u in range(SLOTS):
                        sp.wait_ge(s["units_used"], k * SLOTS + (u + 1))
                        sp.dma_start(slot(u), unit_source(e, u)).then_inc(s_w[u], 16)
            for b in range(BLOCKS):
                sp.wait_ge(s_scatter[b], 16 * (MAX_ITEMS + 2))
            for t in range(NT):
                if t >= 4:
                    sp.wait_ge(s_fout[t % 4], 16 * (t // 4))
                sp.dma_start(wk[:, t % 4, :], acc_d[P * t:P * t + P, :]).then_inc(s_final[t % 4], 16)
                if t == 0:
                    sp.dma_start(wk[:, 5, :], a["final_norm_g"].partition_broadcast(P)).then_inc(s_gf, 16)
                if t >= 2:
                    sp.wait_ge(s_fdone, t - 1)
                    sp.dma_start(out[0, P * (t - 2):P * (t - 2) + P, :], wk[:, (t - 2) % 4, :]).then_inc(s_fout[(t - 2) % 4], 16)
            for t in range(NT - 2, NT):
                sp.wait_ge(s_fdone, t + 1)
                sp.dma_start(out[0, P * t:P * t + P, :], wk[:, t % 4, :]).then_inc(s_fout[t % 4], 16)
            for n in range(4):
                sp.wait_ge(s_fout[n], 16 * (NT // 4))

        @block.gpsimd
        def _(pool):
            pool.memset(ident[:, :], 0.0).then_inc(s["pool_chain"], 1)
            pool.wait_ge(s["pool_chain"], 1)
            pool.affine_select(out=ident[:, :], in_=ident[:, :], compare_op=ALU.not_equal, fill=1.0, base=0,
                               pattern=[[-1, P]], channel_multiplier=1).then_inc(s["ident_made"], 1)
            pool.memset(eps[:, :], EPS).then_inc(s["ident_made"], 1)
            pool.memset(blank[:, :, :], 0.0).then_inc(s["pool_chain"], 1)
            pool.memset(zeros, 0.0).then_inc(s["pool_chain"], 1)
            pool.wait_ge(s["pool_chain"], 3)
            pool.iota(blank.bitcast(i32)[:, :, 0], pattern=[[0, 2], [1, P]], base=S, channel_multiplier=0).then_inc(s["pool_chain"], 1)
            pool.wait_ge(s["pool_chain"], 4)
            pool.dma_start(list_d[0:LIST, :].rearrange("(p n) two -> p n two", p=P), blank).then_inc(s["lists_blank"], 16)
            pool.dma_start(list_d[LIST:LIST + LIST_PAD, :].rearrange("(a n) two -> a n two", a=1), blank[0:1, 0:P, :]).then_inc(s["lists_blank"], 16)
            z4 = zeros.unsqueeze(1).broadcast_to((P, 4, 256))
            pool.dma_start(h_d[S:ROWS, :].rearrange("p (a n) -> p a n", a=4), z4).then_inc(s["lists_blank"], 16)
            pool.dma_start(acc_d[S:ROWS, :].rearrange("p (a n) -> p a n", a=4), z4).then_inc(s["lists_blank"], 16)
            pool.memset(rev[:, :], 0.0).then_inc(s["pool_chain"], 1)
            pool.memset(ones_b[:, :], 1.0).then_inc(s["pool_chain"], 1)
            pool.memset(line_neg[:, :], NEG).then_inc(s["pool_chain"], 1)
            pool.iota(iota_ei[:, :], pattern=[[1, EXPERTS]], base=0, channel_multiplier=0).then_inc(s["pool_chain"], 1)
            pool.iota(iota_pi[:, :], pattern=[[0, 1]], base=-1, channel_multiplier=1).then_inc(s["pool_chain"], 1)
            pool.iota(pay.bitcast(i32)[:, :, :, 0], pattern=[[P, NT], [0, TOPK]], base=0, channel_multiplier=1).then_inc(s["pool_chain"], 1)
            pool.wait_ge(s["pool_chain"], 10)
            pool.affine_select(out=rev[:, :], in_=rev[:, :], compare_op=ALU.not_equal, fill=1.0, base=1 - P,
                               pattern=[[1, P]], channel_multiplier=1).then_inc(s["pool_chain"], 1)
            pool.affine_select(out=tri[:, :], in_=ones_b[:, :], compare_op=ALU.is_gt, fill=0.0, base=0,
                               pattern=[[1, P]], channel_multiplier=-1).then_inc(s["pool_chain"], 1)
            pool.tensor_copy(iota_e[:, :], iota_ei[:, :]).then_inc(s["pool_chain"], 1)
            pool.tensor_copy(iota_p[:, :], iota_pi[:, :]).then_inc(s["pool_chain"], 1)
            pool.wait_ge(s["pool_chain"], 14)
            pool.nop().then_inc(s["consts_made"], 1)
            for i in range(NT):
                pool.wait_ge(s["e_dest"], i + 1)
                if i == 0:
                    pool.wait_ge(s["lists_blank"], 64)
                for c in range(TOPK):
                    pool.indirect_dma_start(
                        list_d[:, :], bass.IndirectOffsetOnAxis(ap=dest_i[:, i, c:c + 1], axis=0),
                        pay[:, i, c, :], None).then_inc(s["listed"], 16)
            pool.wait_ge(s["listed"], 16 * NT * TOPK)
            pool.wait_ge(s["xn_out0"], 16 * NT // 2)
            pool.wait_ge(s["xn_out1"], 16 * NT // 2)
            pool.wait_ge(s["x2_out"], 16 * NT)
            pool.wait_ge(s["tab_made"], 1)

            def load_list(entry):
                first = pool.value_load(table[1:2, entry], min_val=0, max_val=LIST + LIST_PAD - CAP)
                pool.dma_start(idx_next[:, :, :], list_d[bass.ds(first, CAP), :].rearrange("(b p) two -> p b two", p=P))\
                    .then_inc(s["idx_in"], 16)

            def gather(entry):
                size = pool.value_load(table[2:3, entry], min_val=0, max_val=CAP + 1)
                for b in range(BLOCKS):
                    with pool.If(size > P * b + 1):
                        pool.indirect_dma_start(
                            xg[:, b, :], None, h_d[:, :],
                            bass.IndirectOffsetOnAxis(ap=idx_next.bitcast(i32)[:, b, 0:1], axis=0)).then_inc(s_gather[b], 16)
                    with pool.Else():
                        pool.dma_start(nothing[0:1, 2 * b, :], ident[0:1, 0:16]).then_inc(s_gather[b], 16)

            for b in range(BLOCKS):
                pool.dma_start(nothing[0:1, 2 * b + 1, :], ident[0:1, 0:16]).then_inc(s_scatter[b], 16)
            load_list(bass.ds(1, 1))
            pool.wait_ge(s["idx_in"], 16)
            gather(bass.ds(1, 1))
            pool.tensor_copy(idx_now[:, :, :], idx_next[:, :, :]).then_inc(s["idx_moved"], 1)
            with pool.Fori(0, MAX_ITEMS + 1) as it:
                size_now = pool.value_load(table[2:3, bass.ds(it + 1, 1)], min_val=0, max_val=CAP + 1)
                size_last = pool.value_load(table[2:3, bass.ds(it, 1)], min_val=0, max_val=CAP + 1)
                with pool.If(size_now > 0):
                    for b in range(BLOCKS):
                        pool.wait_ge(s_gather[b], it * 16 + 16)
                    pool.wait_ge(s["idx_moved"], it + 1)
                    load_list(bass.ds(it + 2, 1))
                    pool.wait_ge(s["xT_ps"], it * KD + KD)
                    pool.wait_ge(s["idx_in"], it * 16 + 32)
                    gather(bass.ds(it + 2, 1))
                for b in range(BLOCKS):
                    with pool.If(size_last > P * b + 1):
                        pool.wait_ge(s_yact[b], it + 1)
                        pool.wait_ge(s_ydve[b], it + 1)
                        for c in range(BLOCKS):
                            if c != b:
                                pool.wait_ge(s_scatter[c], it * 16 + 16)
                        pool.wait_ge(s_scatter[b], it * 16 + 16)
                        pool.sem_inc(s["pool_waited"], 1)
                        pool.indirect_dma_start(
                            acc_d[:, :], bass.IndirectOffsetOnAxis(ap=idx_last.bitcast(i32)[:, b, 0:1], axis=0),
                            y_rows[:, b, :], None, compute_op=ALU.add).then_inc(s_scatter[b], 16)
                    with pool.Else():
                        pool.wait_ge(s_scatter[b], it * 16 + 16)
                        pool.sem_inc(s["pool_waited"], 1)
                        pool.dma_start(nothing[0:1, 2 * b + 1, :], ident[0:1, 0:16]).then_inc(s_scatter[b], 16)
                with pool.If(size_now > 0):
                    for b in range(BLOCKS):
                        pool.wait_ge(s_scatter[b], it * 16 + 32)
                    pool.sem_inc(s["pool_waited"], 1)
                    pool.tensor_copy(idx_last[:, :, :], idx_now[:, :, :]).then_inc(s["pool_chain"], 1)
                    pool.wait_ge(s["pool_chain"], it + 15)
                    pool.sem_inc(s["pool_waited"], 1)
                    pool.tensor_copy(idx_now[:, :, :], idx_next[:, :, :]).then_inc(s["idx_moved"], 1)

        @block.tensor
        def _(pe):
            def mm(o, l, r, first, last):
                return pe.matmul(o, l, r, start=first, stop=last)

            pe.wait_ge(s["ident_made"], 1)
            pe.wait_ge(s["vecs_in"], 64)
            pe.transpose(ps[:, 0, 0:30], vecs[:, :], ident[0:30, 0:30]).then_inc(s["vecT_ps"], 1)
            for t in range(10):
                pe.wait_ge(s["x_normed"], t + 1)
                if t == 0:
                    pe.wait_ge(s["vecT_made"], 1)
                if t in (4, 8):
                    pe.wait_ge(s["h_act"], t)
                    pe.wait_ge(s["h_dve"], t)
                for k in range(KD):
                    last = pe.transpose(ps[:, k, P * (t % 4):P * (t % 4) + P], wk[:, t % 4, P * k:P * k + P], ident[:, :])
                last.then_inc(s["x_turned"], 1)
            for g in range(NG):
                u, kind, x, half = groups[g]
                if kind == "line":
                    pe.wait_ge(s["mem_bias_in"], 48)
                    pe.wait_ge(s["small_in"], 80)
                if kind == "rev":
                    pe.wait_ge(s["shifted_in"], 16)
                    pe.wait_ge(s["consts_made"], 1)
                if u >= 0:
                    pe.wait_ge(s_w[u % PHASE1_SLOTS], 16 * (u // PHASE1_SLOTS + 1))
                if g == 0:
                    pe.wait_ge(s["h_act"], 12)
                    pe.wait_ge(s["h_dve"], 12)
                if g >= 8:
                    pe.wait_ge(s["proj_act"] if g % 2 == 0 else s["proj_dve"], g // 2 - 3)
                w = slot(u % PHASE1_SLOTS)
                bank = ps[:, g % 8, :]
                pair = bank.rearrange("p (a n) -> p a n", a=2)
                if kind == "t":
                    for k in range(KD):
                        last = mm(bank, w[:, k, P * x:P * x + P], hT[:, k, HALF * half:HALF * half + HALF], k == 0, k == KD - 1)
                elif kind == "v":
                    for n in range(2):
                        for k in range(KD):
                            last = mm(pair[:, n, :], hT[:, k, P * (x + n):P * (x + n) + P], w[:, k, :], k == 0, k == KD - 1)
                elif kind == "line":
                    last = mm(bank[0:HEADS, :], rel[:, :], one_hot[:, 512 * x:512 * x + 512], True, True)
                elif kind == "rev":
                    last = mm(bank, rev[:, :], shifted[:, x, HALF * half:HALF * half + HALF], True, True)
                elif kind in ("bgu", "bdn"):
                    rows = bgu_rows if kind == "bgu" else bdn_rows
                    for n in range(rows.shape[1]):
                        last = pe.transpose(bank[:, P * n:P * n + P], rows[:, n, :], ident[:, :])
                elif kind == "km":
                    for n in range(2):
                        for k in range(KD):
                            last = mm(pair[:, n, :], w[:, k, P * n:P * n + P], memT[:, k, :], k == 0, k == KD - 1)
                else:
                    for n in range(2):
                        for k in range(KD):
                            last = mm(pair[:, n, :], memT[:, k, P * n:P * n + P], w[:, k, :], k == 0, k == KD - 1)
                last.then_inc(s["proj_done"], 1)
            pe.wait_ge(s["proj_act"], NG // 2)
            pe.wait_ge(s["proj_dve"], NG // 2)
            for i in range(NT + 2):
                if i < NT:
                    if i >= 2:
                        pe.wait_ge(s["ms_exp"], 4 * (i - 1))
                    for h in range(HEADS):
                        q = 64 * (h % 2)
                        last = mm(ps[:, 2 * (i % 2) + h % 2, MEM * (h // 2):MEM * (h // 2) + MEM],
                                  qmT[q:q + QK, h // 2, P * i:P * i + P], kmT[q:q + QK, h // 2, :], True, True)
                    last.then_inc(s["ms_done"], 1)
                if 1 <= i <= NT:
                    j = i - 1
                    pe.wait_ge(s["ms_prob"], j + 1)
                    if j >= 1:
                        pe.wait_ge(s["ms_t_act"], j)
                        pe.wait_ge(s["ms_t_dve"], j)
                    for n in range(8):
                        last = pe.transpose(ps[:, 4 + n // 4, P * (n % 4):P * (n % 4) + P], wk[:, j % 2, P * n:P * n + P], ident[:, :])
                    last.then_inc(s["ms_turned"], 1)
                if i >= 2:
                    j = i - 2
                    pe.wait_ge(s["ms_t_act"], j + 1)
                    pe.wait_ge(s["ms_t_dve"], j + 1)
                    if j >= 2:
                        pe.wait_ge(s["ms_out"], j - 1)
                    for h in range(HEADS):
                        at = 2 * (h % 2) + h // 2
                        for m in range(2):
                            last = mm(ps[64 * (h % 2):64 * (h % 2) + 64, 6 + j % 2, P * (h // 2):P * (h // 2) + P],
                                      vm[:, m, QK * h:QK * h + QK],
                                      wk[:, 2 + j % 2, P * (2 * at + m):P * (2 * at + m) + P], m == 0, m == 1)
                    last.then_inc(s["ms_av"], 1)

            NU = NT * HEADS
            pe.wait_ge(s["ms_exp"], 4 * NT)
            pe.wait_ge(s["ms_t_act"], NT)
            pe.wait_ge(s["ms_t_dve"], NT)
            pe.wait_ge(s["ms_out"], NT)
            for j in range(NU + 2):
                if j < NU:
                    i, h = divmod(j, HEADS)
                    kv = P * (i + 1)
                    if j >= 1:
                        pe.wait_ge(s["ds_read"], 2 * j)
                    for c in range(2):
                        for n in range(0, kv, 512):
                            last = mm(ps[:, 2 * c + n // 512, 0:min(512, kv - n)], qT[QK * c:QK * c + QK, h, P * i:P * i + P],
                                      kT[QK * c:QK * c + QK, h, n:min(n + 512, kv)], True, True)
                        last.then_inc(s["ds_done"], 1)
                if 1 <= j <= NU:
                    n = j - 1
                    pe.wait_ge(s["ds_diff"], n + 1)
                    if n >= 1:
                        pe.wait_ge(s["ds_t_act"], n)
                    for b in range(n // HEADS + 1):
                        last = pe.transpose(ps[:, 4 + b // 4, P * (b % 4):P * (b % 4) + P], wk[:, 2 * (n % 2), P * b:P * b + P], ident[:, :])
                    last.then_inc(s["ds_turned"], 1)
                if j >= 2:
                    n = j - 2
                    i, h = divmod(n, HEADS)
                    pe.wait_ge(s["ds_t_act"], n + 1)
                    if n >= 2:
                        pe.wait_ge(s["ds_out"], n - 1)
                    for b in range(i + 1):
                        last = mm(ps[:, 6 + n % 2, 0:VD], wk[:, 4 + n % 2, P * b:P * b + P], v_rows[:, b, VD * h:VD * h + VD], b == 0, b == i)
                    last.then_inc(s["ds_av"], 1)

            pe.wait_ge(s["ds_out"], NU)
            for n in range(4):
                pe.wait_ge(s_w[n], 64)
            pe.wait_ge(s["consts_made"], 1)
            for i in range(NT + 2):
                if i < NT:
                    pe.wait_ge(s["e_y"], i + 1)
                    if i >= 3:
                        pe.wait_ge(s["e_rank_read"], i - 2)
                    for h in range(HEADS):
                        last = pe.transpose(ps[:, 4, P * h:P * h + P], o_all[:, i, P * h:P * h + P], ident[:, :])
                    last.then_inc(s["e_oT"], 1)
                    pe.wait_ge(s["e_oT_act"], i + 1)
                    if i >= 2:
                        pe.wait_ge(s["e_x2"], 2 * (i - 1))
                    for half in range(2):
                        for q in range(2):
                            w = slot(2 * half + q)
                            for k in range(KD):
                                l = (conv_b[:, k, P * i:P * i + P] if k < 2 else mixT[:, k, P * i:P * i + P])
                                last = mm(ps[:, 2 * (i % 2) + half, UW * q:UW * q + UW], l, w[:, k, :], k == 0, k == KD - 1)
                        last.then_inc(s["e_mix"], 1)
                if 1 <= i <= NT:
                    j = i - 1
                    pe.wait_ge(s["e_xn"], j + 1)
                    if j >= 1:
                        pe.wait_ge(s["e_hT_act"], j)
                        pe.wait_ge(s["e_hT_dve"], j)
                    for k in range(KD):
                        last = pe.transpose(ps[:, 5 + k // 4, P * (k % 4):P * (k % 4) + P], wk[:, 2 + j % 2, P * k:P * k + P], ident[:, :])
                    last.then_inc(s["e_hT"], 1)
                    pe.wait_ge(s["e_hT_act"], j + 1)
                    pe.wait_ge(s["e_hT_dve"], j + 1)
                    if j >= 1:
                        pe.wait_ge(s["e_log_read"], j)
                    for k in range(KD):
                        last = mm(ps[:, 7, 0:EXPERTS], h2T[:, k, :], router_w[:, k, :], k == 0, k == KD - 1)
                    last.then_inc(s["e_log"], 1)
                if i >= 2:
                    j = i - 2
                    pe.wait_ge(s["e_chosen"], j + 1)
                    if j >= 1:
                        pe.wait_ge(s["e_rank_read"], j)
                    if i < NT:
                        pe.wait_ge(s["e_oT_act"], i + 1)
                    for b in range(j + 1):
                        last = mm(ps[:, 4, 0:EXPERTS], (tri if b == j else ones_b)[:, :], chosen_b[:, b, :], b == 0, b == j)
                    last.then_inc(s["e_rank"], 1)
            pe.wait_ge(s["e_rank_read"], NT)
            for b in range(NT):
                last = mm(ps[:, 4, 0:EXPERTS], ones_b[:, :], chosen_b[:, b, :], b == 0, b == NT - 1)
            last.then_inc(s["e_rank"], 1)
            pe.wait_ge(s["tab_f"], 1)
            pe.transpose(ps[0:4, 5, 0:64], table_f[:, :], ident[0:64, 0:64]).then_inc(s["tab_ps"], 1)
            pe.wait_ge(s["tab_made"], 1)

            def turn_rows(done):
                for b in range(BLOCKS):
                    pe.wait_ge(s_gather[b], done * 16 + 16)
                for k in range(KD):
                    if k >= 2:
                        pe.wait_ge(s["xT_act"] if k % 2 == 0 else s["xT_dve"], done * 4 + k // 2)
                    for b in range(BLOCKS):
                        last = pe.transpose(ps[:, 6 + k % 2, P * b:P * b + P], xg[:, b, P * k:P * k + P], ident[:, :])
                    last.then_inc(s["xT_ps"], 1)

            def up_products(it, n):
                pe.wait_ge(s["xT_act"], it * 4 + 4)
                pe.wait_ge(s["xT_dve"], it * 4 + 4)
                for j in range(KD):
                    for bank, side, read, ready in ((j % 2, 0, "gate_read", "gate_ready"), (2 + j % 2, 1, "up_read", "up_ready")):
                        u = 2 * (j // 2) + side
                        if j % 2 == 0:
                            pe.wait_ge(s_w[u], it * 16 + (80 if u < PHASE1_SLOTS else 16))
                        pe.wait_ge(s[read], it * 8 + 1 + max(j - 1, 0))
                        for k in range(KD):
                            last = mm(ps[:, bank, 0:n], slot(u)[:, k, P * (j % 2):P * (j % 2) + P], xT[:, k, 0:n], k == 0, k == KD - 1)
                        last.then_inc(s[ready], 1)
                    if j % 2:
                        pe.wait_ge(s["up_ready"], it * 8 + (j + 1))
                        pe.sem_inc(s["units_used"], 2)

            def down_products(it, n):
                pe.wait_ge(s["act_ready"], it * 8 + 9)
                for m in range(KD):
                    u = GU_UNITS + m // 2
                    if m % 2 == 0:
                        pe.wait_ge(s_w[u], it * 16 + 16)
                    pe.wait_ge(s["yT_act"] if m % 2 == 0 else s["yT_dve"], it * 4 + 1 + m // 2)
                    for k in range(KD):
                        last = mm(ps[:, 4 + m % 2, 0:n], slot(u)[:, k, P * (m % 2):P * (m % 2) + P], actT[:, k, 0:n], k == 0, k == KD - 1)
                    last.then_inc(s["down_ready"], 1)
                    if m % 2:
                        pe.wait_ge(s["down_ready"], it * 8 + (m + 1))
                        pe.sem_inc(s["units_used"], 1)

            turn_rows(0)
            with pe.Fori(0, MAX_ITEMS + 1) as it:
                size_last = pe.value_load(table[2:3, bass.ds(it, 1)], min_val=0, max_val=CAP + 1)
                kind_now = pe.value_load(table[3:4, bass.ds(it + 1, 1)], min_val=0, max_val=len(SIZES))
                for c, n in enumerate(SIZES):
                    with pe.If(kind_now == c + 1):
                        up_products(it, n)
                for b in range(BLOCKS):
                    with pe.If(size_last > P * b + 1):
                        pe.wait_ge(s["yT_act"], it * 4 + 1)
                        pe.wait_ge(s["yT_dve"], it * 4 + 1)
                        for half in range(2):
                            if b == 0:
                                pe.wait_ge(s["xT_act"] if half == 0 else s["xT_dve"], it * 4 + 4)
                            else:
                                pe.wait_ge(s_yact[b - 1] if half == 0 else s_ydve[b - 1], it + 1)
                            for m in range(4):
                                last = pe.transpose(ps[:, 6 + half, P * m:P * m + P], yT[:, 4 * half + m, P * b:P * b + P], ident[:, :])
                            last.then_inc(s_yps[b], 1)
                    with pe.Else():
                        pe.drain().then_inc(s_yps[b], 2)
                with pe.If(kind_now > 0):
                    for b in range(BLOCKS):
                        pe.wait_ge(s_yact[b], it + 1)
                        pe.wait_ge(s_ydve[b], it + 1)
                    turn_rows(it + 1)
                for c, n in enumerate(SIZES):
                    with pe.If(kind_now == c + 1):
                        down_products(it, n)

        @block.scalar
        def _(act):
            act.wait_ge(s["ident_made"], 2)
            for t in range(10):
                act.wait_ge(s_x[t % 4], 16 * (t // 4 + 1))
                act.activation(wk[:, 4, :], wk[:, t % 4, :], ACT.Square, accum_out=ssq[:, t:t + 1]).then_inc(s["act_chain"], 1)
                act.wait_ge(s["act_chain"], t + 1)
                act.activation(std[:, t:t + 1], ssq[:, t:t + 1], ACT.Sqrt, scale=1.0 / D, bias=eps[:, :]).then_inc(s["x_std"], 1)
                if t in (3, 7, 9):
                    act.wait_ge(s["x_turned"], t + 1)
                    if t == 3:
                        act.wait_ge(s["vecT_made"], 1)
                    for k in range(0, KD, 2):
                        gain = (mem_g if t == 9 else attn_g)[:, k:k + 1]
                        to = memT[:, k, :] if t == 9 else hT[:, k, HALF * (t // 4):HALF * (t // 4) + HALF]
                        act.activation(to, ps[:, k, 0:to.shape[1]], ACT.Identity, scale=gain).then_inc(s["h_act"], 1)
            for g in range(0, NG, 2):
                act.wait_ge(s["proj_done"], g + 1)
                if groups[g][1] == "line":
                    act.wait_ge(s["lists_blank"], 64)
                act.activation(group_dest(g), group_source(g), ACT.Copy).then_inc(s["proj_act"], 1)
            act.wait_ge(s["dve_chain"], 14)
            act.activation(lam[:, 2:4], lam[:, 0:2], ACT.Exp).then_inc(s["lam_exp"], 1)
            for i in range(NT + 1):
                if i < NT:
                    act.wait_ge(s["ms_done"], i + 1)
                    act.wait_ge(s["ms_max"], i + 1)
                    if i >= 2:
                        act.wait_ge(s["ms_turned"], i - 1)
                    for h in range(HEADS):
                        act.activation(wk[:, i % 2, MEM * h:MEM * h + MEM],
                                       ps[:, 2 * (i % 2) + h // 2, MEM * (h % 2):MEM * (h % 2) + MEM], ACT.Exp,
                                       scale=SCALE, bias=m_neg[:, i % 2, h:h + 1], accum_out=m_sum[:, i % 2, h:h + 1])\
                            .then_inc(s["ms_exp"], 1)
                if i >= 1:
                    j = i - 1
                    act.wait_ge(s["ms_turned"], j + 1)
                    if j >= 2:
                        act.wait_ge(s["ms_av"], j - 1)
                    act.activation(wk[:, 2 + j % 2, 0:512], ps[:, 4, :], ACT.Copy).then_inc(s["ms_t_act"], 1)

            NU = NT * HEADS
            act.wait_ge(s["ms_turned"], NT)
            act.wait_ge(s["ms_av"], NT)
            for j in range(NU + 2):
                if j < NU:
                    kv = P * (j // HEADS + 1)
                    for c in range(2):
                        act.wait_ge(s["ds_read"], 2 * j + c + 1)
                        src = wk[:, 2 * (j % 2) + c, 0:kv]
                        act.activation(src, src, ACT.Exp, bias=d_neg[:, j % 2, c:c + 1], accum_out=d_sum[:, j % 2, c:c + 1])\
                            .then_inc(s["ds_exp"], 1)
                if 1 <= j <= NU:
                    n = j - 1
                    nb = n // HEADS + 1
                    act.wait_ge(s["ds_turned"], n + 1)
                    if n >= 2:
                        act.wait_ge(s["ds_av"], n - 1)
                    act.activation(wk[:, 4 + n % 2, 0:P * nb], ps[:, 4:6, :].rearrange("p b n -> p (b n)")[:, 0:P * nb], ACT.Copy)\
                        .then_inc(s["ds_t_act"], 1)
                if j >= 2:
                    n = j - 2
                    i, h = divmod(n, HEADS)
                    act.wait_ge(s["ds_av"], n + 1)
                    act.activation(o_all[:, i, VD * h:VD * h + VD], ps[:, 6 + n % 2, 0:VD], ACT.Copy,
                                   scale=d_inv[:, n % 3, 0:1]).then_inc(s["ds_out"], 1)
                    act.wait_ge(s["ds_out"], n + 1)
                    act.activation(sq_junk[:, :], o_all[:, i, VD * h:VD * h + VD], ACT.Square,
                                   accum_out=o_ssq[:, n:n + 1]).then_inc(s["ds_sq"], 1)

            act.wait_ge(s["ds_sq"], NU)
            act.activation(o_std[:, :], o_ssq[:, :], ACT.Sqrt, scale=1.0 / VD, bias=eps[:, :]).then_inc(s["ds_sq"], 1)
            for i in range(NT + 1):
                if i < NT:
                    act.wait_ge(s["e_oT"], i + 1)
                    act.activation(mixT[:, 2:6, P * i:P * i + P], ps[:, 4, :].rearrange("p (h t) -> p h t", h=HEADS), ACT.Copy)\
                        .then_inc(s["e_oT_act"], 1)
                if i >= 1:
                    j = i - 1
                    act.wait_ge(s["e_x2"], 2 * j + 2)
                    act.activation(wk[:, 4, :], wk[:, j % 2, :], ACT.Square, accum_out=e_ssq[:, j:j + 1]).then_inc(s["act_chain"], 1)
                    act.wait_ge(s["act_chain"], 10 + j + 1)
                    act.activation(e_std[:, j:j + 1], e_ssq[:, j:j + 1], ACT.Sqrt, scale=1.0 / D, bias=eps[:, :]).then_inc(s["e_x2_sq"], 1)
                    act.wait_ge(s["e_hT"], j + 1)
                    if j >= 1:
                        act.wait_ge(s["e_log"], j)
                    for k in range(4):
                        last = act.activation(h2T[:, k, :], ps[:, 5, P * k:P * k + P], ACT.Identity, scale=ffn_g[:, k:k + 1])
                    last.then_inc(s["e_hT_act"], 1)
                    act.wait_ge(s["e_chosen"], j + 1)
                    act.activation(top_exp[:, :], top8[:, 0:TOPK], ACT.Exp, bias=top_neg[:, :], accum_out=top_sum[:, :]).then_inc(s["e_exp"], 1)

            act.preload_act_table(ACT.Sigmoid)
            act.wait_ge(s["tab_made"], 1)

            def xT_part(done):
                for k in range(0, KD, 2):
                    act.wait_ge(s["xT_ps"], done * 8 + (k + 1))
                    act.activation(xT[:, k, :], ps[:, 6, 0:CAP], ACT.Identity, scale=ffn_g[:, k:k + 1]).then_inc(s["xT_act"], 1)

            def gate_sigmoids(it, n):
                for j in range(KD):
                    act.wait_ge(s["gate_read"], it * 8 + 1 + (j + 1))
                    act.wait_ge(s["act_ready"], it * 8 + 1 + max(j - 1, 0))
                    act.activation(sig_b[:, j % 2, 0:n], gate_b[:, j % 2, 0:n], ACT.Sigmoid, scale=ALPHA).then_inc(s["sig_ready"], 1)

            def down_part(it, n):
                act.wait_ge(s["bias_now"], it * 2 + 2)
                for m in range(0, KD, 2):
                    act.wait_ge(s["down_ready"], it * 8 + (m + 1))
                    act.activation(yT[:, m, 0:n], ps[:, 4, 0:n], ACT.Identity, bias=b_now[:, 16 + m:17 + m]).then_inc(s["yT_act"], 1)

            xT_part(0)
            act.sem_inc(s["sig_ready"], 1)
            act.sem_inc(s["yT_act"], 1)
            with act.Fori(0, MAX_ITEMS + 1) as it:
                size_last = act.value_load(table[2:3, bass.ds(it, 1)], min_val=0, max_val=CAP + 1)
                kind_now = act.value_load(table[3:4, bass.ds(it + 1, 1)], min_val=0, max_val=len(SIZES))
                for c, n in enumerate(SIZES):
                    with act.If(kind_now == c + 1):
                        gate_sigmoids(it, n)
                for b in range(BLOCKS):
                    with act.If(size_last > P * b + 1):
                        act.wait_ge(s_yps[b], it * 2 + 1)
                        act.wait_ge(s["idx_moved"], it + 1)
                        act.wait_ge(s_scatter[b], it * 16 + 16)
                        act.activation(y_rows[:, b, 0:512], ps[:, 6, :], ACT.Copy, scale=idx_last[:, b, 1:2]).then_inc(s_yact[b], 1)
                    with act.Else():
                        act.drain().then_inc(s_yact[b], 1)
                with act.If(kind_now > 0):
                    xT_part(it + 1)
                for c, n in enumerate(SIZES):
                    with act.If(kind_now == c + 1):
                        down_part(it, n)
            for t in range(NT):
                act.wait_ge(s_final[t % 4], 16 * (t // 4 + 1))
                act.activation(wk[:, 4, :], wk[:, t % 4, :], ACT.Square, accum_out=e_ssq[:, t:t + 1]).then_inc(s["act_chain"], 1)
                act.wait_ge(s["act_chain"], 18 + t + 1)
                act.activation(e_std[:, t:t + 1], e_ssq[:, t:t + 1], ACT.Sqrt, scale=1.0 / D, bias=eps[:, :]).then_inc(s_fsq, 1)

        @block.vector
        def _(dve):
            chain = [0]

            def link(ins):
                chain[0] += 1
                ins.then_inc(s["dve_chain"], 1)
                dve.wait_ge(s["dve_chain"], chain[0])

            dve.wait_ge(s["vecT_ps"], 1)
            dve.tensor_copy(vecT[:, :], ps[:, 0, 0:30]).then_inc(s["vecT_made"], 1)
            dve.wait_ge(s["vecT_made"], 1)
            for t in range(10):
                dve.wait_ge(s["x_std"], t + 1)
                link(dve.reciprocal(rstd[:, t:t + 1], std[:, t:t + 1]))
                dve.tensor_scalar(wk[:, t % 4, :], wk[:, t % 4, :], rstd[:, t:t + 1], None, ALU.mult).then_inc(s["x_normed"], 1)
                if t in (3, 7, 9):
                    dve.wait_ge(s["x_turned"], t + 1)
                    for k in range(1, KD, 2):
                        gain = (mem_g if t == 9 else attn_g)[:, k:k + 1]
                        to = memT[:, k, :] if t == 9 else hT[:, k, HALF * (t // 4):HALF * (t // 4) + HALF]
                        dve.tensor_scalar(to, ps[:, k, 0:to.shape[1]], gain, None, ALU.mult).then_inc(s["h_dve"], 1)
            dve.wait_ge(s["small_in"], 80)
            lv = lam_in.rearrange("p (a d) -> p a d", a=4)
            link(dve.tensor_tensor(lv[:, 0, :], lv[:, 0, :], lv[:, 1, :], ALU.mult))
            link(dve.tensor_tensor(lv[:, 2, :], lv[:, 2, :], lv[:, 3, :], ALU.mult))
            link(dve.reduce_sum(lam[:, 0:1], lv[:, 0, :], axis=AX.X))
            link(dve.reduce_sum(lam[:, 1:2], lv[:, 2, :], axis=AX.X))
            link(dve.tensor_scalar(sub_g[:, :], sub_g[:, :], 1.0 - LAM_INIT, None, ALU.mult))
            lam_dots = chain[0]
            for g in range(1, NG, 2):
                dve.wait_ge(s["proj_done"], g + 1)
                if groups[g][1] == "line":
                    dve.wait_ge(s["lists_blank"], 64)
                dve.tensor_copy(group_dest(g), group_source(g)).then_inc(s["proj_dve"], 1)
                if g == conv_ready + 2:
                    dve.wait_ge(s["proj_act"], 6)
                    dve.wait_ge(s["proj_dve"], 6)
                    for c in range(2):
                        link(dve.tensor_tensor(conv_u[:, c, :], conv_u[:, c, :], conv_c[:, c, :], ALU.mult))
                        link(dve.tensor_scalar(conv_c[:, c, :], conv_u[:, c, :], taps[:, 4 + c:5 + c], None, ALU.mult))
                        for tap in range(2):
                            late = 2 - tap
                            link(dve.scalar_tensor_tensor(out=conv_c[:, c, late:S], in0=conv_u[:, c, 0:S - late],
                                                          scalar=taps[:, 2 * tap + c:2 * tap + c + 1],
                                                          in1=conv_c[:, c, late:S], op0=ALU.mult, op1=ALU.add))
                        link(dve.tensor_tensor(conv_b[:, c, :], conv_b[:, c, :], conv_c[:, c, :], ALU.mult))
            dve.wait_ge(s["proj_act"], NG // 2)
            link(dve.tensor_scalar(bguT[:, :, 8:16], bguT[:, :, 8:16], 1.0, None, ALU.add))

            for i in range(NT + 2):
                if i < NT:
                    dve.wait_ge(s["ms_done"], i + 1)
                    link(dve.tensor_reduce(m_max[:, i % 2, :], ps[:, 2 * (i % 2):2 * (i % 2) + 2, :].rearrange("p b (a n) -> p (b a) n", a=2),
                                           axis=AX.X, op=ALU.max))
                    if i >= 2:
                        dve.wait_ge(s["ms_exp"], 4 * (i - 1))
                    dve.tensor_scalar(m_neg[:, i % 2, :], m_max[:, i % 2, :], -SCALE, None, ALU.mult).then_inc(s["ms_max"], 1)
                    dve.wait_ge(s["ms_exp"], 4 * (i + 1))
                    link(dve.reciprocal(m_inv[:, i % 2, :], m_sum[:, i % 2, :]))
                    pv = wk[:, i % 2, :].rearrange("p (h n) -> p h n", h=HEADS)
                    dve.tensor_tensor(pv, pv, m_inv[:, i % 2, :].unsqueeze(2).broadcast_to((P, HEADS, MEM)), ALU.mult).then_inc(s["ms_prob"], 1)
                if 1 <= i <= NT:
                    j = i - 1
                    dve.wait_ge(s["ms_turned"], j + 1)
                    if j >= 2:
                        dve.wait_ge(s["ms_av"], j - 1)
                    dve.tensor_copy(wk[:, 2 + j % 2, 512:1024], ps[:, 5, :]).then_inc(s["ms_t_dve"], 1)
                if i >= 2:
                    j = i - 2
                    dve.wait_ge(s["ms_av"], j + 1)
                    dve.tensor_copy(mixT[:, 6:8, P * j:P * j + P], ps[:, 6 + j % 2, 0:256].rearrange("p (c t) -> p c t", c=2)).then_inc(s["ms_out"], 1)

            dve.wait_ge(s["lam_exp"], 1)
            link(dve.tensor_tensor(lam[:, 4:5], lam[:, 3:4], lam[:, 2:3], ALU.subtract))
            link(dve.tensor_scalar(lam[:, 5:6], lam[:, 4:5], -LAM_INIT, None, ALU.add))
            NU = NT * HEADS
            dve.wait_ge(s["ms_av"], NT)
            for j in range(NU + 1):
                if j < NU:
                    i, h = divmod(j, HEADS)
                    kv = P * (i + 1)
                    for c in range(2):
                        dve.wait_ge(s["ds_done"], 2 * j + c + 1)
                        if j >= 2:
                            dve.wait_ge(s["ds_turned"], j - 1)
                        sc = wk[:, 2 * (j % 2) + c, 0:kv]
                        raw = ps[:, 2 * c:2 * c + 2, :].rearrange("p b n -> p (b n)")[:, 0:kv]
                        link(dve.scalar_tensor_tensor(out=sc, in0=raw, scalar=SCALE, in1=master[:, h, S - kv:S], op0=ALU.mult, op1=ALU.add))
                        dve.tensor_reduce(d_neg[:, j % 2, c:c + 1], sc, axis=AX.X, op=ALU.max, negate=True).then_inc(s["ds_read"], 1)
                if j >= 1:
                    n = j - 1
                    kv = P * (n // HEADS + 1)
                    dve.wait_ge(s["ds_exp"], 2 * n + 2)
                    if n >= 3:
                        dve.wait_ge(s["ds_out"], n - 2)
                    link(dve.reciprocal(d_inv[:, n % 3, :], d_sum[:, n % 2, :]))
                    link(dve.scalar_tensor_tensor(out=d_lam[:, n % 2:n % 2 + 1], in0=d_sum[:, n % 2, 0:1], scalar=lam[:, 5:6],
                                                  in1=d_inv[:, n % 3, 1:2], op0=ALU.mult, op1=ALU.mult))
                    p0, p1 = wk[:, 2 * (n % 2), 0:kv], wk[:, 2 * (n % 2) + 1, 0:kv]
                    dve.scalar_tensor_tensor(out=p0, in0=p1, scalar=d_lam[:, n % 2:n % 2 + 1], in1=p0, op0=ALU.mult, op1=ALU.add)\
                        .then_inc(s["ds_diff"], 1)

            dve.wait_ge(s["ds_sq"], NU + 1)
            link(dve.reciprocal(o_rs[:, :], o_std[:, :]))

            def norm_heads(i):
                ov = o_all[:, i, :].rearrange("p (h n) -> p h n", h=HEADS)
                link(dve.tensor_tensor(ov, ov, o_rs[:, HEADS * i:HEADS * i + HEADS].unsqueeze(2).broadcast_to((P, HEADS, VD)), ALU.mult))
                dve.tensor_tensor(ov, ov, sub_g[:, :].unsqueeze(1).broadcast_to((P, HEADS, VD)), ALU.mult).then_inc(s["e_y"], 1)

            def ranks_read(j):
                dve.wait_ge(s["e_rank"], j + 1)
                dve.tensor_copy(place[:, :], ps[:, 4, 0:EXPERTS]).then_inc(s["e_rank_read"], 1)
                dve.wait_ge(s["e_rank_read"], j + 1)

            norm_heads(0)
            dve.wait_ge(s["consts_made"], 1)
            for i in range(NT + 2):
                if i < NT:
                    if i + 1 < NT:
                        norm_heads(i + 1)
                    dve.wait_ge(s_x[i % 2], 16 * (3 + i // 2 + 1))
                    for half in range(2):
                        dve.wait_ge(s["e_mix"], 2 * i + half + 1)
                        x_half = wk[:, i % 2, HALF * half:HALF * half + HALF]
                        dve.tensor_tensor(x_half, ps[:, 2 * (i % 2) + half, :], x_half, ALU.add).then_inc(s["e_x2"], 1)
                    dve.wait_ge(s["e_x2_sq"], i + 1)
                    link(dve.reciprocal(e_rstd[:, i:i + 1], e_std[:, i:i + 1]))
                    if i >= 2:
                        dve.wait_ge(s[f"xn_out{i % 2}"], 16 * (i // 2))
                        dve.wait_ge(s["e_hT"], i - 1)
                    dve.wait_ge(s["e_x2"], 2 * i + 2)
                    dve.tensor_scalar(wk[:, 2 + i % 2, :], wk[:, i % 2, :], e_rstd[:, i:i + 1], None, ALU.mult).then_inc(s["e_xn"], 1)
                    j = i
                    dve.wait_ge(s["e_hT"], j + 1)
                    if j >= 1:
                        dve.wait_ge(s["e_log"], j)
                    for k in range(4, 8):
                        last = dve.tensor_scalar(h2T[:, k, :], ps[:, 6, P * (k - 4):P * (k - 4) + P], ffn_g[:, k:k + 1], None, ALU.mult)
                    last.then_inc(s["e_hT_dve"], 1)
                    dve.wait_ge(s["e_log"], j + 1)
                    dve.tensor_tensor(logits[:, :], ps[:, 7, 0:EXPERTS], router_b[:, :], ALU.add).then_inc(s["e_log_read"], 1)
                    dve.wait_ge(s["e_log_read"], j + 1)
                    link(dve.max(top8[:, :], logits[:, :]))
                    link(dve.tensor_scalar(top_neg[:, :], top8[:, 0:1], -1.0, None, ALU.mult))
                    link(dve.max_index(top8i[:, :], top8[:, :], logits[:, :]))
                    link(dve.tensor_copy(top_e[:, j, :], top8i[:, 0:TOPK]))
                    link(dve.tensor_scalar(chosen[:, :], iota_e[:, :], top_e[:, j, 0:1], None, ALU.is_equal))
                    for c in range(1, TOPK):
                        to = chosen_b[:, j, :] if c == TOPK - 1 else chosen[:, :]
                        ins = dve.scalar_tensor_tensor(out=to, in0=iota_e[:, :], scalar=top_e[:, j, c:c + 1], in1=chosen[:, :],
                                                       op0=ALU.is_equal, op1=ALU.add)
                        if c < TOPK - 1:
                            link(ins)
                        else:
                            ins.then_inc(s["e_chosen"], 1)
                    dve.wait_ge(s["e_exp"], j + 1)
                    link(dve.reciprocal(top_inv[:, :], top_sum[:, :]))
                    link(dve.tensor_scalar(pay[:, j, :, 1], top_exp[:, :], top_inv[:, :], None, ALU.mult))
                if 1 <= i <= NT:
                    j = i - 1
                    ranks_read(j)
                    link(dve.scalar_tensor_tensor(out=place[:, :], in0=iota_e[:, :], scalar=float(S), in1=place[:, :], op0=ALU.mult, op1=ALU.add))
                    for c in range(TOPK):
                        ins = dve.scalar_tensor_tensor(out=dest_j[:, c, :], in0=iota_e[:, :], scalar=top_e[:, j, c:c + 1], in1=place[:, :],
                                                       op0=ALU.is_equal, op1=ALU.mult)
                    link(ins)
                    link(dve.reduce_sum(dest_f[:, j, :], dest_j[:, :, :], axis=AX.X))
                    dve.tensor_copy(dest_i[:, j, :], dest_f[:, j, :]).then_inc(s["e_dest"], 1)

            ranks_read(NT)
            cnt, nch, end, start, tmp, oh = (t32[:, n, :] for n in range(6))
            e0 = place[0:64, :]
            jj = iota_p[0:64, :]
            link(dve.tensor_copy(cnt, e0))
            link(dve.tensor_scalar(nch, cnt, float(CAP), 1.0, ALU.is_gt, ALU.add))
            link(dve.scalar_tensor_tensor(out=nch, in0=cnt, scalar=float(2 * CAP), in1=nch, op0=ALU.is_gt, op1=ALU.add))
            link(dve.memset(tmp, 1.0))
            link(dve.tensor_tensor_scan(end, tmp, nch, 0.0, ALU.mult, ALU.add))
            link(dve.tensor_tensor(start, end, nch, ALU.subtract))
            link(dve.tensor_scalar(tmp, end, jj, None, ALU.is_le))
            link(dve.reduce_sum(t1[:, 0:1], tmp, axis=AX.X))
            link(dve.scalar_tensor_tensor(out=tmp, in0=start, scalar=jj, in1=start, op0=ALU.is_le, op1=ALU.mult))
            link(dve.tensor_reduce(t1[:, 1:2], tmp, axis=AX.X, op=ALU.max))
            link(dve.scalar_tensor_tensor(out=oh, in0=iota_e[0:64, :], scalar=t1[:, 0:1], in1=cnt, op0=ALU.is_equal, op1=ALU.mult))
            link(dve.reduce_sum(t1[:, 2:3], oh, axis=AX.X))
            link(dve.tensor_tensor(t1[:, 3:4], jj, t1[:, 1:2], ALU.subtract))
            link(dve.scalar_tensor_tensor(out=t1[:, 4:5], in0=t1[:, 3:4], scalar=-float(CAP), in1=t1[:, 2:3], op0=ALU.mult, op1=ALU.add))
            link(dve.tensor_scalar(t1[:, 4:5], t1[:, 4:5], float(CAP), None, ALU.min))
            link(dve.tensor_scalar(t1[:, 5:6], t1[:, 0:1], float(EXPERTS), None, ALU.is_lt))
            link(dve.scalar_tensor_tensor(out=t1[:, 5:6], in0=jj, scalar=0.0, in1=t1[:, 5:6], op0=ALU.is_ge, op1=ALU.mult))
            link(dve.tensor_tensor(table_f[:, 0:1], t1[:, 0:1], t1[:, 5:6], ALU.mult))
            link(dve.tensor_scalar(t1[:, 6:7], t1[:, 3:4], float(CAP), None, ALU.mult))
            link(dve.scalar_tensor_tensor(out=t1[:, 6:7], in0=t1[:, 0:1], scalar=float(S), in1=t1[:, 6:7], op0=ALU.mult, op1=ALU.add))
            link(dve.tensor_tensor(table_f[:, 1:2], t1[:, 6:7], t1[:, 5:6], ALU.mult))
            link(dve.scalar_tensor_tensor(out=table_f[:, 2:3], in0=t1[:, 4:5], scalar=1.0, in1=t1[:, 5:6], op0=ALU.add, op1=ALU.mult))
            link(dve.tensor_scalar(t1[:, 7:8], t1[:, 4:5], float(SIZES[0]), 1.0, ALU.is_gt, ALU.add))
            for n in SIZES[1:-1]:
                link(dve.scalar_tensor_tensor(out=t1[:, 7:8], in0=t1[:, 4:5], scalar=float(n), in1=t1[:, 7:8], op0=ALU.is_gt, op1=ALU.add))
            dve.tensor_tensor(table_f[:, 3:4], t1[:, 7:8], t1[:, 5:6], ALU.mult).then_inc(s["tab_f"], 1)
            dve.wait_ge(s["tab_ps"], 1)
            dve.tensor_copy(table[:, :], ps[0:4, 5, 0:64]).then_inc(s["tab_made"], 1)
            dve.wait_ge(s["tab_made"], 1)

            def xT_part(done):
                for k in range(1, KD, 2):
                    dve.wait_ge(s["xT_ps"], done * 8 + (k + 1))
                    dve.tensor_scalar(xT[:, k, :], ps[:, 7, 0:CAP], ffn_g[:, k:k + 1], None, ALU.mult).then_inc(s["xT_dve"], 1)

            def activations(it, n):
                dve.wait_ge(s["bias_now"], it * 2 + 2)
                for j in range(KD + 1):
                    if j < KD:
                        g, u = gate_b[:, j % 2, 0:n], up_b[:, j % 2, 0:n]
                        dve.wait_ge(s["gate_ready"], it * 8 + (j + 1))
                        dve.wait_ge(s["sig_ready"], it * 8 + 1 + max(j - 1, 0))
                        dve.wait_ge(s["act_ready"], it * 8 + 1 + max(j - 1, 0))
                        dve.tensor_scalar(g, ps[:, j % 2, 0:n], b_now[:, j:j + 1], LIMIT, ALU.add, ALU.min).then_inc(s["gate_read"], 1)
                        dve.wait_ge(s["up_ready"], it * 8 + (j + 1))
                        dve.tensor_scalar(u, ps[:, 2 + j % 2, 0:n], b_now[:, 8 + j:9 + j], LIMIT + 1.0, ALU.add, ALU.min).then_inc(s["up_read"], 1)
                    if j >= 1:
                        m = j - 1
                        g, u, sg = gate_b[:, m % 2, 0:n], up_b[:, m % 2, 0:n], sig_b[:, m % 2, 0:n]
                        dve.wait_ge(s["sig_ready"], it * 8 + 1 + j)
                        dve.wait_ge(s["up_read"], it * 8 + 1 + j)
                        dve.tensor_tensor(sg, g, sg, ALU.mult).then_inc(s["silu"], 1)
                        dve.wait_ge(s["silu"], it * 8 + j)
                        dve.scalar_tensor_tensor(out=actT[:, m, 0:n], in0=u, scalar=1.0 - LIMIT, in1=sg, op0=ALU.max, op1=ALU.mult)\
                            .then_inc(s["act_ready"], 1)

            def down_part(it, n):
                for m in range(1, KD, 2):
                    dve.wait_ge(s["down_ready"], it * 8 + (m + 1))
                    dve.tensor_scalar(yT[:, m, 0:n], ps[:, 5, 0:n], b_now[:, 16 + m:17 + m], None, ALU.add).then_inc(s["yT_dve"], 1)

            xT_part(0)
            for name in ("gate_read", "up_read", "act_ready", "yT_dve"):
                dve.sem_inc(s[name], 1)
            with dve.Fori(0, MAX_ITEMS + 1) as it:
                size_last = dve.value_load(table[2:3, bass.ds(it, 1)], min_val=0, max_val=CAP + 1)
                kind_now = dve.value_load(table[3:4, bass.ds(it + 1, 1)], min_val=0, max_val=len(SIZES))
                with dve.If(kind_now > 0):
                    e = dve.value_load(table[0:1, bass.ds(it + 1, 1)], min_val=0, max_val=EXPERTS - 1)
                    dve.wait_ge(s["yT_act"], it * 4 + 1)
                    dve.wait_ge(s["yT_dve"], it * 4 + 1)
                    dve.tensor_copy(b_now[:, 0:16], bguT[:, bass.ds(e, 1), :].rearrange("p e m -> p (e m)")).then_inc(s["bias_now"], 1)
                    dve.tensor_copy(b_now[:, 16:24], bdnT[:, bass.ds(e, 1), :].rearrange("p e m -> p (e m)")).then_inc(s["bias_now"], 1)
                for c, n in enumerate(SIZES):
                    with dve.If(kind_now == c + 1):
                        activations(it, n)
                for b in range(BLOCKS):
                    with dve.If(size_last > P * b + 1):
                        dve.wait_ge(s_yps[b], it * 2 + 2)
                        dve.wait_ge(s["idx_moved"], it + 1)
                        dve.wait_ge(s_scatter[b], it * 16 + 16)
                        dve.tensor_scalar(y_rows[:, b, 512:1024], ps[:, 7, :], idx_last[:, b, 1:2], None, ALU.mult).then_inc(s_ydve[b], 1)
                    with dve.Else():
                        dve.drain().then_inc(s_ydve[b], 1)
                with dve.If(kind_now > 0):
                    xT_part(it + 1)
                for c, n in enumerate(SIZES):
                    with dve.If(kind_now == c + 1):
                        down_part(it, n)
            dve.wait_ge(s_gf, 16)
            for t in range(NT):
                dve.wait_ge(s_fsq, t + 1)
                link(dve.reciprocal(e_rstd[:, t:t + 1], e_std[:, t:t + 1]))
                dve.scalar_tensor_tensor(out=wk[:, t % 4, :], in0=wk[:, t % 4, :], scalar=e_rstd[:, t:t + 1], in1=wk[:, 5, :],
                                         op0=ALU.mult, op1=ALU.mult).then_inc(s_fdone, 1)


_INS = ["x", "mem", "rel_bias", "attn_norm_g", "w_mix_in", "conv_w", "lambda_qk", "diff_subln_g", "mem_norm_g",
        "w_mem_kv", "w_mix_out", "ffn_norm_g", "router_w", "router_b", "w_gate_up", "b_gate_up", "w_down", "b_down",
        "final_norm_g"]


def kernel(**inputs):
    import concourse.bacc as _bacc
    from concourse.bass_utils import run_bass_kernel_spmd as _run

    nc = _bacc.Bacc("TRN2", target_bir_lowering=False, num_devices=1)
    arrays, aps = {}, {}
    for name in _INS:
        arrays[f"in_{name}"] = np.ascontiguousarray(inputs[name])
    arrays["in_distance_one_hot"] = distance_one_hot()
    for key, value in arrays.items():
        aps[key[3:]] = nc.dram_tensor(key, value.shape, mybir.dt.from_np(value.dtype), kind="ExternalInput").ap()
    out = nc.dram_tensor("out_rows", (1, S, D), f32, kind="ExternalOutput").ap()
    hymba_kernel(nc, aps, out)
    r = _run(nc, [arrays], core_ids=[0])
    return r.results[0]["out_rows"]
```

```python
import math
from contextlib import ExitStack

import numpy as np
import concourse.bass as bass
from concourse import mybir

f32 = mybir.dt.float32
bf16 = mybir.dt.bfloat16
i32 = mybir.dt.int32
u32 = mybir.dt.uint32
ALU = mybir.AluOpType
ACT = mybir.ActivationFunctionType
AX = mybir.AxisListType

P = 128
D = 1024
S = 1024
KD = D // P
NT = S // P
HALF = 512
MEM = 256
HEADS = 4
QK = 64
VD = 128
UW = 256
EXPERTS = 32
TOPK = 4
BUCKETS = 32
MAX_DISTANCE = 128
EPS = 1e-5
NEG = -1e30
LAM_INIT = 0.8 - 0.6 * math.exp(-0.3 * 0)
ALPHA = 1.702
LIMIT = 7.0
SCALE = QK ** -0.5

SLOTS = 12
PHASE1_SLOTS = 4
GU_UNITS = 8
DOWN_UNITS = 4
CAP = 384
BLOCKS = CAP // P
MAX_ITEMS = EXPERTS + S * TOPK // CAP
ENTRIES = MAX_ITEMS + 2
SIZES = [128, 144, 160, 176, 192, 224, 256, 288, 320, 352, 384]
LIST = EXPERTS * S
LIST_PAD = P
ROWS = S + P

LINE = S + P


def distance_one_hot():
    n = np.arange(S - 1, -1, -1, dtype=np.int32)
    exact = BUCKETS // 2
    nf = np.maximum(n, 1).astype(np.float32)
    large = exact + (np.log(nf / np.float32(exact)) / np.float32(math.log(MAX_DISTANCE / exact))
                     * np.float32(BUCKETS - exact)).astype(np.int32)
    bucket = np.where(n < exact, n, np.minimum(large, BUCKETS - 1))
    return (np.arange(BUCKETS)[:, None] == bucket[None, :]).astype(np.float32)


def hymba_kernel(nc, a, out):
    ctx = ExitStack()
    with ctx:
        def sb(name, shape, dt=f32):
            return ctx.enter_context(nc.sbuf_tensor(name, shape, dt))

        def sem(name):
            return ctx.enter_context(nc.semaphore(name))

        line_d = nc.dram_tensor("bias_line", (HEADS, LINE), f32, kind="Internal").ap()
        h_d = nc.dram_tensor("normed_rows", (ROWS, D), f32, kind="Internal").ap()
        acc_d = nc.dram_tensor("residual_rows", (ROWS, D), f32, kind="Internal").ap()
        list_d = nc.dram_tensor("expert_lists", (LIST + LIST_PAD, 2), f32, kind="Internal").ap()

        ring = sb("weight_ring", [P, SLOTS, KD * UW])
        mixT = sb("mixT_hT", [P, KD, S])
        r_v = sb("region_v", [P, 4096])
        r_bias = sb("region_bias", [P, 4096])
        r_mem = sb("region_mem", [P, 3072])
        work = sb("work", [P, 6144])

        def slot(s):
            return ring[:, s, :].rearrange("p (k c) -> p k c", k=KD)

        def home(u):
            return (u + PHASE1_SLOTS) % SLOTS

        def arrived(u, it):
            before = 4 if home(u) < PHASE1_SLOTS else 0
            return it * 16 + 16 * (before + 1)

        def x_tile(t):
            return ring[:, 4 + t // 2, D * (t % 2):D * (t % 2) + D]

        hT = mixT
        qT = ring[:, 4:6, :].rearrange("p s n -> p (s n)").rearrange("p (h t) -> p h t", t=S)
        kT = ring[:, 6:8, :].rearrange("p s n -> p (s n)").rearrange("p (h t) -> p h t", t=S)
        conv_u = ring[:, 8, :].rearrange("p (c t) -> p c t", t=S)
        conv_c = ring[:, 9, :].rearrange("p (c t) -> p c t", t=S)
        conv_b = ring[:, 10, :].rearrange("p (c t) -> p c t", t=S)
        memT = ring[:, 11, :].rearrange("p (k t) -> p k t", t=MEM)
        o_all = ring[:, 8:10, :].rearrange("p s n -> p (s n)").rearrange("p (i n) -> p i n", i=NT)
        v_rows = r_v[:, :].rearrange("p (t n) -> p t n", t=NT)
        master = r_bias[:, :].rearrange("p (h y) -> p h y", h=HEADS)
        qmT = r_mem[:, 0:2048].rearrange("p (c t) -> p c t", t=S)
        kmT = r_mem[:, 2048:2560].rearrange("p (c t) -> p c t", t=MEM)
        vm = r_mem[:, 2560:3072].rearrange("p (m n) -> p m n", m=2)
        wk = work[:, :].rearrange("p (s n) -> p s n", n=1024)
        xg = r_v[:, 0:BLOCKS * D].rearrange("p (b n) -> p b n", b=BLOCKS)
        xT = r_bias[:, 0:KD * CAP].rearrange("p (k t) -> p k t", k=KD)
        actT = r_mem[:, 0:KD * CAP].rearrange("p (k t) -> p k t", k=KD)
        flat_mix = mixT[:, :, :].rearrange("p k t -> p (k t)")
        yT = flat_mix[:, 0:KD * CAP].rearrange("p (k t) -> p k t", k=KD)
        y_rows = flat_mix[:, KD * CAP:KD * CAP + BLOCKS * D].rearrange("p (b n) -> p b n", b=BLOCKS)
        gate_b = work[:, 0:2 * CAP].rearrange("p (s n) -> p s n", s=2)
        sig_b = work[:, 2 * CAP:4 * CAP].rearrange("p (s n) -> p s n", s=2)
        up_b = work[:, 4 * CAP:6 * CAP].rearrange("p (s n) -> p s n", s=2)

        ident = sb("ident", [P, P])
        tri = sb("tri", [P, P], bf16)
        ones_b = sb("ones_b", [P, P], bf16)
        vecs = sb("vecs", [22, P])
        vecT = sb("vecT", [P, 22])
        attn_g, mem_g = (vecT[:, 8 * n:8 * n + 8] for n in range(2))
        ffn_g = r_bias[:, 0:D]
        taps = vecT[:, 16:22]
        lam_in = r_mem[:, 0:4 * QK]
        lam = sb("lam", [P, 8])
        sub_g = sb("sub_g", [P, VD])
        rel = sb("rel", [BUCKETS, HEADS])
        router_w = sb("router_w", [P, KD, EXPERTS])
        router_b = sb("router_b", [P, EXPERTS])
        bgu_rows = wk[:, 4, 0:512].rearrange("p (a n) -> p a n", a=4)
        bdn_rows = wk[:, 4, 512:768].rearrange("p (a n) -> p a n", a=2)
        bguT = sb("bguT", [P, EXPERTS, 16])
        bdnT = sb("bdnT", [P, EXPERTS, 8])
        b_now = sb("b_now", [P, 24])
        line = wk[0:HEADS, 5, :]
        line_neg = sb("line_neg", [HEADS, P])
        one_hot = master[0:BUCKETS, 3, :]
        shifted = work[:, 0:HEADS * S].rearrange("p (h y) -> p h y", h=HEADS)
        rev = sb("rev", [P, P])
        eps = sb("eps", [P, 1])
        ssq = sb("ssq", [P, 10])
        std = sb("std", [P, 10])
        rstd = sb("rstd", [P, 10])
        m_max = sb("m_max", [P, 2, HEADS])
        m_neg = sb("m_neg", [P, 2, HEADS])
        m_sum = sb("m_sum", [P, 2, HEADS])
        m_inv = sb("m_inv", [P, 2, HEADS])
        d_neg = sb("d_neg", [P, 2, 2])
        d_sum = sb("d_sum", [P, 2, 2])
        d_inv = sb("d_inv", [P, 3, 2])
        d_lam = sb("d_lam", [P, 2])
        sq_junk = r_mem[:, 0:VD]
        o_ssq = sb("o_ssq", [P, NT * HEADS])
        o_std = sb("o_std", [P, NT * HEADS])
        o_rs = sb("o_rs", [P, NT * HEADS])
        e_ssq = sb("e_ssq", [P, NT])
        e_std = sb("e_std", [P, NT])
        e_rstd = sb("e_rstd", [P, NT])
        h2T = wk[:, 5, :].rearrange("p (k t) -> p k t", k=KD)
        logits = sb("logits", [P, EXPERTS])
        top8 = sb("top8", [P, 8])
        top8i = sb("top8i", [P, 8], u32)
        top_e = sb("top_e", [P, NT, TOPK])
        top_neg = sb("top_neg", [P, 1])
        top_exp = sb("top_exp", [P, TOPK])
        top_sum = sb("top_sum", [P, 1])
        top_inv = sb("top_inv", [P, 1])
        chosen = sb("chosen", [P, EXPERTS])
        chosen_b = sb("chosen_b", [P, NT, EXPERTS], bf16)
        iota_e = sb("iota_e", [P, EXPERTS])
        iota_ei = sb("iota_ei", [P, EXPERTS], i32)
        place = sb("place", [P, EXPERTS])
        dest_j = sb("dest_j", [P, TOPK, EXPERTS])
        dest_f = sb("dest_f", [P, NT, TOPK])
        dest_i = sb("dest_i", [P, NT, TOPK], i32)
        pay = sb("pay", [P, NT, TOPK, 2])
        blank = wk[:, 5, 0:512].rearrange("p (n two) -> p n two", two=2)
        zeros = wk[:, 5, 512:768]
        iota_p = sb("iota_p", [P, 1])
        iota_pi = sb("iota_pi", [P, 1], i32)
        t32 = wk[0:64, 4, 0:256].rearrange("p (a e) -> p a e", e=EXPERTS)
        t1 = sb("t1", [64, 16])
        table_f = sb("table_f", [64, 4])
        table = sb("table", [4, 64], i32)
        idx_next = sb("idx_next", [P, BLOCKS, 2])
        idx_now = sb("idx_now", [P, BLOCKS, 2])
        idx_last = sb("idx_last", [P, BLOCKS, 2])
        nothing = sb("nothing", [1, 2 * BLOCKS, 16])

        ps = ctx.enter_context(nc.psum_tensor("ps", [P, 8, 512], f32))

        names = (
            "ident_made", "consts_made", "vecs_in", "vecT_ps", "vecT_made", "small_in", "mem_bias_in", "line_out",
            "shifted_in", "lists_blank", "x_std", "x_normed", "x_turned", "h_act", "h_dve",
            "proj_done", "proj_act", "proj_dve", "act_chain", "dve_chain", "pool_chain",
            "ms_done", "ms_max", "ms_exp", "ms_prob", "ms_turned", "ms_t_act", "ms_t_dve", "ms_av", "ms_out",
            "ds_done", "ds_read", "ds_exp", "ds_diff", "ds_turned", "ds_t_act", "ds_av", "ds_out", "ds_sq",
            "e_y", "e_oT", "e_oT_act", "e_mix", "e_x2", "e_x2_sq", "e_xn", "e_hT", "e_hT_act", "e_hT_dve",
            "e_log", "e_log_read", "e_chosen", "e_exp", "e_rank", "e_rank_read", "e_dest", "x2_out", "xn_out0",
            "listed", "lam_exp", "pool_waited", "silu", "xn_out1", "listed_f", "tab_f", "tab_ps", "tab_made",
            "gain_in", "gate_ready", "gate_read", "sig_ready", "up_ready", "up_read", "act_ready",
            "down_ready", "yT_act", "yT_dve", "idx_in", "idx_moved", "all_added", "bias_now",
        )
        s = {n: sem(n) for n in names}
        s_x = [sem(f"x_in{n}") for n in range(10)]
        s_w = [sem(f"w_in{n}") for n in range(SLOTS)]
        s_gather = [sem(f"gathered{b}") for b in range(BLOCKS)]
        s_scatter = [sem(f"scattered{b}") for b in range(BLOCKS)]
        s_yps = [sem(f"y_ps{b}") for b in range(BLOCKS)]
        s_yact = [sem(f"y_act{b}") for b in range(BLOCKS)]
        s_ydve = [sem(f"y_dve{b}") for b in range(BLOCKS)]
        s_xps = [sem(f"x_ps{b}") for b in range(BLOCKS)]
        s_xact = [sem(f"x_act{b}") for b in range(BLOCKS)]
        s_xdve = [sem(f"x_dve{b}") for b in range(BLOCKS)]
        s_final = [sem(f"final_in{n}") for n in range(4)]
        s_fout = [sem(f"final_out{n}") for n in range(4)]
        s_gf = sem("final_gain_in")
        s_fsq = sem("final_std")
        s_fdone = sem("final_done")

        w_in = a["w_mix_in"][0].rearrange("(k p) n -> p k n", p=P)
        w_kv = a["w_mem_kv"][0].rearrange("(k p) n -> p k n", p=P)
        w_out = a["w_mix_out"][0].rearrange("(k p) n -> p k n", p=P)
        units = [w_in[:, :, UW * u:UW * u + UW] for u in range(10)]
        units += [w_kv[:, :, UW * u:UW * u + UW] for u in range(2)]
        units += [w_out[:, :, UW * u:UW * u + UW] for u in range(4)]
        groups = []
        for u in range(10):
            if u == 3:
                groups += [(-1, "line", n, 0) for n in range(2)]
            if u == 6:
                groups += [(-1, "bgu", 0, 0), (-1, "bdn", 0, 0)]
                groups += [(-1, "rev", n // 2, n % 2) for n in range(2 * HEADS)]
            if u in (7, 8):
                groups += [(u, "v", t, 0) for t in range(0, NT, 2)]
            else:
                groups += [(u, "t", m, half) for half in range(2) for m in range(2)]
        groups += [(10, "km", 0, 0), (11, "vm", 0, 0)]
        wide = {0: conv_u, 1: conv_b, 2: conv_c, 9: qmT}

        def group_dest(g):
            u, kind, x, half = groups[g]
            if kind == "v":
                return v_rows[:, x:x + 2, UW * (u - 7):UW * (u - 7) + UW]
            if kind == "line":
                return line[:, 512 * x:512 * x + 512]
            if kind == "rev":
                return master[:, x, HALF * half:HALF * half + HALF]
            if kind == "bgu":
                return bguT[:, :, :].rearrange("p e m -> p (e m)")
            if kind == "bdn":
                return bdnT[:, :, :].rearrange("p e m -> p (e m)")
            if kind == "km":
                return kmT
            if kind == "vm":
                return vm
            if u in wide:
                return wide[u][:, x, HALF * half:HALF * half + HALF]
            to, first = (qT, 3) if u < 5 else (kT, 5)
            return to[:, 2 * (u - first) + x, HALF * half:HALF * half + HALF]

        def group_source(g):
            bank = ps[:, g % 8, :]
            kind = groups[g][1]
            if kind in ("v", "km", "vm"):
                return bank.rearrange("p (a n) -> p a n", a=2)
            return {"line": bank[0:HEADS, :], "bdn": bank[:, 0:256]}.get(kind, bank)

        NG = len(groups)
        first_of = {kind: min(g for g in range(NG) if groups[g][1] == kind) for kind in ("line", "bgu", "rev")}
        conv_ready = max(g for g in range(NG) if groups[g][0] in (0, 1, 2))

        def for_size(eng, kind, body, low=0, high=len(SIZES) + 1):
            if high - low == 1:
                body(SIZES[low] if low < len(SIZES) else 0)
                return
            mid = (low + high) // 2
            with eng.If(kind < mid + 1):
                for_size(eng, kind, body, low, mid)
            with eng.Else():
                for_size(eng, kind, body, mid, high)

        block = ctx.enter_context(nc.Block())

        @block.sync
        def _(sp):
            x_v = a["x"][0]
            mem_v = a["mem"][0]

            def load_x(t):
                src = x_v[P * t:P * t + P, :] if t < NT else mem_v[P * (t - NT):P * (t - NT) + P, :]
                sp.dma_start(x_tile(t), src).then_inc(s_x[t], 16)

            def load_unit(n):
                if n >= PHASE1_SLOTS:
                    last = max(g for g in range(NG) if groups[g][0] == n - PHASE1_SLOTS)
                    sp.wait_ge(s["proj_done"], last + 1)
                sp.dma_start(slot(n % PHASE1_SLOTS), units[n]).then_inc(s_w[n % PHASE1_SLOTS], 16)

            load_x(0)
            for n, name in enumerate(("attn_norm_g", "mem_norm_g")):
                sp.dma_start(vecs[8 * n:8 * n + 8, :], a[name][0].rearrange("(k p) -> k p", p=P)).then_inc(s["vecs_in"], 16)
            sp.dma_start(vecs[16:22, :], a["conv_w"][0].rearrange("t (c p) -> (t c) p", p=P)).then_inc(s["vecs_in"], 16)
            for t in range(1, 10):
                load_x(t)
            for n in range(4):
                load_unit(n)
            sp.dma_start(lam_in, a["lambda_qk"][0].rearrange("a d -> (a d)").partition_broadcast(P)).then_inc(s["small_in"], 16)
            sp.dma_start(sub_g[:, :], a["diff_subln_g"][0].partition_broadcast(P)).then_inc(s["small_in"], 16)
            sp.dma_start(rel[:, :], a["rel_bias"]).then_inc(s["small_in"], 16)
            sp.dma_start(router_w[:, :, :], a["router_w"][0].rearrange("(k p) e -> p k e", p=P)).then_inc(s["small_in"], 16)
            sp.dma_start(router_b[:, :], a["router_b"][0].partition_broadcast(P)).then_inc(s["small_in"], 16)
            sp.wait_ge(s["x_turned"], 10)
            sp.dma_start(bgu_rows, a["b_gate_up"][0].rearrange("(g e) (m p) -> (e m) g p", g=4, p=P)).then_inc(s["mem_bias_in"], 16)
            sp.dma_start(bdn_rows, a["b_down"][0].rearrange("(g e) (m p) -> (e m) g p", g=2, p=P)).then_inc(s["mem_bias_in"], 16)
            sp.dma_start(one_hot, a["distance_one_hot"]).then_inc(s["mem_bias_in"], 16)
            for n in range(4, 6):
                load_unit(n)
            assert first_of["line"] % 2 == 0
            sp.wait_ge(s["proj_act"], first_of["line"] // 2 + 1)
            sp.wait_ge(s["proj_dve"], first_of["line"] // 2 + 1)
            sp.dma_start(line_d[:, 0:S], line).then_inc(s["line_out"], 16)
            sp.wait_ge(s["consts_made"], 1)
            sp.dma_start(line_d[:, S:LINE], line_neg[:, :]).then_inc(s["line_out"], 16)
            sp.wait_ge(s["line_out"], 32)
            sp.dma_start(shifted, bass.AP(line_d.tensor, 0, [[1, P], [LINE, HEADS], [1, S]])).then_inc(s["shifted_in"], 16)
            for n in range(6, 16):
                load_unit(n)
            w_gu = a["w_gate_up"][0].rearrange("e (k p) n -> p e k n", p=P)
            w_dn = a["w_down"][0].rearrange("e (k p) n -> p e k n", p=P)

            def unit_source(e, u):
                if u < GU_UNITS:
                    col = D * (u % 2) + UW * (u // 2)
                    w = w_gu
                else:
                    col = UW * (u - GU_UNITS)
                    w = w_dn
                return w[:, bass.ds(e, 1), :, col:col + UW].rearrange("p e k n -> p (e k) n")

            def load_first(u):
                sp.dma_start(slot(home(u)), unit_source(0, u)).then_inc(s_w[home(u)], 16)

            sp.wait_ge(s["ds_diff"], NT * HEADS)
            sp.wait_ge(s["ds_av"], NT * HEADS)
            sp.dma_start(ffn_g, a["ffn_norm_g"][0].partition_broadcast(P)).then_inc(s["gain_in"], 16)
            early = [u for u in range(SLOTS) if home(u) in (4, 5, 6, 7, 11)]
            for i in range(NT + 1):
                if i == 1:
                    for u in early:
                        load_first(u)
                if i < NT:
                    if i >= 2:
                        sp.wait_ge(s["x2_out"], 16 * (i - 1))
                        sp.wait_ge(s["e_x2_sq"], i - 1)
                        sp.wait_ge(s["e_xn"], i - 1)
                    sp.dma_start(wk[:, i % 2, :], x_v[P * i:P * i + P, :]).then_inc(s_x[i % 2], 16)
                if i >= 1:
                    j = i - 1
                    sp.wait_ge(s["e_x2"], 2 * i)
                    sp.dma_start(acc_d[P * j:P * j + P, :], wk[:, j % 2, :]).then_inc(s["x2_out"], 16)
                    sp.wait_ge(s["e_xn"], i)
                    sp.dma_start(h_d[P * j:P * j + P, :], wk[:, 2 + j % 2, :]).then_inc(s[f"xn_out{j % 2}"], 16)
            sp.wait_ge(s["e_mix"], 2 * NT)
            sp.wait_ge(s["e_oT"], NT)
            for u in range(SLOTS):
                if u == GU_UNITS:
                    for b in range(BLOCKS):
                        sp.wait_ge(s_gather[b], 16)
                if u not in early:
                    load_first(u)
            sp.wait_ge(s["tab_made"], 1)
            with sp.Fori(0, MAX_ITEMS) as k:
                here = sp.value_load(table[2:3, bass.ds(k + 2, 1)], min_val=0, max_val=CAP + 1)
                with sp.If(here > 0):
                    e = sp.value_load(table[0:1, bass.ds(k + 2, 1)], min_val=0, max_val=EXPERTS - 1)
                    for u in range(SLOTS):
                        if u < GU_UNITS:
                            sp.wait_ge(s["gate_ready"] if u % 2 == 0 else s["up_ready"], k * 8 + (2 * (u // 2) + 2))
                        else:
                            sp.wait_ge(s["down_ready"], k * 8 + (2 * (u - GU_UNITS) + 2))
                        sp.dma_start(slot(home(u)), unit_source(e, u)).then_inc(s_w[home(u)], 16)
            sp.wait_ge(s["all_added"], 1)
            for t in range(NT):
                if t >= 4:
                    sp.wait_ge(s_fout[t % 4], 16 * (t // 4))
                sp.dma_start(wk[:, t % 4, :], acc_d[P * t:P * t + P, :]).then_inc(s_final[t % 4], 16)
                if t == 0:
                    sp.dma_start(wk[:, 5, :], a["final_norm_g"].partition_broadcast(P)).then_inc(s_gf, 16)
                if t >= 2:
                    sp.wait_ge(s_fdone, t - 1)
                    sp.dma_start(out[0, P * (t - 2):P * (t - 2) + P, :], wk[:, (t - 2) % 4, :]).then_inc(s_fout[(t - 2) % 4], 16)
            for t in range(NT - 2, NT):
                sp.wait_ge(s_fdone, t + 1)
                sp.dma_start(out[0, P * t:P * t + P, :], wk[:, t % 4, :]).then_inc(s_fout[t % 4], 16)
            for n in range(4):
                sp.wait_ge(s_fout[n], 16 * (NT // 4))

        @block.gpsimd
        def _(pool):
            pool.memset(ident[:, :], 0.0).then_inc(s["pool_chain"], 1)
            pool.wait_ge(s["pool_chain"], 1)
            pool.affine_select(out=ident[:, :], in_=ident[:, :], compare_op=ALU.not_equal, fill=1.0, base=0,
                               pattern=[[-1, P]], channel_multiplier=1).then_inc(s["ident_made"], 1)
            pool.memset(eps[:, :], EPS).then_inc(s["ident_made"], 1)
            pool.memset(blank[:, :, :], 0.0).then_inc(s["pool_chain"], 1)
            pool.memset(zeros, 0.0).then_inc(s["pool_chain"], 1)
            pool.wait_ge(s["pool_chain"], 3)
            pool.iota(blank.bitcast(i32)[:, :, 0], pattern=[[0, 2], [1, P]], base=S, channel_multiplier=0).then_inc(s["pool_chain"], 1)
            pool.wait_ge(s["pool_chain"], 4)
            pool.dma_start(list_d[0:LIST, :].rearrange("(p n) two -> p n two", p=P), blank).then_inc(s["lists_blank"], 16)
            pool.dma_start(list_d[LIST:LIST + LIST_PAD, :].rearrange("(a n) two -> a n two", a=1), blank[0:1, 0:P, :]).then_inc(s["lists_blank"], 16)
            z4 = zeros.unsqueeze(1).broadcast_to((P, 4, 256))
            pool.dma_start(h_d[S:ROWS, :].rearrange("p (a n) -> p a n", a=4), z4).then_inc(s["lists_blank"], 16)
            pool.dma_start(acc_d[S:ROWS, :].rearrange("p (a n) -> p a n", a=4), z4).then_inc(s["lists_blank"], 16)
            pool.memset(rev[:, :], 0.0).then_inc(s["pool_chain"], 1)
            pool.memset(ones_b[:, :], 1.0).then_inc(s["pool_chain"], 1)
            pool.memset(line_neg[:, :], NEG).then_inc(s["pool_chain"], 1)
            pool.iota(iota_ei[:, :], pattern=[[1, EXPERTS]], base=0, channel_multiplier=0).then_inc(s["pool_chain"], 1)
            pool.iota(iota_pi[:, :], pattern=[[0, 1]], base=-1, channel_multiplier=1).then_inc(s["pool_chain"], 1)
            pool.iota(pay.bitcast(i32)[:, :, :, 0], pattern=[[P, NT], [0, TOPK]], base=0, channel_multiplier=1).then_inc(s["pool_chain"], 1)
            pool.wait_ge(s["pool_chain"], 10)
            pool.affine_select(out=rev[:, :], in_=rev[:, :], compare_op=ALU.not_equal, fill=1.0, base=1 - P,
                               pattern=[[1, P]], channel_multiplier=1).then_inc(s["pool_chain"], 1)
            pool.affine_select(out=tri[:, :], in_=ones_b[:, :], compare_op=ALU.is_gt, fill=0.0, base=0,
                               pattern=[[1, P]], channel_multiplier=-1).then_inc(s["pool_chain"], 1)
            pool.tensor_copy(iota_e[:, :], iota_ei[:, :]).then_inc(s["pool_chain"], 1)
            pool.tensor_copy(iota_p[:, :], iota_pi[:, :]).then_inc(s["pool_chain"], 1)
            pool.wait_ge(s["pool_chain"], 14)
            pool.nop().then_inc(s["consts_made"], 1)
            for i in range(NT):
                pool.wait_ge(s["e_dest"], i + 1)
                if i == 0:
                    pool.wait_ge(s["lists_blank"], 64)
                for c in range(TOPK):
                    pool.indirect_dma_start(
                        list_d[:, :], bass.IndirectOffsetOnAxis(ap=dest_i[:, i, c:c + 1], axis=0),
                        pay[:, i, c, :], None).then_inc(s["listed"], 16)
            pool.wait_ge(s["listed"], 16 * NT * TOPK)
            pool.wait_ge(s["xn_out0"], 16 * NT // 2)
            pool.wait_ge(s["xn_out1"], 16 * NT // 2)
            pool.wait_ge(s["x2_out"], 16 * NT)

            def load_list(first):
                pool.dma_start(idx_next[:, :, :], list_d[first, :].rearrange("(b p) two -> p b two", p=P))\
                    .then_inc(s["idx_in"], 16)

            def gather(entry):
                size = pool.value_load(table[2:3, entry], min_val=0, max_val=CAP + 1)
                for b in range(BLOCKS):
                    with pool.If(size > P * b + 1):
                        pool.indirect_dma_start(
                            xg[:, b, :], None, h_d[:, :],
                            bass.IndirectOffsetOnAxis(ap=idx_next.bitcast(i32)[:, b, 0:1], axis=0)).then_inc(s_gather[b], 16)
                    with pool.Else():
                        pool.dma_start(nothing[0:1, 2 * b, :], ident[0:1, 0:16]).then_inc(s_gather[b], 16)

            for b in range(BLOCKS):
                pool.dma_start(nothing[0:1, 2 * b + 1, :], ident[0:1, 0:16]).then_inc(s_scatter[b], 16)
            load_list(slice(0, CAP))
            pool.wait_ge(s["idx_in"], 16)
            for b in range(BLOCKS):
                pool.indirect_dma_start(
                    xg[:, b, :], None, h_d[:, :],
                    bass.IndirectOffsetOnAxis(ap=idx_next.bitcast(i32)[:, b, 0:1], axis=0)).then_inc(s_gather[b], 16)
            pool.tensor_copy(idx_now[:, :, :], idx_next[:, :, :]).then_inc(s["idx_moved"], 1)
            pool.wait_ge(s["tab_made"], 1)
            with pool.Fori(0, MAX_ITEMS + 1) as it:
                size_last = pool.value_load(table[2:3, bass.ds(it, 1)], min_val=0, max_val=CAP + 1)
                size_now = pool.value_load(table[2:3, bass.ds(it + 1, 1)], min_val=0, max_val=CAP + 1)
                with pool.If(size_now > 0):
                    for b in range(BLOCKS):
                        pool.wait_ge(s_gather[b], it * 16 + 16)
                    pool.wait_ge(s["idx_moved"], it + 1)
                    first = pool.value_load(table[1:2, bass.ds(it + 2, 1)], min_val=0, max_val=LIST + LIST_PAD - CAP)
                    load_list(bass.ds(first, CAP))
                    for b in range(BLOCKS):
                        pool.wait_ge(s_xps[b], it * 2 + 2)
                    pool.wait_ge(s["idx_in"], it * 16 + 32)
                    gather(bass.ds(it + 2, 1))
                with pool.If(size_last > 0):
                    for b in range(BLOCKS):
                        with pool.If(size_last > P * b + 1):
                            pool.wait_ge(s_yact[b], it + 1)
                            pool.wait_ge(s_ydve[b], it + 1)
                            if b > 0:
                                pool.wait_ge(s_scatter[b - 1], it * 16 + 16)
                            pool.sem_inc(s["pool_waited"], 1)
                            pool.indirect_dma_start(
                                acc_d[:, :], bass.IndirectOffsetOnAxis(ap=idx_last.bitcast(i32)[:, b, 0:1], axis=0),
                                y_rows[:, b, :], None, compute_op=ALU.add).then_inc(s_scatter[b], 16)
                        with pool.Else():
                            pool.dma_start(nothing[0:1, 2 * b + 1, :], ident[0:1, 0:16]).then_inc(s_scatter[b], 16)
                    for b in range(BLOCKS):
                        pool.wait_ge(s_scatter[b], it * 16 + 16)
                    pool.sem_inc(s["pool_waited"], 1)
                with pool.If(size_now > 0):
                    pool.tensor_copy(idx_last[:, :, :], idx_now[:, :, :]).then_inc(s["pool_chain"], 1)
                    pool.wait_ge(s["pool_chain"], it + 15)
                    pool.sem_inc(s["pool_waited"], 1)
                    pool.tensor_copy(idx_now[:, :, :], idx_next[:, :, :]).then_inc(s["idx_moved"], 1)
            pool.sem_inc(s["all_added"], 1)

        @block.tensor
        def _(pe):
            def mm(o, l, r, first, last):
                return pe.matmul(o, l, r, start=first, stop=last)

            pe.wait_ge(s["ident_made"], 1)
            pe.wait_ge(s["vecs_in"], 48)
            pe.transpose(ps[:, 0, 0:22], vecs[:, :], ident[0:22, 0:22]).then_inc(s["vecT_ps"], 1)
            for t in range(10):
                pe.wait_ge(s["x_normed"], t + 1)
                if t == 0:
                    pe.wait_ge(s["vecT_made"], 1)
                if t in (4, 8):
                    pe.wait_ge(s["h_act"], t)
                    pe.wait_ge(s["h_dve"], t)
                for k in range(KD):
                    last = pe.transpose(ps[:, k, P * (t % 4):P * (t % 4) + P], x_tile(t)[:, P * k:P * k + P], ident[:, :])
                last.then_inc(s["x_turned"], 1)
            for g in range(NG):
                u, kind, x, half = groups[g]
                if kind == "line":
                    pe.wait_ge(s["mem_bias_in"], 48)
                    pe.wait_ge(s["small_in"], 80)
                if kind == "rev":
                    pe.wait_ge(s["shifted_in"], 16)
                    pe.wait_ge(s["consts_made"], 1)
                if u >= 0:
                    pe.wait_ge(s_w[u % PHASE1_SLOTS], 16 * (u // PHASE1_SLOTS + 1))
                if g == 0:
                    pe.wait_ge(s["h_act"], 12)
                    pe.wait_ge(s["h_dve"], 12)
                if g >= 8:
                    pe.wait_ge(s["proj_act"] if g % 2 == 0 else s["proj_dve"], g // 2 - 3)
                w = slot(u % PHASE1_SLOTS)
                bank = ps[:, g % 8, :]
                pair = bank.rearrange("p (a n) -> p a n", a=2)
                if kind == "t":
                    for k in range(KD):
                        last = mm(bank, w[:, k, P * x:P * x + P], hT[:, k, HALF * half:HALF * half + HALF], k == 0, k == KD - 1)
                elif kind == "v":
                    for n in range(2):
                        for k in range(KD):
                            last = mm(pair[:, n, :], hT[:, k, P * (x + n):P * (x + n) + P], w[:, k, :], k == 0, k == KD - 1)
                elif kind == "line":
                    last = mm(bank[0:HEADS, :], rel[:, :], one_hot[:, 512 * x:512 * x + 512], True, True)
                elif kind == "rev":
                    last = mm(bank, rev[:, :], shifted[:, x, HALF * half:HALF * half + HALF], True, True)
                elif kind in ("bgu", "bdn"):
                    rows = bgu_rows if kind == "bgu" else bdn_rows
                    for n in range(rows.shape[1]):
                        last = pe.transpose(bank[:, P * n:P * n + P], rows[:, n, :], ident[:, :])
                elif kind == "km":
                    for n in range(2):
                        for k in range(KD):
                            last = mm(pair[:, n, :], w[:, k, P * n:P * n + P], memT[:, k, :], k == 0, k == KD - 1)
                else:
                    for n in range(2):
                        for k in range(KD):
                            last = mm(pair[:, n, :], memT[:, k, P * n:P * n + P], w[:, k, :], k == 0, k == KD - 1)
                last.then_inc(s["proj_done"], 1)
            pe.wait_ge(s["proj_act"], NG // 2)
            pe.wait_ge(s["proj_dve"], NG // 2)
            for i in range(NT + 2):
                if i < NT:
                    if i >= 2:
                        pe.wait_ge(s["ms_exp"], 4 * (i - 1))
                    for h in range(HEADS):
                        q = 64 * (h % 2)
                        last = mm(ps[:, 2 * (i % 2) + h % 2, MEM * (h // 2):MEM * (h // 2) + MEM],
                                  qmT[q:q + QK, h // 2, P * i:P * i + P], kmT[q:q + QK, h // 2, :], True, True)
                    last.then_inc(s["ms_done"], 1)
                if 1 <= i <= NT:
                    j = i - 1
                    pe.wait_ge(s["ms_prob"], j + 1)
                    if j >= 1:
                        pe.wait_ge(s["ms_t_act"], j)
                        pe.wait_ge(s["ms_t_dve"], j)
                    for n in range(8):
                        last = pe.transpose(ps[:, 4 + n // 4, P * (n % 4):P * (n % 4) + P], wk[:, j % 2, P * n:P * n + P], ident[:, :])
                    last.then_inc(s["ms_turned"], 1)
                if i >= 2:
                    j = i - 2
                    pe.wait_ge(s["ms_t_act"], j + 1)
                    pe.wait_ge(s["ms_t_dve"], j + 1)
                    if j >= 2:
                        pe.wait_ge(s["ms_out"], j - 1)
                    for h in range(HEADS):
                        at = 2 * (h % 2) + h // 2
                        for m in range(2):
                            last = mm(ps[64 * (h % 2):64 * (h % 2) + 64, 6 + j % 2, P * (h // 2):P * (h // 2) + P],
                                      vm[:, m, QK * h:QK * h + QK],
                                      wk[:, 2 + j % 2, P * (2 * at + m):P * (2 * at + m) + P], m == 0, m == 1)
                    last.then_inc(s["ms_av"], 1)

            NU = NT * HEADS
            pe.wait_ge(s["ms_exp"], 4 * NT)
            pe.wait_ge(s["ms_t_act"], NT)
            pe.wait_ge(s["ms_t_dve"], NT)
            pe.wait_ge(s["ms_out"], NT)
            for j in range(NU + 2):
                if j < NU:
                    i, h = divmod(j, HEADS)
                    kv = P * (i + 1)
                    for c in range(2):
                        if j >= 1:
                            pe.wait_ge(s["ds_read"], 2 * j - 1 + c)
                        for n in range(0, kv, 512):
                            last = mm(ps[:, 2 * c + n // 512, 0:min(512, kv - n)], qT[QK * c:QK * c + QK, h, P * i:P * i + P],
                                      kT[QK * c:QK * c + QK, h, n:min(n + 512, kv)], True, True)
                        last.then_inc(s["ds_done"], 1)
                if j >= 2:
                    n = j - 2
                    i, h = divmod(n, HEADS)
                    pe.wait_ge(s["ds_t_act"], n + 1)
                    if n >= 2:
                        pe.wait_ge(s["ds_out"], n - 1)
                    for b in range(i + 1):
                        last = mm(ps[:, 6 + n % 2, 0:VD], wk[:, 4 + n % 2, P * b:P * b + P], v_rows[:, b, VD * h:VD * h + VD], b == 0, b == i)
                    last.then_inc(s["ds_av"], 1)
                if 1 <= j <= NU:
                    n = j - 1
                    pe.wait_ge(s["ds_diff"], n + 1)
                    if n >= 1:
                        pe.wait_ge(s["ds_t_act"], n)
                    for b in range(n // HEADS + 1):
                        last = pe.transpose(ps[:, 4 + b // 4, P * (b % 4):P * (b % 4) + P], wk[:, 2 * (n % 2), P * b:P * b + P], ident[:, :])
                    last.then_inc(s["ds_turned"], 1)

            pe.wait_ge(s["ds_out"], NU)
            for n in range(4):
                pe.wait_ge(s_w[n], 64)
            pe.wait_ge(s["consts_made"], 1)
            def turn_heads(i):
                pe.wait_ge(s["e_y"], i + 1)
                if i >= 4:
                    pe.wait_ge(s["e_rank_read"], i - 3)
                if i >= 1:
                    pe.wait_ge(s["e_oT_act"], i)
                for h in range(HEADS):
                    last = pe.transpose(ps[:, 4, P * h:P * h + P], o_all[:, i, P * h:P * h + P], ident[:, :])
                last.then_inc(s["e_oT"], 1)

            turn_heads(0)
            for i in range(NT + 2):
                if i < NT:
                    pe.wait_ge(s["e_oT_act"], i + 1)
                    if i >= 2:
                        pe.wait_ge(s["e_x2"], 2 * (i - 1))
                    for half in range(2):
                        for q in range(2):
                            w = slot(2 * half + q)
                            for k in range(KD):
                                l = (conv_b[:, k, P * i:P * i + P] if k < 2 else mixT[:, k, P * i:P * i + P])
                                last = mm(ps[:, 2 * (i % 2) + half, UW * q:UW * q + UW], l, w[:, k, :], k == 0, k == KD - 1)
                        last.then_inc(s["e_mix"], 1)
                if 1 <= i <= NT:
                    j = i - 1
                    pe.wait_ge(s["e_xn"], j + 1)
                    if j >= 1:
                        pe.wait_ge(s["e_hT_act"], j)
                        pe.wait_ge(s["e_hT_dve"], j)
                    for k in range(KD):
                        last = pe.transpose(ps[:, 5 + k // 4, P * (k % 4):P * (k % 4) + P], wk[:, 2 + j % 2, P * k:P * k + P], ident[:, :])
                    last.then_inc(s["e_hT"], 1)
                if i + 1 < NT:
                    turn_heads(i + 1)
                if 1 <= i <= NT:
                    j = i - 1
                    pe.wait_ge(s["e_hT_act"], j + 1)
                    pe.wait_ge(s["e_hT_dve"], j + 1)
                    if j >= 1:
                        pe.wait_ge(s["e_log_read"], j)
                    for k in range(KD):
                        last = mm(ps[:, 7, 0:EXPERTS], h2T[:, k, :], router_w[:, k, :], k == 0, k == KD - 1)
                    last.then_inc(s["e_log"], 1)
                if i >= 2:
                    j = i - 2
                    pe.wait_ge(s["e_chosen"], j + 1)
                    if j >= 1:
                        pe.wait_ge(s["e_rank_read"], j)
                    pe.wait_ge(s["e_oT_act"], min(i + 2, NT))
                    for b in range(j + 1):
                        last = mm(ps[:, 4, 0:EXPERTS], (tri if b == j else ones_b)[:, :], chosen_b[:, b, :], b == 0, b == j)
                    last.then_inc(s["e_rank"], 1)
            pe.wait_ge(s["e_rank_read"], NT)
            for b in range(NT):
                last = mm(ps[:, 4, 0:EXPERTS], ones_b[:, :], chosen_b[:, b, :], b == 0, b == NT - 1)
            last.then_inc(s["e_rank"], 1)
            pe.wait_ge(s["tab_f"], 1)
            pe.transpose(ps[0:4, 5, 0:64], table_f[:, :], ident[0:64, 0:64]).then_inc(s["tab_ps"], 1)
            pe.wait_ge(s["tab_made"], 1)

            def turn_x(b, done):
                pe.wait_ge(s_gather[b], done * 16 + 16)
                if b > 0:
                    pe.wait_ge(s_xact[b - 1], done + 1)
                    pe.wait_ge(s_xdve[b - 1], done + 1)
                for half in range(2):
                    for k in range(4):
                        last = pe.transpose(ps[:, 4 + half, P * k:P * k + P],
                                            xg[:, b, HALF * half + P * k:HALF * half + P * k + P], ident[:, :])
                    last.then_inc(s_xps[b], 1)

            def turn_y(b, it):
                if b > 0:
                    pe.wait_ge(s_yact[b - 1], it + 1)
                    pe.wait_ge(s_ydve[b - 1], it + 1)
                for half in range(2):
                    for m in range(4):
                        last = pe.transpose(ps[:, 6 + half, P * m:P * m + P], yT[:, 4 * half + m, P * b:P * b + P], ident[:, :])
                    last.then_inc(s_yps[b], 1)

            def turn_rows(it, size_last, size_next):
                for b in range(BLOCKS):
                    if size_next is not None:
                        with pe.If(size_next > P * b + 1):
                            turn_x(b, it + 1)
                        with pe.Else():
                            pe.sem_inc(s_xps[b], 2)
                    with pe.If(size_last > P * b + 1):
                        turn_y(b, it)
                    with pe.Else():
                        pe.sem_inc(s_yps[b], 2)

            def up_products(it, n):
                for b in range(-(-n // P)):
                    pe.wait_ge(s_xact[b], it + 1)
                    pe.wait_ge(s_xdve[b], it + 1)
                sizes = []
                for j in range(KD):
                    if j in (2, 4):
                        sizes.append(pe.value_load(table[2:3, bass.ds(it + j - 2, 1)], min_val=0, max_val=CAP + 1))
                    for bank, side, read, ready in ((j % 2, 0, "gate_read", "gate_ready"), (2 + j % 2, 1, "up_read", "up_ready")):
                        u = 2 * (j // 2) + side
                        if j % 2 == 0:
                            pe.wait_ge(s_w[home(u)], arrived(u, it))
                        if j < 2:
                            pe.wait_ge(s["yT_act"] if j == 0 else s["yT_dve"], it * 4 + 1 + side)
                        else:
                            pe.wait_ge(s[read], it * 8 + 1 + (j - 1))
                        for k in range(KD):
                            last = mm(ps[:, bank, 0:n], slot(home(u))[:, k, P * (j % 2):P * (j % 2) + P], xT[:, k, 0:n], k == 0, k == KD - 1)
                        last.then_inc(s[ready], 1)
                return sizes

            def down_products(it, n):
                for m in range(KD):
                    u = GU_UNITS + m // 2
                    if m % 2 == 0:
                        pe.wait_ge(s_w[home(u)], arrived(u, it))
                    if m >= 4:
                        pe.wait_ge(s["yT_act"] if m % 2 == 0 else s["yT_dve"], it * 4 + 2 + (m - 4) // 2 + 1)
                    if m == 1:
                        pe.wait_ge(s["up_read"], it * 8 + 9)
                    for k in range(KD):
                        if m == 0 and k in (0, 6, 7):
                            pe.wait_ge(s["act_ready"], it * 8 + 1 + (6 if k == 0 else k + 1))
                        last = mm(ps[:, m % 4, 0:n], slot(home(u))[:, k, P * (m % 2):P * (m % 2) + P], actT[:, k, 0:n], k == 0, k == KD - 1)
                    last.then_inc(s["down_ready"], 1)

            for b in range(BLOCKS):
                turn_x(b, 0)
            with pe.Fori(0, MAX_ITEMS + 1) as it:
                kind_now = pe.value_load(table[3:4, bass.ds(it + 1, 1)], min_val=0, max_val=len(SIZES) + 1)

                def item(n):
                    if n > 0:
                        size_last, size_next = up_products(it, n)
                        turn_rows(it, size_last, size_next)
                        down_products(it, n)
                    else:
                        size_last = pe.value_load(table[2:3, bass.ds(it, 1)], min_val=0, max_val=CAP + 1)
                        pe.wait_ge(s["yT_act"], it * 4 + 2)
                        pe.wait_ge(s["yT_dve"], it * 4 + 2)
                        turn_rows(it, size_last, None)

                with pe.If(kind_now > 0):
                    for_size(pe, kind_now, item)

        @block.scalar
        def _(act):
            act.wait_ge(s["ident_made"], 2)
            for t in range(10):
                act.wait_ge(s_x[t], 16)
                act.activation(wk[:, 4, :], x_tile(t), ACT.Square, accum_out=ssq[:, t:t + 1]).then_inc(s["act_chain"], 1)
                act.wait_ge(s["act_chain"], t + 1)
                act.activation(std[:, t:t + 1], ssq[:, t:t + 1], ACT.Sqrt, scale=1.0 / D, bias=eps[:, :]).then_inc(s["x_std"], 1)
                if t in (3, 7, 9):
                    act.wait_ge(s["x_turned"], t + 1)
                    if t == 3:
                        act.wait_ge(s["vecT_made"], 1)
                    for k in range(0, KD, 2):
                        gain = (mem_g if t == 9 else attn_g)[:, k:k + 1]
                        to = memT[:, k, :] if t == 9 else hT[:, k, HALF * (t // 4):HALF * (t // 4) + HALF]
                        act.activation(to, ps[:, k, 0:to.shape[1]], ACT.Identity, scale=gain).then_inc(s["h_act"], 1)
            for g in range(0, NG, 2):
                act.wait_ge(s["proj_done"], g + 1)
                if groups[g][1] == "line":
                    act.wait_ge(s["lists_blank"], 64)
                act.activation(group_dest(g), group_source(g), ACT.Copy).then_inc(s["proj_act"], 1)
            act.wait_ge(s["dve_chain"], 14)
            act.activation(lam[:, 2:4], lam[:, 0:2], ACT.Exp).then_inc(s["lam_exp"], 1)
            for i in range(NT + 1):
                if i < NT:
                    act.wait_ge(s["ms_done"], i + 1)
                    act.wait_ge(s["ms_max"], i + 1)
                    if i >= 2:
                        act.wait_ge(s["ms_turned"], i - 1)
                    for h in range(HEADS):
                        act.activation(wk[:, i % 2, MEM * h:MEM * h + MEM],
                                       ps[:, 2 * (i % 2) + h // 2, MEM * (h % 2):MEM * (h % 2) + MEM], ACT.Exp,
                                       scale=SCALE, bias=m_neg[:, i % 2, h:h + 1], accum_out=m_sum[:, i % 2, h:h + 1])\
                            .then_inc(s["ms_exp"], 1)
                if i >= 1:
                    j = i - 1
                    act.wait_ge(s["ms_turned"], j + 1)
                    if j >= 2:
                        act.wait_ge(s["ms_av"], j - 1)
                    act.activation(wk[:, 2 + j % 2, 0:512], ps[:, 4, :], ACT.Copy).then_inc(s["ms_t_act"], 1)

            NU = NT * HEADS
            act.wait_ge(s["ms_turned"], NT)
            act.wait_ge(s["ms_av"], NT)

            def exponentials(j, c):
                kv = P * (j // HEADS + 1)
                act.wait_ge(s["ds_read"], 2 * j + c + 1)
                src = wk[:, 2 * (j % 2) + c, 0:kv]
                act.activation(src, src, ACT.Exp, bias=d_neg[:, j % 2, c:c + 1], accum_out=d_sum[:, j % 2, c:c + 1])\
                    .then_inc(s["ds_exp"], 1)

            for j in range(NU + 2):
                if j < NU:
                    exponentials(j, 0)
                if j >= 2:
                    n = j - 2
                    i, h = divmod(n, HEADS)
                    act.wait_ge(s["ds_av"], n + 1)
                    act.activation(o_all[:, i, VD * h:VD * h + VD], ps[:, 6 + n % 2, 0:VD], ACT.Copy,
                                   scale=d_inv[:, n % 3, 0:1]).then_inc(s["ds_out"], 1)
                    act.wait_ge(s["ds_out"], n + 1)
                    act.activation(sq_junk[:, :], o_all[:, i, VD * h:VD * h + VD], ACT.Square,
                                   accum_out=o_ssq[:, n:n + 1]).then_inc(s["ds_sq"], 1)
                if 1 <= j <= NU:
                    n = j - 1
                    nb = n // HEADS + 1
                    act.wait_ge(s["ds_turned"], n + 1)
                    if n >= 2:
                        act.wait_ge(s["ds_av"], n - 1)
                    act.activation(wk[:, 4 + n % 2, 0:P * nb], ps[:, 4:6, :].rearrange("p b n -> p (b n)")[:, 0:P * nb], ACT.Copy)\
                        .then_inc(s["ds_t_act"], 1)
                if j < NU:
                    exponentials(j, 1)

            act.wait_ge(s["ds_sq"], NU)
            act.activation(o_std[:, :], o_ssq[:, :], ACT.Sqrt, scale=1.0 / VD, bias=eps[:, :]).then_inc(s["ds_sq"], 1)

            def heads_turned(i):
                act.wait_ge(s["e_oT"], i + 1)
                act.activation(mixT[:, 2:6, P * i:P * i + P], ps[:, 4, :].rearrange("p (h t) -> p h t", h=HEADS), ACT.Copy)\
                    .then_inc(s["e_oT_act"], 1)

            heads_turned(0)
            heads_turned(1)
            for i in range(1, NT + 1):
                j = i - 1
                act.wait_ge(s["e_x2"], 2 * j + 2)
                act.activation(wk[:, 4, :], wk[:, j % 2, :], ACT.Square, accum_out=e_ssq[:, j:j + 1]).then_inc(s["act_chain"], 1)
                act.wait_ge(s["act_chain"], 10 + j + 1)
                act.activation(e_std[:, j:j + 1], e_ssq[:, j:j + 1], ACT.Sqrt, scale=1.0 / D, bias=eps[:, :]).then_inc(s["e_x2_sq"], 1)
                act.wait_ge(s["e_hT"], j + 1)
                if j >= 1:
                    act.wait_ge(s["e_log"], j)
                act.activation(h2T[:, 0:4, :], ps[:, 5, :].rearrange("p (k t) -> p k t", t=P), ACT.Copy).then_inc(s["e_hT_act"], 1)
                if i + 1 < NT:
                    heads_turned(i + 1)
                act.wait_ge(s["e_chosen"], j + 1)
                act.activation(top_exp[:, :], top8[:, 0:TOPK], ACT.Exp, bias=top_neg[:, :], accum_out=top_sum[:, :]).then_inc(s["e_exp"], 1)

            act.preload_act_table(ACT.Sigmoid)
            act.wait_ge(s["tab_made"], 1)

            def read_x(b, done):
                act.wait_ge(s_xps[b], done * 2 + 1)
                act.activation(xT[:, 0:4, P * b:P * b + P], ps[:, 4, :].rearrange("p (k t) -> p k t", t=P), ACT.Copy)\
                    .then_inc(s_xact[b], 1)

            def read_y(b, it):
                act.wait_ge(s_yps[b], it * 2 + 1)
                act.wait_ge(s["idx_moved"], it + 1)
                act.wait_ge(s_scatter[b], it * 16)
                act.activation(y_rows[:, b, 0:512], ps[:, 6, :], ACT.Copy, scale=idx_last[:, b, 1:2]).then_inc(s_yact[b], 1)

            def read_rows(it, size_last, size_next):
                for b in range(BLOCKS):
                    if size_next is not None:
                        with act.If(size_next > P * b + 1):
                            read_x(b, it + 1)
                        with act.Else():
                            act.sem_inc(s_xact[b], 1)
                    with act.If(size_last > P * b + 1):
                        read_y(b, it)
                    with act.Else():
                        act.sem_inc(s_yact[b], 1)

            def gate_sigmoids(it, n):
                for j in range(KD):
                    act.wait_ge(s["gate_read"], it * 8 + 1 + (j + 1))
                    act.wait_ge(s["act_ready"], it * 8 + 1 + max(j - 1, 0))
                    act.activation(sig_b[:, j % 2, 0:n], gate_b[:, j % 2, 0:n], ACT.Sigmoid, scale=ALPHA).then_inc(s["sig_ready"], 1)

            def down_part(it, n):
                act.wait_ge(s["bias_now"], it * 2 + 2)
                for m in range(0, KD, 2):
                    act.wait_ge(s["down_ready"], it * 8 + (m + 1))
                    act.activation(yT[:, m, 0:n], ps[:, m % 4, 0:n], ACT.Identity, bias=b_now[:, 16 + m:17 + m]).then_inc(s["yT_act"], 1)

            for b in range(BLOCKS):
                read_x(b, 0)
            act.sem_inc(s["sig_ready"], 1)
            act.sem_inc(s["yT_act"], 2)
            with act.Fori(0, MAX_ITEMS + 1) as it:
                kind_now = act.value_load(table[3:4, bass.ds(it + 1, 1)], min_val=0, max_val=len(SIZES) + 1)
                with act.If(kind_now > 0):
                    size_last = act.value_load(table[2:3, bass.ds(it, 1)], min_val=0, max_val=CAP + 1)
                    size_next = act.value_load(table[2:3, bass.ds(it + 2, 1)], min_val=0, max_val=CAP + 1)

                    def item(n):
                        if n > 0:
                            gate_sigmoids(it, n)
                            read_rows(it, size_last, size_next)
                            down_part(it, n)
                        else:
                            read_rows(it, size_last, None)

                    for_size(act, kind_now, item)
            for t in range(NT):
                act.wait_ge(s_final[t % 4], 16 * (t // 4 + 1))
                act.activation(wk[:, 4, :], wk[:, t % 4, :], ACT.Square, accum_out=e_ssq[:, t:t + 1]).then_inc(s["act_chain"], 1)
                act.wait_ge(s["act_chain"], 18 + t + 1)
                act.activation(e_std[:, t:t + 1], e_ssq[:, t:t + 1], ACT.Sqrt, scale=1.0 / D, bias=eps[:, :]).then_inc(s_fsq, 1)

        @block.vector
        def _(dve):
            chain = [0]

            def link(ins):
                chain[0] += 1
                ins.then_inc(s["dve_chain"], 1)
                dve.wait_ge(s["dve_chain"], chain[0])

            dve.wait_ge(s["vecT_ps"], 1)
            dve.tensor_copy(vecT[:, :], ps[:, 0, 0:22]).then_inc(s["vecT_made"], 1)
            dve.wait_ge(s["vecT_made"], 1)
            for t in range(10):
                dve.wait_ge(s["x_std"], t + 1)
                link(dve.reciprocal(rstd[:, t:t + 1], std[:, t:t + 1]))
                dve.tensor_scalar(x_tile(t), x_tile(t), rstd[:, t:t + 1], None, ALU.mult).then_inc(s["x_normed"], 1)
                if t in (3, 7, 9):
                    dve.wait_ge(s["x_turned"], t + 1)
                    for k in range(1, KD, 2):
                        gain = (mem_g if t == 9 else attn_g)[:, k:k + 1]
                        to = memT[:, k, :] if t == 9 else hT[:, k, HALF * (t // 4):HALF * (t // 4) + HALF]
                        dve.tensor_scalar(to, ps[:, k, 0:to.shape[1]], gain, None, ALU.mult).then_inc(s["h_dve"], 1)
            dve.wait_ge(s["small_in"], 80)
            lv = lam_in.rearrange("p (a d) -> p a d", a=4)
            link(dve.tensor_tensor(lv[:, 0, :], lv[:, 0, :], lv[:, 1, :], ALU.mult))
            link(dve.tensor_tensor(lv[:, 2, :], lv[:, 2, :], lv[:, 3, :], ALU.mult))
            link(dve.reduce_sum(lam[:, 0:1], lv[:, 0, :], axis=AX.X))
            link(dve.reduce_sum(lam[:, 1:2], lv[:, 2, :], axis=AX.X))
            link(dve.tensor_scalar(sub_g[:, :], sub_g[:, :], 1.0 - LAM_INIT, None, ALU.mult))
            lam_dots = chain[0]
            for g in range(1, NG, 2):
                dve.wait_ge(s["proj_done"], g + 1)
                if groups[g][1] == "line":
                    dve.wait_ge(s["lists_blank"], 64)
                dve.tensor_copy(group_dest(g), group_source(g)).then_inc(s["proj_dve"], 1)
                if g == conv_ready + 2:
                    dve.wait_ge(s["proj_act"], 6)
                    dve.wait_ge(s["proj_dve"], 6)
                    for c in range(2):
                        link(dve.tensor_tensor(conv_u[:, c, :], conv_u[:, c, :], conv_c[:, c, :], ALU.mult))
                        link(dve.tensor_scalar(conv_c[:, c, :], conv_u[:, c, :], taps[:, 4 + c:5 + c], None, ALU.mult))
                        for tap in range(2):
                            late = 2 - tap
                            link(dve.scalar_tensor_tensor(out=conv_c[:, c, late:S], in0=conv_u[:, c, 0:S - late],
                                                          scalar=taps[:, 2 * tap + c:2 * tap + c + 1],
                                                          in1=conv_c[:, c, late:S], op0=ALU.mult, op1=ALU.add))
                        link(dve.tensor_tensor(conv_b[:, c, :], conv_b[:, c, :], conv_c[:, c, :], ALU.mult))
            dve.wait_ge(s["proj_act"], NG // 2)
            link(dve.tensor_scalar(bguT[:, :, 8:16], bguT[:, :, 8:16], 1.0, None, ALU.add))

            for i in range(NT + 2):
                if i < NT:
                    dve.wait_ge(s["ms_done"], i + 1)
                    link(dve.tensor_reduce(m_max[:, i % 2, :], ps[:, 2 * (i % 2):2 * (i % 2) + 2, :].rearrange("p b (a n) -> p (b a) n", a=2),
                                           axis=AX.X, op=ALU.max))
                    if i >= 2:
                        dve.wait_ge(s["ms_exp"], 4 * (i - 1))
                    dve.tensor_scalar(m_neg[:, i % 2, :], m_max[:, i % 2, :], -SCALE, None, ALU.mult).then_inc(s["ms_max"], 1)
                    dve.wait_ge(s["ms_exp"], 4 * (i + 1))
                    link(dve.reciprocal(m_inv[:, i % 2, :], m_sum[:, i % 2, :]))
                    pv = wk[:, i % 2, :].rearrange("p (h n) -> p h n", h=HEADS)
                    dve.tensor_tensor(pv, pv, m_inv[:, i % 2, :].unsqueeze(2).broadcast_to((P, HEADS, MEM)), ALU.mult).then_inc(s["ms_prob"], 1)
                if 1 <= i <= NT:
                    j = i - 1
                    dve.wait_ge(s["ms_turned"], j + 1)
                    if j >= 2:
                        dve.wait_ge(s["ms_av"], j - 1)
                    dve.tensor_copy(wk[:, 2 + j % 2, 512:1024], ps[:, 5, :]).then_inc(s["ms_t_dve"], 1)
                if i >= 2:
                    j = i - 2
                    dve.wait_ge(s["ms_av"], j + 1)
                    dve.tensor_copy(mixT[:, 6:8, P * j:P * j + P], ps[:, 6 + j % 2, 0:256].rearrange("p (c t) -> p c t", c=2)).then_inc(s["ms_out"], 1)

            dve.wait_ge(s["lam_exp"], 1)
            link(dve.tensor_tensor(lam[:, 4:5], lam[:, 3:4], lam[:, 2:3], ALU.subtract))
            link(dve.tensor_scalar(lam[:, 5:6], lam[:, 4:5], -LAM_INIT, None, ALU.add))
            NU = NT * HEADS
            dve.wait_ge(s["ms_av"], NT)
            def scores_read(j, c):
                i, h = divmod(j, HEADS)
                kv = P * (i + 1)
                dve.wait_ge(s["ds_done"], 2 * j + c + 1)
                if j >= 2:
                    dve.wait_ge(s["ds_turned"], j - 1)
                sc = wk[:, 2 * (j % 2) + c, 0:kv]
                raw = ps[:, 2 * c:2 * c + 2, :].rearrange("p b n -> p (b n)")[:, 0:kv]
                link(dve.scalar_tensor_tensor(out=sc, in0=raw, scalar=SCALE, in1=master[:, h, S - kv:S], op0=ALU.mult, op1=ALU.add))
                dve.tensor_reduce(d_neg[:, j % 2, c:c + 1], sc, axis=AX.X, op=ALU.max, negate=True).then_inc(s["ds_read"], 1)

            def difference(n):
                kv = P * (n // HEADS + 1)
                dve.wait_ge(s["ds_exp"], 2 * n + 2)
                if n >= 3:
                    dve.wait_ge(s["ds_out"], n - 2)
                link(dve.reciprocal(d_inv[:, n % 3, :], d_sum[:, n % 2, :]))
                link(dve.scalar_tensor_tensor(out=d_lam[:, n % 2:n % 2 + 1], in0=d_sum[:, n % 2, 0:1], scalar=lam[:, 5:6],
                                              in1=d_inv[:, n % 3, 1:2], op0=ALU.mult, op1=ALU.mult))
                p0, p1 = wk[:, 2 * (n % 2), 0:kv], wk[:, 2 * (n % 2) + 1, 0:kv]
                dve.scalar_tensor_tensor(out=p0, in0=p1, scalar=d_lam[:, n % 2:n % 2 + 1], in1=p0, op0=ALU.mult, op1=ALU.add)\
                    .then_inc(s["ds_diff"], 1)

            for j in range(NU + 1):
                if j < NU:
                    scores_read(j, 0)
                if j >= 1:
                    difference(j - 1)
                if j < NU:
                    scores_read(j, 1)

            dve.wait_ge(s["ds_sq"], NU + 1)
            link(dve.reciprocal(o_rs[:, :], o_std[:, :]))

            def norm_heads(i):
                ov = o_all[:, i, :].rearrange("p (h n) -> p h n", h=HEADS)
                link(dve.tensor_tensor(ov, ov, o_rs[:, HEADS * i:HEADS * i + HEADS].unsqueeze(2).broadcast_to((P, HEADS, VD)), ALU.mult))
                dve.tensor_tensor(ov, ov, sub_g[:, :].unsqueeze(1).broadcast_to((P, HEADS, VD)), ALU.mult).then_inc(s["e_y"], 1)

            def ranks_read(j):
                dve.wait_ge(s["e_rank"], j + 1)
                dve.tensor_copy(place[:, :], ps[:, 4, 0:EXPERTS]).then_inc(s["e_rank_read"], 1)
                dve.wait_ge(s["e_rank_read"], j + 1)

            norm_heads(0)
            norm_heads(1)
            dve.wait_ge(s["consts_made"], 1)
            for i in range(NT + 2):
                if i < NT:
                    if i + 2 < NT:
                        norm_heads(i + 2)
                    dve.wait_ge(s_x[i % 2], 16 * (1 + i // 2 + 1))
                    for half in range(2):
                        dve.wait_ge(s["e_mix"], 2 * i + half + 1)
                        x_half = wk[:, i % 2, HALF * half:HALF * half + HALF]
                        dve.tensor_tensor(x_half, ps[:, 2 * (i % 2) + half, :], x_half, ALU.add).then_inc(s["e_x2"], 1)
                    dve.wait_ge(s["e_x2_sq"], i + 1)
                    link(dve.reciprocal(e_rstd[:, i:i + 1], e_std[:, i:i + 1]))
                    if i >= 2:
                        dve.wait_ge(s[f"xn_out{i % 2}"], 16 * (i // 2))
                        dve.wait_ge(s["e_hT"], i - 1)
                    dve.wait_ge(s["e_x2"], 2 * i + 2)
                    if i == 0:
                        dve.wait_ge(s["gain_in"], 16)
                    dve.scalar_tensor_tensor(out=wk[:, 2 + i % 2, :], in0=wk[:, i % 2, :], scalar=e_rstd[:, i:i + 1], in1=ffn_g,
                                             op0=ALU.mult, op1=ALU.mult).then_inc(s["e_xn"], 1)
                    j = i
                    dve.wait_ge(s["e_hT"], j + 1)
                    if j >= 1:
                        dve.wait_ge(s["e_log"], j)
                    dve.tensor_copy(h2T[:, 4:8, :], ps[:, 6, :].rearrange("p (k t) -> p k t", t=P)).then_inc(s["e_hT_dve"], 1)
                    dve.wait_ge(s["e_log"], j + 1)
                    dve.tensor_tensor(logits[:, :], ps[:, 7, 0:EXPERTS], router_b[:, :], ALU.add).then_inc(s["e_log_read"], 1)
                    dve.wait_ge(s["e_log_read"], j + 1)
                    link(dve.max(top8[:, :], logits[:, :]))
                    link(dve.tensor_scalar(top_neg[:, :], top8[:, 0:1], -1.0, None, ALU.mult))
                    link(dve.max_index(top8i[:, :], top8[:, :], logits[:, :]))
                    link(dve.tensor_copy(top_e[:, j, :], top8i[:, 0:TOPK]))
                    link(dve.tensor_scalar(chosen[:, :], iota_e[:, :], top_e[:, j, 0:1], None, ALU.is_equal))
                    for c in range(1, TOPK):
                        to = chosen_b[:, j, :] if c == TOPK - 1 else chosen[:, :]
                        ins = dve.scalar_tensor_tensor(out=to, in0=iota_e[:, :], scalar=top_e[:, j, c:c + 1], in1=chosen[:, :],
                                                       op0=ALU.is_equal, op1=ALU.add)
                        if c < TOPK - 1:
                            link(ins)
                        else:
                            ins.then_inc(s["e_chosen"], 1)
                    dve.wait_ge(s["e_exp"], j + 1)
                    link(dve.reciprocal(top_inv[:, :], top_sum[:, :]))
                    link(dve.tensor_scalar(pay[:, j, :, 1], top_exp[:, :], top_inv[:, :], None, ALU.mult))
                if 1 <= i <= NT:
                    j = i - 1
                    ranks_read(j)
                    link(dve.scalar_tensor_tensor(out=place[:, :], in0=iota_e[:, :], scalar=float(S), in1=place[:, :], op0=ALU.mult, op1=ALU.add))
                    for c in range(TOPK):
                        ins = dve.scalar_tensor_tensor(out=dest_j[:, c, :], in0=iota_e[:, :], scalar=top_e[:, j, c:c + 1], in1=place[:, :],
                                                       op0=ALU.is_equal, op1=ALU.mult)
                    link(ins)
                    link(dve.reduce_sum(dest_f[:, j, :], dest_j[:, :, :], axis=AX.X))
                    dve.tensor_copy(dest_i[:, j, :], dest_f[:, j, :]).then_inc(s["e_dest"], 1)

            ranks_read(NT)
            cnt, nch, end, start, tmp, oh = (t32[:, n, :] for n in range(6))
            e0 = place[0:64, :]
            jj = iota_p[0:64, :]
            link(dve.tensor_copy(cnt, e0))
            link(dve.tensor_scalar(nch, cnt, float(CAP), 1.0, ALU.is_gt, ALU.add))
            link(dve.scalar_tensor_tensor(out=nch, in0=cnt, scalar=float(2 * CAP), in1=nch, op0=ALU.is_gt, op1=ALU.add))
            link(dve.memset(tmp, 1.0))
            link(dve.tensor_tensor_scan(end, tmp, nch, 0.0, ALU.mult, ALU.add))
            link(dve.tensor_tensor(start, end, nch, ALU.subtract))
            link(dve.tensor_scalar(tmp, end, jj, None, ALU.is_le))
            link(dve.reduce_sum(t1[:, 0:1], tmp, axis=AX.X))
            link(dve.scalar_tensor_tensor(out=tmp, in0=start, scalar=jj, in1=start, op0=ALU.is_le, op1=ALU.mult))
            link(dve.tensor_reduce(t1[:, 1:2], tmp, axis=AX.X, op=ALU.max))
            link(dve.scalar_tensor_tensor(out=oh, in0=iota_e[0:64, :], scalar=t1[:, 0:1], in1=cnt, op0=ALU.is_equal, op1=ALU.mult))
            link(dve.reduce_sum(t1[:, 2:3], oh, axis=AX.X))
            link(dve.tensor_tensor(t1[:, 3:4], jj, t1[:, 1:2], ALU.subtract))
            link(dve.scalar_tensor_tensor(out=t1[:, 4:5], in0=t1[:, 3:4], scalar=-float(CAP), in1=t1[:, 2:3], op0=ALU.mult, op1=ALU.add))
            link(dve.tensor_scalar(t1[:, 4:5], t1[:, 4:5], float(CAP), None, ALU.min))
            link(dve.tensor_scalar(t1[:, 5:6], t1[:, 0:1], float(EXPERTS), None, ALU.is_lt))
            link(dve.scalar_tensor_tensor(out=t1[:, 5:6], in0=jj, scalar=0.0, in1=t1[:, 5:6], op0=ALU.is_ge, op1=ALU.mult))
            link(dve.tensor_tensor(table_f[:, 0:1], t1[:, 0:1], t1[:, 5:6], ALU.mult))
            link(dve.tensor_scalar(t1[:, 6:7], t1[:, 3:4], float(CAP), None, ALU.mult))
            link(dve.scalar_tensor_tensor(out=t1[:, 6:7], in0=t1[:, 0:1], scalar=float(S), in1=t1[:, 6:7], op0=ALU.mult, op1=ALU.add))
            link(dve.tensor_tensor(table_f[:, 1:2], t1[:, 6:7], t1[:, 5:6], ALU.mult))
            link(dve.scalar_tensor_tensor(out=table_f[:, 2:3], in0=t1[:, 4:5], scalar=1.0, in1=t1[:, 5:6], op0=ALU.add, op1=ALU.mult))
            link(dve.tensor_scalar(t1[:, 7:8], t1[:, 4:5], float(SIZES[0]), 1.0, ALU.is_gt, ALU.add))
            for n in SIZES[1:-1]:
                link(dve.scalar_tensor_tensor(out=t1[:, 7:8], in0=t1[:, 4:5], scalar=float(n), in1=t1[:, 7:8], op0=ALU.is_gt, op1=ALU.add))
            link(dve.tensor_tensor(t1[:, 8:9], t1[:, 7:8], t1[:, 5:6], ALU.mult))
            link(dve.tensor_scalar(t1[:, 9:10], end[:, EXPERTS - 1:EXPERTS], jj, float(len(SIZES) + 1), ALU.is_equal, ALU.mult))
            dve.tensor_tensor(table_f[:, 3:4], t1[:, 8:9], t1[:, 9:10], ALU.add).then_inc(s["tab_f"], 1)
            dve.wait_ge(s["tab_ps"], 1)
            dve.tensor_copy(table[:, :], ps[0:4, 5, 0:64]).then_inc(s["tab_made"], 1)
            dve.wait_ge(s["tab_made"], 1)

            def read_x(b, done):
                dve.wait_ge(s_xps[b], done * 2 + 2)
                dve.tensor_copy(xT[:, 4:8, P * b:P * b + P], ps[:, 5, :].rearrange("p (k t) -> p k t", t=P)).then_inc(s_xdve[b], 1)

            def read_y(b, it):
                dve.wait_ge(s_yps[b], it * 2 + 2)
                dve.wait_ge(s["idx_moved"], it + 1)
                dve.wait_ge(s_scatter[b], it * 16)
                dve.tensor_scalar(y_rows[:, b, 512:1024], ps[:, 7, :], idx_last[:, b, 1:2], None, ALU.mult).then_inc(s_ydve[b], 1)

            def read_rows(it, size_last, size_next):
                for b in range(BLOCKS):
                    if size_next is not None:
                        with dve.If(size_next > P * b + 1):
                            read_x(b, it + 1)
                        with dve.Else():
                            dve.sem_inc(s_xdve[b], 1)
                    with dve.If(size_last > P * b + 1):
                        read_y(b, it)
                    with dve.Else():
                        dve.sem_inc(s_ydve[b], 1)

            def activations(it, n):
                dve.wait_ge(s["bias_now"], it * 2 + 2)
                for j in range(KD + 1):
                    if j < KD:
                        g, u = gate_b[:, j % 2, 0:n], up_b[:, j % 2, 0:n]
                        dve.wait_ge(s["gate_ready"], it * 8 + (j + 1))
                        dve.wait_ge(s["sig_ready"], it * 8 + 1 + max(j - 1, 0))
                        dve.wait_ge(s["act_ready"], it * 8 + 1 + max(j - 1, 0))
                        dve.tensor_scalar(g, ps[:, j % 2, 0:n], b_now[:, j:j + 1], LIMIT, ALU.add, ALU.min).then_inc(s["gate_read"], 1)
                        dve.wait_ge(s["up_ready"], it * 8 + (j + 1))
                        dve.tensor_scalar(u, ps[:, 2 + j % 2, 0:n], b_now[:, 8 + j:9 + j], LIMIT + 1.0, ALU.add, ALU.min).then_inc(s["up_read"], 1)
                    if j >= 1:
                        m = j - 1
                        g, u, sg = gate_b[:, m % 2, 0:n], up_b[:, m % 2, 0:n], sig_b[:, m % 2, 0:n]
                        dve.wait_ge(s["sig_ready"], it * 8 + 1 + j)
                        dve.wait_ge(s["up_read"], it * 8 + 1 + j)
                        dve.tensor_tensor(sg, g, sg, ALU.mult).then_inc(s["silu"], 1)
                        dve.wait_ge(s["silu"], it * 8 + j)
                        dve.scalar_tensor_tensor(out=actT[:, m, 0:n], in0=u, scalar=1.0 - LIMIT, in1=sg, op0=ALU.max, op1=ALU.mult)\
                            .then_inc(s["act_ready"], 1)

            def down_part(it, n):
                for m in range(1, KD, 2):
                    dve.wait_ge(s["down_ready"], it * 8 + (m + 1))
                    dve.tensor_scalar(yT[:, m, 0:n], ps[:, m % 4, 0:n], b_now[:, 16 + m:17 + m], None, ALU.add).then_inc(s["yT_dve"], 1)

            for b in range(BLOCKS):
                read_x(b, 0)
            for name in ("gate_read", "up_read", "act_ready"):
                dve.sem_inc(s[name], 1)
            dve.sem_inc(s["yT_dve"], 2)
            with dve.Fori(0, MAX_ITEMS + 1) as it:
                kind_now = dve.value_load(table[3:4, bass.ds(it + 1, 1)], min_val=0, max_val=len(SIZES) + 1)
                with dve.If(kind_now > 0):
                    e = dve.value_load(table[0:1, bass.ds(it + 1, 1)], min_val=0, max_val=EXPERTS - 1)
                    size_last = dve.value_load(table[2:3, bass.ds(it, 1)], min_val=0, max_val=CAP + 1)
                    size_next = dve.value_load(table[2:3, bass.ds(it + 2, 1)], min_val=0, max_val=CAP + 1)
                    dve.wait_ge(s["yT_act"], it * 4 + 2)
                    dve.wait_ge(s["yT_dve"], it * 4 + 2)
                    dve.tensor_copy(b_now[:, 0:16], bguT[:, bass.ds(e, 1), :].rearrange("p e m -> p (e m)")).then_inc(s["bias_now"], 1)
                    dve.tensor_copy(b_now[:, 16:24], bdnT[:, bass.ds(e, 1), :].rearrange("p e m -> p (e m)")).then_inc(s["bias_now"], 1)

                    def item(n):
                        if n > 0:
                            activations(it, n)
                            read_rows(it, size_last, size_next)
                            down_part(it, n)
                        else:
                            read_rows(it, size_last, None)

                    for_size(dve, kind_now, item)
            dve.wait_ge(s_gf, 16)
            for t in range(NT):
                dve.wait_ge(s_fsq, t + 1)
                link(dve.reciprocal(e_rstd[:, t:t + 1], e_std[:, t:t + 1]))
                dve.scalar_tensor_tensor(out=wk[:, t % 4, :], in0=wk[:, t % 4, :], scalar=e_rstd[:, t:t + 1], in1=wk[:, 5, :],
                                         op0=ALU.mult, op1=ALU.mult).then_inc(s_fdone, 1)


_INS = ["x", "mem", "rel_bias", "attn_norm_g", "w_mix_in", "conv_w", "lambda_qk", "diff_subln_g", "mem_norm_g",
        "w_mem_kv", "w_mix_out", "ffn_norm_g", "router_w", "router_b", "w_gate_up", "b_gate_up", "w_down", "b_down",
        "final_norm_g"]


def kernel(**inputs):
    import concourse.bacc as _bacc
    from concourse.bass_utils import run_bass_kernel_spmd as _run

    nc = _bacc.Bacc("TRN2", target_bir_lowering=False, num_devices=1)
    arrays, aps = {}, {}
    for name in _INS:
        arrays[f"in_{name}"] = np.ascontiguousarray(inputs[name])
    arrays["in_distance_one_hot"] = distance_one_hot()
    for key, value in arrays.items():
        aps[key[3:]] = nc.dram_tensor(key, value.shape, mybir.dt.from_np(value.dtype), kind="ExternalInput").ap()
    out = nc.dram_tensor("out_rows", (1, S, D), f32, kind="ExternalOutput").ap()
    hymba_kernel(nc, aps, out)
    r = _run(nc, [arrays], core_ids=[0])
    return r.results[0]["out_rows"]
```

```python
import math
from contextlib import ExitStack

import numpy as np
import concourse.bass as bass
from concourse import mybir

f32 = mybir.dt.float32
f32r = mybir.dt.float32r
bf16 = mybir.dt.bfloat16
i32 = mybir.dt.int32
u32 = mybir.dt.uint32
ALU = mybir.AluOpType
ACT = mybir.ActivationFunctionType
AX = mybir.AxisListType

P = 128
D = 1024
S = 1024
KD = D // P
NT = S // P
HALF = 512
MEM = 256
HEADS = 4
QK = 64
VD = 128
UW = 256
EXPERTS = 32
TOPK = 4
BUCKETS = 32
MAX_DISTANCE = 128
EPS = 1e-5
NEG = -1e30
LAM_INIT = 0.8 - 0.6 * math.exp(-0.3 * 0)
ALPHA = 1.702
LIMIT = 7.0
SCALE = QK ** -0.5

SLOTS = 12
PHASE1_SLOTS = 4
GU_UNITS = 8
CAP = 384
BLOCKS = CAP // P
MAX_ITEMS = EXPERTS + S * TOPK // CAP
SIZES = [128, 144, 160, 176, 192, 224, 256, 288, 320, 352, 384]
LIST = EXPERTS * S
LIST_PAD = P
ROWS = S + P

LINE = S + P


def distance_one_hot():
    n = np.arange(S - 1, -1, -1, dtype=np.int32)
    exact = BUCKETS // 2
    nf = np.maximum(n, 1).astype(np.float32)
    large = exact + (np.log(nf / np.float32(exact)) / np.float32(math.log(MAX_DISTANCE / exact))
                     * np.float32(BUCKETS - exact)).astype(np.int32)
    bucket = np.where(n < exact, n, np.minimum(large, BUCKETS - 1))
    return (np.arange(BUCKETS)[:, None] == bucket[None, :]).astype(np.float32)


def hymba_kernel(nc, a, out):
    ctx = ExitStack()
    with ctx:
        def sb(name, shape, dt=f32):
            return ctx.enter_context(nc.sbuf_tensor(name, shape, dt))

        def sem(name):
            return ctx.enter_context(nc.semaphore(name))

        line_d = nc.dram_tensor("bias_line", (HEADS, LINE), f32, kind="Internal").ap()
        h_d = nc.dram_tensor("normed_rows", (ROWS, D), f32, kind="Internal").ap()
        acc_d = nc.dram_tensor("residual_rows", (ROWS, D), f32, kind="Internal").ap()
        list_d = nc.dram_tensor("expert_lists", (LIST + LIST_PAD, 2), f32, kind="Internal").ap()

        with ExitStack() as early_ctx:
            def early_sb(name, shape):
                return early_ctx.enter_context(nc.sbuf_tensor(name, shape, f32r))

            w_lo_r = early_sb("w_lo", [P, PHASE1_SLOTS, KD * UW])
            early_sb("slots_between", [P, SLOTS - PHASE1_SLOTS - 1, KD * UW])
            last_slot = early_sb("last_slot", [P, KD * UW])
            hT_hi = early_sb("hT_hi", [P, KD, S])
            hT_lo_r = early_sb("hT_lo", [P, KD, S])
            mem_r = early_sb("mem_there", [P, 3072])
            w_hi_r = early_sb("w_hi", [P, 2, KD * UW])

        ring = sb("weight_ring", [P, SLOTS, KD * UW])
        mixT = sb("mixT_hT", [P, KD, S])
        r_v = sb("region_v", [P, 4096])
        r_bias = sb("region_bias", [P, 4096])
        r_mem = sb("region_mem", [P, 3072])
        work = sb("work", [P, 6144])

        def slot(s):
            return ring[:, s, :].rearrange("p (k c) -> p k c", k=KD)

        def home(u):
            return (u + PHASE1_SLOTS) % SLOTS

        def arrived(u, it):
            before = 4 if home(u) < PHASE1_SLOTS else 0
            return it * 16 + 16 * (before + 1)

        def x_tile(t):
            return ring[:, (4 + t // 2 if t < NT else 9), D * (t % 2):D * (t % 2) + D]

        def hT_lo(k):
            return hT_lo_r[:, k, :]

        def w_hi(u):
            return w_hi_r[:, u % 2, :]

        def w_lo(u):
            return w_lo_r[:, u % PHASE1_SLOTS, :]

        def w_out_hi(q):
            return (hT_hi[:, 0:2, :].rearrange("p k t -> p (k t)"), hT_hi[:, 2:4, :].rearrange("p k t -> p (k t)"),
                    last_slot[:, :], mem_r[:, S:3 * S])[q]

        def mix_parts(i):
            place = (hT_hi[:, 4:6, :] if i % 2 == 0 else hT_lo_r[:, 6:8, :]).rearrange("p k t -> p (k t)")
            return (place[:, 0:D].rearrange("p (k t) -> p k t", k=KD), place[:, D:2 * D].rearrange("p (k t) -> p k t", k=KD))

        qT = ring[:, 4:6, :].rearrange("p s n -> p (s n)").rearrange("p (h t) -> p h t", t=S)
        kT = ring[:, 6:8, :].rearrange("p s n -> p (s n)").rearrange("p (h t) -> p h t", t=S)
        conv_u = ring[:, 8, :].rearrange("p (c t) -> p c t", t=S)
        conv_c = ring[:, 9, :].rearrange("p (c t) -> p c t", t=S)
        conv_b = ring[:, 10, :].rearrange("p (c t) -> p c t", t=S)
        memT = ring[:, 11, :].rearrange("p (k t) -> p k t", t=MEM)
        o_all = r_v[:, :].rearrange("p (i n) -> p i n", i=NT)
        v_rows = ring[:, 8:10, :].rearrange("p s n -> p (s n)").rearrange("p (t n) -> p t n", t=NT)
        master = r_bias[:, :].rearrange("p (h y) -> p h y", h=HEADS)
        qmT = r_mem[:, 0:2048].rearrange("p (c t) -> p c t", t=S)
        kmT = r_mem[:, 2048:2560].rearrange("p (c t) -> p c t", t=MEM)
        vm = r_mem[:, 2560:3072].rearrange("p (m n) -> p m n", m=2)
        wk = work[:, :].rearrange("p (s n) -> p s n", n=1024)
        xg = r_v[:, 0:BLOCKS * D].rearrange("p (b n) -> p b n", b=BLOCKS)
        xT = r_bias[:, 0:KD * CAP].rearrange("p (k t) -> p k t", k=KD)
        actT = r_mem[:, 0:KD * CAP].rearrange("p (k t) -> p k t", k=KD)
        flat_mix = mixT[:, :, :].rearrange("p k t -> p (k t)")
        yT = flat_mix[:, 0:KD * CAP].rearrange("p (k t) -> p k t", k=KD)
        y_rows = flat_mix[:, KD * CAP:KD * CAP + BLOCKS * D].rearrange("p (b n) -> p b n", b=BLOCKS)
        gate_b = work[:, 0:2 * CAP].rearrange("p (s n) -> p s n", s=2)
        sig_b = work[:, 2 * CAP:4 * CAP].rearrange("p (s n) -> p s n", s=2)
        up_b = work[:, 4 * CAP:6 * CAP].rearrange("p (s n) -> p s n", s=2)

        ident = sb("ident", [P, P])
        tri = sb("tri", [P, P], bf16)
        ones_b = sb("ones_b", [P, P], bf16)
        vecs = sb("vecs", [22, P])
        vecT = sb("vecT", [P, 22])
        attn_g, mem_g = (vecT[:, 8 * n:8 * n + 8] for n in range(2))
        ffn_g = r_bias[:, 0:D]
        taps = vecT[:, 16:22]
        lam_in = r_mem[:, 0:4 * QK]
        lam = sb("lam", [P, 8])
        sub_g = sb("sub_g", [P, VD])
        rel = sb("rel", [BUCKETS, HEADS])
        router_w = sb("router_w", [P, KD, EXPERTS])
        router_b = sb("router_b", [P, EXPERTS])
        bgu_rows = wk[:, 4, 0:512].rearrange("p (a n) -> p a n", a=4)
        bdn_rows = wk[:, 4, 512:768].rearrange("p (a n) -> p a n", a=2)
        bguT = sb("bguT", [P, EXPERTS, 16])
        bdnT = sb("bdnT", [P, EXPERTS, 8])
        b_now = sb("b_now", [P, 24])
        line = wk[0:HEADS, 5, :]
        line_neg = sb("line_neg", [HEADS, P])
        one_hot = r_mem[0:BUCKETS, S:2 * S]
        shifted = work[:, 0:HEADS * S].rearrange("p (h y) -> p h y", h=HEADS)
        rev = sb("rev", [P, P])
        eps = sb("eps", [P, 1])
        ssq = sb("ssq", [P, 10])
        std = sb("std", [P, 10])
        rstd = sb("rstd", [P, 10])
        m_max = sb("m_max", [P, 2, HEADS])
        m_neg = sb("m_neg", [P, 2, HEADS])
        m_sum = sb("m_sum", [P, 2, HEADS])
        m_inv = sb("m_inv", [P, 2, HEADS])
        d_neg = sb("d_neg", [P, 2, 2])
        d_sum = sb("d_sum", [P, 2, 2])
        d_inv = sb("d_inv", [P, 3, 2])
        d_lam = sb("d_lam", [P, 2])
        sq_junk = r_mem[:, 0:VD]
        o_ssq = sb("o_ssq", [P, NT * HEADS])
        o_std = sb("o_std", [P, NT * HEADS])
        o_rs = sb("o_rs", [P, NT * HEADS])
        e_ssq = sb("e_ssq", [P, NT])
        e_std = sb("e_std", [P, NT])
        e_rstd = sb("e_rstd", [P, NT])
        h2T = wk[:, 5, :].rearrange("p (k t) -> p k t", k=KD)
        logits = sb("logits", [P, EXPERTS])
        top8 = sb("top8", [P, 8])
        top8i = sb("top8i", [P, 8], u32)
        top_e = sb("top_e", [P, NT, TOPK])
        top_neg = sb("top_neg", [P, 1])
        top_exp = sb("top_exp", [P, TOPK])
        top_sum = sb("top_sum", [P, 1])
        top_inv = sb("top_inv", [P, 1])
        chosen = sb("chosen", [P, EXPERTS])
        chosen_b = sb("chosen_b", [P, NT, EXPERTS], bf16)
        iota_e = sb("iota_e", [P, EXPERTS])
        iota_ei = sb("iota_ei", [P, EXPERTS], i32)
        place = sb("place", [P, EXPERTS])
        dest_j = sb("dest_j", [P, TOPK, EXPERTS])
        dest_f = sb("dest_f", [P, NT, TOPK])
        dest_i = sb("dest_i", [P, NT, TOPK], i32)
        pay = sb("pay", [P, NT, TOPK, 2])
        blank = wk[:, 5, 0:512].rearrange("p (n two) -> p n two", two=2)
        zeros = wk[:, 5, 512:768]
        iota_p = sb("iota_p", [P, 1])
        iota_pi = sb("iota_pi", [P, 1], i32)
        t32 = wk[0:64, 4, 0:256].rearrange("p (a e) -> p a e", e=EXPERTS)
        t1 = sb("t1", [64, 16])
        table_f = sb("table_f", [64, 4])
        table = sb("table", [4, 64], i32)
        idx_next = sb("idx_next", [P, BLOCKS, 2])
        idx_now = sb("idx_now", [P, BLOCKS, 2])
        idx_last = sb("idx_last", [P, BLOCKS, 2])
        nothing = sb("nothing", [1, 2 * BLOCKS, 16])

        ps = ctx.enter_context(nc.psum_tensor("ps", [P, 8, 512], f32))

        names = (
            "ident_made", "consts_made", "vecs_in", "vecT_ps", "vecT_made", "small_in", "mem_bias_in", "line_out",
            "shifted_in", "lists_blank", "x_std", "x_normed", "x_turned", "h_act", "h_dve",
            "w_high", "w_split", "wo_high", "wo_split", "proj_done", "proj_act", "proj_dve", "act_chain", "dve_chain", "pool_chain",
            "ms_done", "ms_max", "ms_exp", "ms_prob", "ms_turned", "ms_t_act", "ms_t_dve", "ms_av", "ms_out",
            "ds_done", "ds_read", "ds_exp", "ds_diff", "ds_turned", "ds_t_act", "ds_av", "ds_out", "ds_sq",
            "e_y", "e_oT", "e_high", "e_split", "e_mix", "e_x2", "e_x2_sq", "e_xn", "e_hT", "e_hT_act", "e_hT_dve",
            "e_log", "e_log_read", "e_chosen", "e_exp", "e_rank", "e_rank_read", "e_dest", "x2_out", "xn_out0",
            "listed", "lam_exp", "pool_waited", "silu", "xn_out1", "tab_f", "tab_ps", "tab_made",
            "gain_in", "gate_ready", "gate_read", "sig_ready", "up_ready", "up_read", "act_ready",
            "down_ready", "yT_act", "yT_dve", "idx_in", "idx_moved", "all_added", "bias_now",
        )
        s = {n: sem(n) for n in names}
        s_x = [sem(f"x_in{n}") for n in range(10)]
        s_w = [sem(f"w_in{n}") for n in range(SLOTS)]
        s_gather = [sem(f"gathered{b}") for b in range(BLOCKS)]
        s_scatter = [sem(f"scattered{b}") for b in range(BLOCKS)]
        s_yps = [sem(f"y_ps{b}") for b in range(BLOCKS)]
        s_yact = [sem(f"y_act{b}") for b in range(BLOCKS)]
        s_ydve = [sem(f"y_dve{b}") for b in range(BLOCKS)]
        s_xps = [sem(f"x_ps{b}") for b in range(BLOCKS)]
        s_xact = [sem(f"x_act{b}") for b in range(BLOCKS)]
        s_xdve = [sem(f"x_dve{b}") for b in range(BLOCKS)]
        s_final = [sem(f"final_in{n}") for n in range(4)]
        s_fout = [sem(f"final_out{n}") for n in range(4)]
        s_gf = sem("final_gain_in")
        s_fsq = sem("final_std")
        s_fdone = sem("final_done")

        w_in = a["w_mix_in"][0].rearrange("(k p) n -> p k n", p=P)
        w_kv = a["w_mem_kv"][0].rearrange("(k p) n -> p k n", p=P)
        w_out = a["w_mix_out"][0].rearrange("(k p) n -> p k n", p=P)
        units = [w_in[:, :, UW * u:UW * u + UW] for u in range(10)]
        units += [w_kv[:, :, UW * u:UW * u + UW] for u in range(2)]
        units += [w_out[:, :, UW * u:UW * u + UW] for u in range(4)]
        groups = []
        for u in range(10):
            if u == 1:
                groups += [(-1, "mem", k, 0) for k in range(0, KD, 2)]
            if u == 3:
                groups += [(-1, "line", n, 0) for n in range(2)]
            if u == 6:
                groups += [(-1, "bgu", 0, 0), (-1, "bdn", 0, 0)]
            if u in (7, 8):
                groups += [(u, "v", t, 0) for t in range(0, NT, 2)]
            else:
                groups += [(u, "t", m, half) for half in range(2) for m in range(2)]
        groups += [(10, "km", 0, 0), (11, "vm", 0, 0)]
        groups += [(-1, "rev", n // 2, n % 2) for n in range(2 * HEADS)]
        wide = {0: conv_u, 1: conv_b, 2: conv_c, 9: qmT}

        def group_dest(g):
            u, kind, x, half = groups[g]
            if kind == "v":
                return v_rows[:, x:x + 2, UW * (u - 7):UW * (u - 7) + UW]
            if kind == "line":
                return line[:, 512 * x:512 * x + 512]
            if kind == "rev":
                return master[:, x, HALF * half:HALF * half + HALF]
            if kind == "mem":
                return memT[:, x:x + 2, :]
            if kind == "bgu":
                return bguT[:, :, :].rearrange("p e m -> p (e m)")
            if kind == "bdn":
                return bdnT[:, :, :].rearrange("p e m -> p (e m)")
            if kind == "km":
                return kmT
            if kind == "vm":
                return vm
            if u in wide:
                return wide[u][:, x, HALF * half:HALF * half + HALF]
            to, first = (qT, 3) if u < 5 else (kT, 5)
            return to[:, 2 * (u - first) + x, HALF * half:HALF * half + HALF]

        def group_source(g):
            bank = ps[:, g % 8, :]
            kind = groups[g][1]
            if kind in ("v", "km", "vm", "mem"):
                return bank.rearrange("p (a n) -> p a n", a=2)
            return {"line": bank[0:HEADS, :], "bdn": bank[:, 0:256]}.get(kind, bank)

        NG = len(groups)
        first_of = {kind: min(g for g in range(NG) if groups[g][1] == kind) for kind in ("line", "bgu", "rev")}
        last_of = [max(g for g in range(NG) if groups[g][0] == u) for u in range(12)]
        conv_ready = max(g for g in range(NG) if groups[g][0] in (0, 1, 2))

        def y_bank(b, alone):
            return 4 if alone and b % 2 == 1 else 6

        def for_size(eng, kind, body, low=0, high=len(SIZES) + 1):
            if high - low == 1:
                body(SIZES[low] if low < len(SIZES) else 0)
                return
            mid = (low + high) // 2
            with eng.If(kind < mid + 1):
                for_size(eng, kind, body, low, mid)
            with eng.Else():
                for_size(eng, kind, body, mid, high)

        DOT_LINKS = 14
        CONV_LINKS = DOT_LINKS + 11

        block = ctx.enter_context(nc.Block())

        @block.sync
        def _(sp):
            x_v = a["x"][0]
            mem_v = a["mem"][0]

            def load_x(t):
                src = x_v[P * t:P * t + P, :] if t < NT else mem_v[P * (t - NT):P * (t - NT) + P, :]
                sp.dma_start(x_tile(t), src).then_inc(s_x[t], 16)

            def load_unit(n):
                if n >= PHASE1_SLOTS:
                    sp.wait_ge(s["proj_done"], last_of[n - PHASE1_SLOTS] + 1)
                sp.dma_start(slot(n % PHASE1_SLOTS), units[n]).then_inc(s_w[n % PHASE1_SLOTS], 16)

            load_x(0)
            for n, name in enumerate(("attn_norm_g", "mem_norm_g")):
                sp.dma_start(vecs[8 * n:8 * n + 8, :], a[name][0].rearrange("(k p) -> k p", p=P)).then_inc(s["vecs_in"], 16)
            sp.dma_start(vecs[16:22, :], a["conv_w"][0].rearrange("t (c p) -> (t c) p", p=P)).then_inc(s["vecs_in"], 16)
            for t in range(1, 10):
                load_x(t)
            for n in range(4):
                load_unit(n)
            sp.dma_start(lam_in, a["lambda_qk"][0].rearrange("a d -> (a d)").partition_broadcast(P)).then_inc(s["small_in"], 16)
            sp.dma_start(sub_g[:, :], a["diff_subln_g"][0].partition_broadcast(P)).then_inc(s["small_in"], 16)
            sp.dma_start(rel[:, :], a["rel_bias"]).then_inc(s["small_in"], 16)
            sp.dma_start(router_w[:, :, :], a["router_w"][0].rearrange("(k p) e -> p k e", p=P)).then_inc(s["small_in"], 16)
            sp.dma_start(router_b[:, :], a["router_b"][0].partition_broadcast(P)).then_inc(s["small_in"], 16)
            sp.wait_ge(s["x_turned"], NT)
            sp.dma_start(bgu_rows, a["b_gate_up"][0].rearrange("(g e) (m p) -> (e m) g p", g=4, p=P)).then_inc(s["mem_bias_in"], 16)
            sp.dma_start(bdn_rows, a["b_down"][0].rearrange("(g e) (m p) -> (e m) g p", g=2, p=P)).then_inc(s["mem_bias_in"], 16)
            sp.dma_start(one_hot, a["distance_one_hot"]).then_inc(s["mem_bias_in"], 16)
            for n in range(4, 6):
                load_unit(n)
            assert first_of["line"] % 2 == 0
            sp.wait_ge(s["proj_act"], first_of["line"] // 2 + 1)
            sp.wait_ge(s["proj_dve"], first_of["line"] // 2 + 1)
            sp.dma_start(line_d[:, 0:S], line).then_inc(s["line_out"], 16)
            sp.wait_ge(s["consts_made"], 1)
            sp.dma_start(line_d[:, S:LINE], line_neg[:, :]).then_inc(s["line_out"], 16)
            for n in range(6, 14):
                load_unit(n)
            sp.wait_ge(s["line_out"], 32)
            sp.wait_ge(s["proj_done"], last_of[9] + 1)
            sp.dma_start(shifted, bass.AP(line_d.tensor, 0, [[1, P], [LINE, HEADS], [1, S]])).then_inc(s["shifted_in"], 16)
            for n in range(14, 16):
                load_unit(n)
            w_gu = a["w_gate_up"][0].rearrange("e (k p) n -> p e k n", p=P)
            w_dn = a["w_down"][0].rearrange("e (k p) n -> p e k n", p=P)

            def unit_source(e, u):
                if u < GU_UNITS:
                    col = D * (u % 2) + UW * (u // 2)
                    w = w_gu
                else:
                    col = UW * (u - GU_UNITS)
                    w = w_dn
                return w[:, bass.ds(e, 1), :, col:col + UW].rearrange("p e k n -> p (e k) n")

            def load_first(u):
                sp.dma_start(slot(home(u)), unit_source(0, u)).then_inc(s_w[home(u)], 16)

            sp.wait_ge(s["ds_diff"], NT * HEADS)
            sp.wait_ge(s["ds_av"], NT * HEADS)
            sp.dma_start(ffn_g, a["ffn_norm_g"][0].partition_broadcast(P)).then_inc(s["gain_in"], 16)
            early = [u for u in range(SLOTS) if home(u) in (4, 5, 6, 7, 8, 9)]
            for i in range(NT + 1):
                if i == 1:
                    for u in early:
                        load_first(u)
                if i < NT:
                    if i >= 2:
                        sp.wait_ge(s["x2_out"], 16 * (i - 1))
                        sp.wait_ge(s["e_x2_sq"], i - 1)
                        sp.wait_ge(s["e_xn"], i - 1)
                    sp.dma_start(wk[:, i % 2, :], x_v[P * i:P * i + P, :]).then_inc(s_x[i % 2], 16)
                if i >= 1:
                    j = i - 1
                    sp.wait_ge(s["e_x2"], 2 * i)
                    sp.dma_start(acc_d[P * j:P * j + P, :], wk[:, j % 2, :]).then_inc(s["x2_out"], 16)
                    sp.wait_ge(s["e_xn"], i)
                    sp.dma_start(h_d[P * j:P * j + P, :], wk[:, 2 + j % 2, :]).then_inc(s[f"xn_out{j % 2}"], 16)
            sp.wait_ge(s["e_mix"], 2 * NT)
            sp.wait_ge(s["e_oT"], NT)
            for u in range(SLOTS):
                if u == GU_UNITS:
                    for b in range(BLOCKS):
                        sp.wait_ge(s_gather[b], 16)
                if u not in early:
                    load_first(u)
            sp.wait_ge(s["tab_made"], 1)
            with sp.Fori(0, MAX_ITEMS) as k:
                here = sp.value_load(table[2:3, bass.ds(k + 2, 1)], min_val=0, max_val=CAP + 1)
                with sp.If(here > 0):
                    e = sp.value_load(table[0:1, bass.ds(k + 2, 1)], min_val=0, max_val=EXPERTS - 1)
                    for u in range(SLOTS):
                        if u < GU_UNITS:
                            sp.wait_ge(s["gate_ready"] if u % 2 == 0 else s["up_ready"], k * 8 + (2 * (u // 2) + 2))
                        else:
                            sp.wait_ge(s["down_ready"], k * 8 + (2 * (u - GU_UNITS) + 2))
                        sp.dma_start(slot(home(u)), unit_source(e, u)).then_inc(s_w[home(u)], 16)
            sp.wait_ge(s["all_added"], 1)
            for t in range(NT):
                if t >= 4:
                    sp.wait_ge(s_fout[t % 4], 16 * (t // 4))
                sp.dma_start(wk[:, t % 4, :], acc_d[P * t:P * t + P, :]).then_inc(s_final[t % 4], 16)
                if t == 0:
                    sp.dma_start(wk[:, 5, :], a["final_norm_g"].partition_broadcast(P)).then_inc(s_gf, 16)
                if t >= 2:
                    sp.wait_ge(s_fdone, t - 1)
                    sp.dma_start(out[0, P * (t - 2):P * (t - 2) + P, :], wk[:, (t - 2) % 4, :]).then_inc(s_fout[(t - 2) % 4], 16)
            for t in range(NT - 2, NT):
                sp.wait_ge(s_fdone, t + 1)
                sp.dma_start(out[0, P * t:P * t + P, :], wk[:, t % 4, :]).then_inc(s_fout[t % 4], 16)
            for n in range(4):
                sp.wait_ge(s_fout[n], 16 * (NT // 4))

        @block.gpsimd
        def _(pool):
            pool.memset(ident[:, :], 0.0).then_inc(s["pool_chain"], 1)
            pool.wait_ge(s["pool_chain"], 1)
            pool.affine_select(out=ident[:, :], in_=ident[:, :], compare_op=ALU.not_equal, fill=1.0, base=0,
                               pattern=[[-1, P]], channel_multiplier=1).then_inc(s["ident_made"], 1)
            pool.memset(eps[:, :], EPS).then_inc(s["ident_made"], 1)
            pool.memset(blank[:, :, :], 0.0).then_inc(s["pool_chain"], 1)
            pool.memset(zeros, 0.0).then_inc(s["pool_chain"], 1)
            pool.wait_ge(s["pool_chain"], 3)
            pool.iota(blank.bitcast(i32)[:, :, 0], pattern=[[0, 2], [1, P]], base=S, channel_multiplier=0).then_inc(s["pool_chain"], 1)
            pool.wait_ge(s["pool_chain"], 4)
            pool.dma_start(list_d[0:LIST, :].rearrange("(p n) two -> p n two", p=P), blank).then_inc(s["lists_blank"], 16)
            pool.dma_start(list_d[LIST:LIST + LIST_PAD, :].rearrange("(a n) two -> a n two", a=1), blank[0:1, 0:P, :]).then_inc(s["lists_blank"], 16)
            z4 = zeros.unsqueeze(1).broadcast_to((P, 4, 256))
            pool.dma_start(h_d[S:ROWS, :].rearrange("p (a n) -> p a n", a=4), z4).then_inc(s["lists_blank"], 16)
            pool.dma_start(acc_d[S:ROWS, :].rearrange("p (a n) -> p a n", a=4), z4).then_inc(s["lists_blank"], 16)
            pool.memset(rev[:, :], 0.0).then_inc(s["pool_chain"], 1)
            pool.memset(ones_b[:, :], 1.0).then_inc(s["pool_chain"], 1)
            pool.memset(line_neg[:, :], NEG / SCALE).then_inc(s["pool_chain"], 1)
            pool.iota(iota_ei[:, :], pattern=[[1, EXPERTS]], base=0, channel_multiplier=0).then_inc(s["pool_chain"], 1)
            pool.iota(iota_pi[:, :], pattern=[[0, 1]], base=-1, channel_multiplier=1).then_inc(s["pool_chain"], 1)
            pool.iota(pay.bitcast(i32)[:, :, :, 0], pattern=[[P, NT], [0, TOPK]], base=0, channel_multiplier=1).then_inc(s["pool_chain"], 1)
            pool.wait_ge(s["pool_chain"], 10)
            pool.affine_select(out=rev[:, :], in_=rev[:, :], compare_op=ALU.not_equal, fill=1.0, base=1 - P,
                               pattern=[[1, P]], channel_multiplier=1).then_inc(s["pool_chain"], 1)
            pool.affine_select(out=tri[:, :], in_=ones_b[:, :], compare_op=ALU.is_gt, fill=0.0, base=0,
                               pattern=[[1, P]], channel_multiplier=-1).then_inc(s["pool_chain"], 1)
            pool.tensor_copy(iota_e[:, :], iota_ei[:, :]).then_inc(s["pool_chain"], 1)
            pool.tensor_copy(iota_p[:, :], iota_pi[:, :]).then_inc(s["pool_chain"], 1)
            pool.wait_ge(s["pool_chain"], 14)
            pool.nop().then_inc(s["consts_made"], 1)
            for i in range(NT):
                pool.wait_ge(s["e_dest"], i + 1)
                if i == 0:
                    pool.wait_ge(s["lists_blank"], 64)
                for c in range(TOPK):
                    pool.indirect_dma_start(
                        list_d[:, :], bass.IndirectOffsetOnAxis(ap=dest_i[:, i, c:c + 1], axis=0),
                        pay[:, i, c, :], None).then_inc(s["listed"], 16)
            pool.wait_ge(s["listed"], 16 * NT * TOPK)
            pool.wait_ge(s["xn_out0"], 16 * NT // 2)
            pool.wait_ge(s["xn_out1"], 16 * NT // 2)
            pool.wait_ge(s["x2_out"], 16 * NT)

            def load_list(first):
                pool.dma_start(idx_next[:, :, :], list_d[first, :].rearrange("(b p) two -> p b two", p=P))\
                    .then_inc(s["idx_in"], 16)

            def gather(entry):
                size = pool.value_load(table[2:3, entry], min_val=0, max_val=CAP + 1)
                for b in range(BLOCKS):
                    with pool.If(size > P * b + 1):
                        pool.indirect_dma_start(
                            xg[:, b, :], None, h_d[:, :],
                            bass.IndirectOffsetOnAxis(ap=idx_next.bitcast(i32)[:, b, 0:1], axis=0)).then_inc(s_gather[b], 16)
                    with pool.Else():
                        pool.dma_start(nothing[0:1, 2 * b, :], ident[0:1, 0:16]).then_inc(s_gather[b], 16)

            for b in range(BLOCKS):
                pool.dma_start(nothing[0:1, 2 * b + 1, :], ident[0:1, 0:16]).then_inc(s_scatter[b], 16)
            load_list(slice(0, CAP))
            pool.wait_ge(s["idx_in"], 16)
            for b in range(BLOCKS):
                pool.indirect_dma_start(
                    xg[:, b, :], None, h_d[:, :],
                    bass.IndirectOffsetOnAxis(ap=idx_next.bitcast(i32)[:, b, 0:1], axis=0)).then_inc(s_gather[b], 16)
            pool.tensor_copy(idx_now[:, :, :], idx_next[:, :, :]).then_inc(s["idx_moved"], 1)
            pool.wait_ge(s["tab_made"], 1)
            with pool.Fori(0, MAX_ITEMS + 1) as it:
                size_last = pool.value_load(table[2:3, bass.ds(it, 1)], min_val=0, max_val=CAP + 1)
                size_now = pool.value_load(table[2:3, bass.ds(it + 1, 1)], min_val=0, max_val=CAP + 1)
                with pool.If(size_now > 0):
                    for b in range(BLOCKS):
                        pool.wait_ge(s_gather[b], it * 16 + 16)
                    pool.wait_ge(s["idx_moved"], it + 1)
                    first = pool.value_load(table[1:2, bass.ds(it + 2, 1)], min_val=0, max_val=LIST + LIST_PAD - CAP)
                    load_list(bass.ds(first, CAP))
                    for b in range(BLOCKS):
                        pool.wait_ge(s_xps[b], it * 2 + 2)
                    pool.wait_ge(s["idx_in"], it * 16 + 32)
                    gather(bass.ds(it + 2, 1))
                with pool.If(size_last > 0):
                    for b in range(BLOCKS):
                        with pool.If(size_last > P * b + 1):
                            pool.wait_ge(s_yact[b], it + 1)
                            pool.wait_ge(s_ydve[b], it + 1)
                            if b > 0:
                                pool.wait_ge(s_scatter[b - 1], it * 16 + 16)
                            pool.sem_inc(s["pool_waited"], 1)
                            pool.indirect_dma_start(
                                acc_d[:, :], bass.IndirectOffsetOnAxis(ap=idx_last.bitcast(i32)[:, b, 0:1], axis=0),
                                y_rows[:, b, :], None, compute_op=ALU.add).then_inc(s_scatter[b], 16)
                        with pool.Else():
                            pool.dma_start(nothing[0:1, 2 * b + 1, :], ident[0:1, 0:16]).then_inc(s_scatter[b], 16)
                    for b in range(BLOCKS):
                        pool.wait_ge(s_scatter[b], it * 16 + 16)
                    pool.sem_inc(s["pool_waited"], 1)
                    with pool.If(size_now == 0):
                        pool.sem_inc(s["all_added"], 1)
                with pool.If(size_now > 0):
                    pool.tensor_copy(idx_last[:, :, :], idx_now[:, :, :]).then_inc(s["pool_chain"], 1)
                    pool.wait_ge(s["pool_chain"], it + 15)
                    pool.sem_inc(s["pool_waited"], 1)
                    pool.tensor_copy(idx_now[:, :, :], idx_next[:, :, :]).then_inc(s["idx_moved"], 1)

        @block.tensor
        def _(pe):
            def mm(o, l, r, first, last):
                return pe.matmul(o, l, r, start=first, stop=last)

            pe.wait_ge(s["ident_made"], 1)
            pe.wait_ge(s["vecs_in"], 48)
            pe.transpose(ps[:, 0, 0:22], vecs[:, :], ident[0:22, 0:22]).then_inc(s["vecT_ps"], 1)
            for t in range(NT):
                pe.wait_ge(s["x_normed"], t + 1)
                if t == 0:
                    pe.wait_ge(s["vecT_made"], 1)
                if t == 4:
                    pe.wait_ge(s["h_act"], 2 * t)
                    pe.wait_ge(s["h_dve"], 2 * t)
                for k in range(KD):
                    last = pe.transpose(ps[:, k, P * (t % 4):P * (t % 4) + P], x_tile(t)[:, P * k:P * k + P], ident[:, :])
                last.then_inc(s["x_turned"], 1)
            for g in range(NG):
                u, kind, x, half = groups[g]
                if kind == "line":
                    pe.wait_ge(s["mem_bias_in"], 48)
                    pe.wait_ge(s["small_in"], 80)
                if kind == "rev":
                    pe.wait_ge(s["shifted_in"], 16)
                    pe.wait_ge(s["consts_made"], 1)
                if 0 <= u < 10:
                    pe.wait_ge(s["w_split"], u + 1)
                elif u >= 0:
                    pe.wait_ge(s_w[u % PHASE1_SLOTS], 16 * (u // PHASE1_SLOTS + 1))
                if g == 0:
                    pe.wait_ge(s["h_act"], 16)
                    pe.wait_ge(s["h_dve"], 16)
                if g >= 8:
                    pe.wait_ge(s["proj_act"] if g % 2 == 0 else s["proj_dve"], g // 2 - 3)
                w = slot(u % PHASE1_SLOTS)
                bank = ps[:, g % 8, :]
                pair = bank.rearrange("p (a n) -> p a n", a=2)
                if kind in ("t", "v"):
                    whi = w_hi(u).rearrange("p (k c) -> p k c", k=KD)
                    wlo = w_lo(u).rearrange("p (k c) -> p k c", k=KD)
                if kind == "t":
                    cols, toks = slice(P * x, P * x + P), slice(HALF * half, HALF * half + HALF)
                    for k in range(KD):
                        mm(bank, whi[:, k, cols], hT_hi[:, k, toks], k == 0, False)
                        mm(bank, whi[:, k, cols], hT_lo(k)[:, toks], False, False)
                        last = mm(bank, wlo[:, k, cols], hT_hi[:, k, toks], False, k == KD - 1)
                elif kind == "v":
                    for n in range(2):
                        toks = slice(P * (x + n), P * (x + n) + P)
                        for k in range(KD):
                            mm(pair[:, n, :], hT_hi[:, k, toks], whi[:, k, :], k == 0, False)
                            mm(pair[:, n, :], hT_hi[:, k, toks], wlo[:, k, :], False, False)
                            last = mm(pair[:, n, :], hT_lo(k)[:, toks], whi[:, k, :], False, k == KD - 1)
                elif kind == "mem":
                    pe.wait_ge(s["x_normed"], 10)
                    for n in range(2):
                        for m in range(2):
                            last = pe.transpose(pair[:, n, P * m:P * m + P], x_tile(NT + m)[:, P * (x + n):P * (x + n) + P], ident[:, :])
                elif kind == "line":
                    last = mm(bank[0:HEADS, :], rel[:, :], one_hot[:, 512 * x:512 * x + 512], True, True)
                elif kind == "rev":
                    last = mm(bank, rev[:, :], shifted[:, x, HALF * half:HALF * half + HALF], True, True)
                elif kind in ("bgu", "bdn"):
                    rows = bgu_rows if kind == "bgu" else bdn_rows
                    for n in range(rows.shape[1]):
                        last = pe.transpose(bank[:, P * n:P * n + P], rows[:, n, :], ident[:, :])
                elif kind == "km":
                    for n in range(2):
                        for k in range(KD):
                            last = mm(pair[:, n, :], w[:, k, P * n:P * n + P], memT[:, k, :], k == 0, k == KD - 1)
                else:
                    for n in range(2):
                        for k in range(KD):
                            last = mm(pair[:, n, :], memT[:, k, P * n:P * n + P], w[:, k, :], k == 0, k == KD - 1)
                last.then_inc(s["proj_done"], 1)
            pe.wait_ge(s["proj_act"], NG // 2)
            pe.wait_ge(s["proj_dve"], NG // 2)
            for i in range(NT + 2):
                if i < NT:
                    if i >= 2:
                        pe.wait_ge(s["ms_exp"], 4 * (i - 1))
                    for h in range(HEADS):
                        q = 64 * (h % 2)
                        last = mm(ps[:, 2 * (i % 2) + h % 2, MEM * (h // 2):MEM * (h // 2) + MEM],
                                  qmT[q:q + QK, h // 2, P * i:P * i + P], kmT[q:q + QK, h // 2, :], True, True)
                    last.then_inc(s["ms_done"], 1)
                if 1 <= i <= NT:
                    j = i - 1
                    pe.wait_ge(s["ms_prob"], j + 1)
                    if j >= 1:
                        pe.wait_ge(s["ms_t_act"], j)
                        pe.wait_ge(s["ms_t_dve"], j)
                    for n in range(8):
                        last = pe.transpose(ps[:, 4 + n // 4, P * (n % 4):P * (n % 4) + P], wk[:, j % 2, P * n:P * n + P], ident[:, :])
                    last.then_inc(s["ms_turned"], 1)
                if i >= 2:
                    j = i - 2
                    pe.wait_ge(s["ms_t_act"], j + 1)
                    pe.wait_ge(s["ms_t_dve"], j + 1)
                    if j >= 2:
                        pe.wait_ge(s["ms_out"], j - 1)
                    for h in range(HEADS):
                        at = 2 * (h % 2) + h // 2
                        for m in range(2):
                            last = mm(ps[64 * (h % 2):64 * (h % 2) + 64, 6 + j % 2, P * (h // 2):P * (h // 2) + P],
                                      vm[:, m, QK * h:QK * h + QK],
                                      wk[:, 2 + j % 2, P * (2 * at + m):P * (2 * at + m) + P], m == 0, m == 1)
                    last.then_inc(s["ms_av"], 1)

            NU = NT * HEADS
            pe.wait_ge(s["ms_exp"], 4 * NT)
            pe.wait_ge(s["ms_t_act"], NT)
            pe.wait_ge(s["ms_t_dve"], NT)
            pe.wait_ge(s["ms_out"], NT)
            for j in range(NU + 2):
                if j < NU:
                    i, h = divmod(j, HEADS)
                    kv = P * (i + 1)
                    for c in range(2):
                        if j >= 1:
                            pe.wait_ge(s["ds_read"], 2 * j - 1 + c)
                        for n in range(0, kv, 512):
                            last = mm(ps[:, 2 * c + n // 512, 0:min(512, kv - n)], qT[QK * c:QK * c + QK, h, P * i:P * i + P],
                                      kT[QK * c:QK * c + QK, h, n:min(n + 512, kv)], True, True)
                        last.then_inc(s["ds_done"], 1)
                if j >= 2:
                    n = j - 2
                    i, h = divmod(n, HEADS)
                    pe.wait_ge(s["ds_t_act"], n + 1)
                    if n >= 2:
                        pe.wait_ge(s["ds_out"], n - 1)
                    for b in range(i + 1):
                        last = mm(ps[:, 6 + n % 2, 0:VD], wk[:, 4 + n % 2, P * b:P * b + P], v_rows[:, b, VD * h:VD * h + VD], b == 0, b == i)
                    last.then_inc(s["ds_av"], 1)
                if 1 <= j <= NU:
                    n = j - 1
                    pe.wait_ge(s["ds_diff"], n + 1)
                    if n >= 1:
                        pe.wait_ge(s["ds_t_act"], n)
                    for b in range(n // HEADS + 1):
                        last = pe.transpose(ps[:, 4 + b // 4, P * (b % 4):P * (b % 4) + P], wk[:, 2 * (n % 2), P * b:P * b + P], ident[:, :])
                    last.then_inc(s["ds_turned"], 1)

            pe.wait_ge(s["ds_out"], NU)
            pe.wait_ge(s["wo_split"], 16)
            pe.wait_ge(s["consts_made"], 1)

            def turn_heads(i):
                pe.wait_ge(s["e_y"], i + 1)
                if i >= 1:
                    pe.wait_ge(s["e_split"], i)
                for h in range(HEADS):
                    last = pe.transpose(ps[:, 4, P * h:P * h + P], o_all[:, i, P * h:P * h + P], ident[:, :])
                last.then_inc(s["e_oT"], 1)

            turn_heads(0)
            turn_heads(1)
            for i in range(NT + 2):
                if i < NT:
                    pe.wait_ge(s["e_split"], i + 1)
                    if i >= 2:
                        pe.wait_ge(s["e_x2"], 2 * (i - 1))
                    mhi, mlo = mix_parts(i)
                    for half in range(2):
                        for q in (2 * half, 2 * half + 1):
                            whi = w_out_hi(q).rearrange("p (k c) -> p k c", k=KD)
                            wlo = w_lo(12 + q).rearrange("p (k c) -> p k c", k=KD)
                            to = ps[:, 2 * (i % 2) + half, UW * (q % 2):UW * (q % 2) + UW]
                            for k in range(KD):
                                mm(to, mhi[:, k, :], whi[:, k, :], k == 0, False)
                                mm(to, mhi[:, k, :], wlo[:, k, :], False, False)
                                last = mm(to, mlo[:, k, :], whi[:, k, :], False, k == KD - 1)
                        last.then_inc(s["e_mix"], 1)
                if 1 <= i <= NT:
                    j = i - 1
                    pe.wait_ge(s["e_xn"], j + 1)
                    if j >= 1:
                        pe.wait_ge(s["e_hT_act"], j)
                        pe.wait_ge(s["e_hT_dve"], j)
                    if j >= 2:
                        pe.wait_ge(s["e_rank_read"], j - 1)
                    for k in range(KD):
                        last = pe.transpose(ps[:, 5 + k // 4, P * (k % 4):P * (k % 4) + P], wk[:, 2 + j % 2, P * k:P * k + P], ident[:, :])
                    last.then_inc(s["e_hT"], 1)
                if i + 2 < NT:
                    turn_heads(i + 2)
                if 1 <= i <= NT:
                    j = i - 1
                    pe.wait_ge(s["e_hT_act"], j + 1)
                    pe.wait_ge(s["e_hT_dve"], j + 1)
                    if j >= 1:
                        pe.wait_ge(s["e_log_read"], j)
                    for k in range(KD):
                        last = mm(ps[:, 7, 0:EXPERTS], h2T[:, k, :], router_w[:, k, :], k == 0, k == KD - 1)
                    last.then_inc(s["e_log"], 1)
                if i >= 2:
                    j = i - 2
                    pe.wait_ge(s["e_chosen"], j + 1)
                    if j >= 1:
                        pe.wait_ge(s["e_rank_read"], j)
                    for b in range(j + 1):
                        last = mm(ps[:, 5, 0:EXPERTS], (tri if b == j else ones_b)[:, :], chosen_b[:, b, :], b == 0, b == j)
                    last.then_inc(s["e_rank"], 1)
            pe.wait_ge(s["e_rank_read"], NT)
            for b in range(NT):
                last = mm(ps[:, 5, 0:EXPERTS], ones_b[:, :], chosen_b[:, b, :], b == 0, b == NT - 1)
            last.then_inc(s["e_rank"], 1)
            pe.wait_ge(s["tab_f"], 1)
            pe.transpose(ps[0:4, 4, 0:64], table_f[:, :], ident[0:64, 0:64]).then_inc(s["tab_ps"], 1)
            pe.wait_ge(s["tab_made"], 1)

            def turn_x(b, done):
                pe.wait_ge(s_gather[b], done * 16 + 16)
                if b > 0:
                    pe.wait_ge(s_xact[b - 1], done + 1)
                    pe.wait_ge(s_xdve[b - 1], done + 1)
                for half in range(2):
                    for k in range(4):
                        last = pe.transpose(ps[:, 4 + half, P * k:P * k + P],
                                            xg[:, b, HALF * half + P * k:HALF * half + P * k + P], ident[:, :])
                    last.then_inc(s_xps[b], 1)

            def turn_y(b, it, alone):
                before = b - (2 if alone else 1)
                if before >= 0:
                    pe.wait_ge(s_yact[before], it + 1)
                    pe.wait_ge(s_ydve[before], it + 1)
                for half in range(2):
                    for m in range(4):
                        last = pe.transpose(ps[:, y_bank(b, alone) + half, P * m:P * m + P], yT[:, 4 * half + m, P * b:P * b + P], ident[:, :])
                    last.then_inc(s_yps[b], 1)

            def turn_rows(it, size_last, size_next):
                for b in range(BLOCKS):
                    if size_next is not None:
                        with pe.If(size_next > P * b + 1):
                            turn_x(b, it + 1)
                        with pe.Else():
                            pe.sem_inc(s_xps[b], 2)
                    with pe.If(size_last > P * b + 1):
                        turn_y(b, it, size_next is None)
                    with pe.Else():
                        pe.sem_inc(s_yps[b], 2)

            def up_products(it, n):
                for b in range(-(-n // P)):
                    pe.wait_ge(s_xact[b], it + 1)
                    pe.wait_ge(s_xdve[b], it + 1)
                sizes = []
                for j in range(KD):
                    if j in (2, 4):
                        sizes.append(pe.value_load(table[2:3, bass.ds(it + j - 2, 1)], min_val=0, max_val=CAP + 1))
                    for bank, side, read, ready in ((j % 2, 0, "gate_read", "gate_ready"), (2 + j % 2, 1, "up_read", "up_ready")):
                        u = 2 * (j // 2) + side
                        if j % 2 == 0:
                            pe.wait_ge(s_w[home(u)], arrived(u, it))
                        if j < 2:
                            pe.wait_ge(s["yT_act"] if j == 0 else s["yT_dve"], it * 4 + 1 + side)
                        else:
                            pe.wait_ge(s[read], it * 8 + 1 + (j - 1))
                        for k in range(KD):
                            last = mm(ps[:, bank, 0:n], slot(home(u))[:, k, P * (j % 2):P * (j % 2) + P], xT[:, k, 0:n], k == 0, k == KD - 1)
                        last.then_inc(s[ready], 1)
                return sizes

            def down_products(it, n):
                for m in range(KD):
                    u = GU_UNITS + m // 2
                    if m % 2 == 0:
                        pe.wait_ge(s_w[home(u)], arrived(u, it))
                    if m >= 4:
                        pe.wait_ge(s["yT_act"] if m % 2 == 0 else s["yT_dve"], it * 4 + 2 + (m - 4) // 2 + 1)
                    if m == 1:
                        pe.wait_ge(s["up_read"], it * 8 + 9)
                    for k in range(KD):
                        if m == 0 and k in (0, 6, 7):
                            pe.wait_ge(s["act_ready"], it * 8 + 1 + (6 if k == 0 else k + 1))
                        last = mm(ps[:, m % 4, 0:n], slot(home(u))[:, k, P * (m % 2):P * (m % 2) + P], actT[:, k, 0:n], k == 0, k == KD - 1)
                    last.then_inc(s["down_ready"], 1)

            for b in range(BLOCKS):
                turn_x(b, 0)
            with pe.Fori(0, MAX_ITEMS + 1) as it:
                kind_now = pe.value_load(table[3:4, bass.ds(it + 1, 1)], min_val=0, max_val=len(SIZES) + 1)

                def item(n):
                    if n > 0:
                        size_last, size_next = up_products(it, n)
                        turn_rows(it, size_last, size_next)
                        down_products(it, n)
                    else:
                        size_last = pe.value_load(table[2:3, bass.ds(it, 1)], min_val=0, max_val=CAP + 1)
                        pe.wait_ge(s["yT_act"], it * 4 + 2)
                        pe.wait_ge(s["yT_dve"], it * 4 + 2)
                        turn_rows(it, size_last, None)

                with pe.If(kind_now > 0):
                    for_size(pe, kind_now, item)

        @block.scalar
        def _(act):
            def high_part(u):
                act.wait_ge(s_w[u % PHASE1_SLOTS], 16 * (u // PHASE1_SLOTS + 1))
                if u >= 2:
                    act.wait_ge(s["proj_done"], last_of[u - 2] + 1)
                act.activation(w_hi(u), slot(u % PHASE1_SLOTS).rearrange("p k c -> p (k c)"), ACT.Copy)\
                    .then_inc(s["w_high"], 1)

            act.wait_ge(s["ident_made"], 2)
            for t in range(10):
                act.wait_ge(s_x[t], 16)
                act.activation(r_mem[:, 2 * S:2 * S + D], x_tile(t), ACT.Square, accum_out=ssq[:, t:t + 1]).then_inc(s["act_chain"], 1)
                act.wait_ge(s["act_chain"], t + 1)
                act.activation(std[:, t:t + 1], ssq[:, t:t + 1], ACT.Sqrt, scale=1.0 / D, bias=eps[:, :]).then_inc(s["x_std"], 1)
                if t == 7:
                    high_part(0)
                if t in (3, 7):
                    act.wait_ge(s["x_turned"], t + 1)
                    if t == 3:
                        act.wait_ge(s["vecT_made"], 1)
                    for k in range(KD):
                        act.activation(hT_hi[:, k, HALF * (t // 4):HALF * (t // 4) + HALF], ps[:, k, :], ACT.Identity, scale=attn_g[:, k:k + 1]).then_inc(s["h_act"], 1)
                if t == 7:
                    high_part(1)
            for g in range(0, NG, 2):
                if g >= 2 and g - 1 in last_of[0:8]:
                    high_part(last_of.index(g - 1) + 2)
                act.wait_ge(s["proj_done"], g + 1)
                if groups[g][1] == "v":
                    act.wait_ge(s["dve_chain"], CONV_LINKS)
                if groups[g][1] == "line":
                    act.wait_ge(s["lists_blank"], 64)
                if groups[g][1] == "mem":
                    k = groups[g][2]
                    act.activation(memT[:, k, :], group_source(g)[:, 0, :], ACT.Identity, scale=mem_g[:, k:k + 1])
                    act.activation(memT[:, k + 1, :], group_source(g)[:, 1, :], ACT.Identity, scale=mem_g[:, k + 1:k + 2])\
                        .then_inc(s["proj_act"], 1)
                    continue
                act.activation(group_dest(g), group_source(g), ACT.Copy,
                               scale=1.0 / SCALE if groups[g][1] == "line" else 1.0).then_inc(s["proj_act"], 1)
            act.wait_ge(s["dve_chain"], DOT_LINKS)
            act.activation(lam[:, 2:4], lam[:, 0:2], ACT.Exp).then_inc(s["lam_exp"], 1)
            for i in range(NT + 1):
                if i < NT:
                    act.wait_ge(s["ms_done"], i + 1)
                    act.wait_ge(s["ms_max"], i + 1)
                    if i >= 2:
                        act.wait_ge(s["ms_turned"], i - 1)
                    for h in range(HEADS):
                        act.activation(wk[:, i % 2, MEM * h:MEM * h + MEM],
                                       ps[:, 2 * (i % 2) + h // 2, MEM * (h % 2):MEM * (h % 2) + MEM], ACT.Exp,
                                       scale=SCALE, bias=m_neg[:, i % 2, h:h + 1], accum_out=m_sum[:, i % 2, h:h + 1])\
                            .then_inc(s["ms_exp"], 1)
                if i >= 1:
                    j = i - 1
                    act.wait_ge(s["ms_turned"], j + 1)
                    if j >= 2:
                        act.wait_ge(s["ms_av"], j - 1)
                    act.activation(wk[:, 2 + j % 2, 0:512], ps[:, 4, :], ACT.Copy).then_inc(s["ms_t_act"], 1)

            NU = NT * HEADS
            act.wait_ge(s["ms_turned"], NT)
            act.wait_ge(s["ms_av"], NT)

            def exponentials(j, c):
                kv = P * (j // HEADS + 1)
                act.wait_ge(s["ds_read"], 2 * j + c + 1)
                src = wk[:, 2 * (j % 2) + c, 0:kv]
                act.activation(src, src, ACT.Exp, scale=-1.0, bias=d_neg[:, j % 2, c:c + 1], accum_out=d_sum[:, j % 2, c:c + 1])\
                    .then_inc(s["ds_exp"], 1)

            for j in range(NU + 2):
                if j < NU:
                    exponentials(j, 0)
                if j >= 2:
                    n = j - 2
                    i, h = divmod(n, HEADS)
                    act.wait_ge(s["ds_av"], n + 1)
                    act.activation(o_all[:, i, VD * h:VD * h + VD], ps[:, 6 + n % 2, 0:VD], ACT.Copy,
                                   scale=d_inv[:, n % 3, 0:1]).then_inc(s["ds_out"], 1)
                    act.wait_ge(s["ds_out"], n + 1)
                    act.activation(sq_junk[:, :], o_all[:, i, VD * h:VD * h + VD], ACT.Square,
                                   accum_out=o_ssq[:, n:n + 1]).then_inc(s["ds_sq"], 1)
                if 1 <= j <= NU:
                    n = j - 1
                    nb = n // HEADS + 1
                    act.wait_ge(s["ds_turned"], n + 1)
                    if n >= 2:
                        act.wait_ge(s["ds_av"], n - 1)
                    act.activation(wk[:, 4 + n % 2, 0:P * nb], ps[:, 4:6, :].rearrange("p b n -> p (b n)")[:, 0:P * nb], ACT.Copy)\
                        .then_inc(s["ds_t_act"], 1)
                if j < NU:
                    exponentials(j, 1)
                if NU - 16 <= j < NU:
                    q, part = divmod(j - (NU - 16), 4)
                    cols = slice(HALF * part, HALF * part + HALF)
                    act.wait_ge(s_w[q], 16 * 4)
                    act.activation(w_out_hi(q)[:, cols], ring[:, q, cols], ACT.Copy).then_inc(s["wo_high"], 1)

            act.wait_ge(s["ds_sq"], NU)
            act.activation(o_std[:, :], o_ssq[:, :], ACT.Sqrt, scale=1.0 / VD, bias=eps[:, :]).then_inc(s["ds_sq"], 1)

            def mix_high(i):
                if i >= 2:
                    act.wait_ge(s["e_mix"], 2 * (i - 1))
                high, _ = mix_parts(i)
                act.activation(high[:, 0:2, :], conv_b[:, :, P * i:P * i + P], ACT.Copy)
                act.activation(high[:, 6:8, :], mixT[:, 6:8, P * i:P * i + P], ACT.Copy)
                act.wait_ge(s["e_oT"], i + 1)
                act.activation(high[:, 2:6, :], ps[:, 4, :].rearrange("p (h t) -> p h t", h=HEADS), ACT.Copy).then_inc(s["e_high"], 1)

            for i in range(3):
                mix_high(i)
            for i in range(1, NT + 1):
                j = i - 1
                act.wait_ge(s["e_x2"], 2 * j + 2)
                act.activation(wk[:, 4, :], wk[:, j % 2, :], ACT.Square, accum_out=e_ssq[:, j:j + 1]).then_inc(s["act_chain"], 1)
                act.wait_ge(s["act_chain"], 10 + j + 1)
                act.activation(e_std[:, j:j + 1], e_ssq[:, j:j + 1], ACT.Sqrt, scale=1.0 / D, bias=eps[:, :]).then_inc(s["e_x2_sq"], 1)
                act.wait_ge(s["e_hT"], j + 1)
                if j >= 1:
                    act.wait_ge(s["e_log"], j)
                act.activation(h2T[:, 0:4, :], ps[:, 5, :].rearrange("p (k t) -> p k t", t=P), ACT.Copy).then_inc(s["e_hT_act"], 1)
                if i + 2 < NT:
                    mix_high(i + 2)
                act.wait_ge(s["e_chosen"], j + 1)
                act.activation(top_exp[:, :], top8[:, 0:TOPK], ACT.Exp, bias=top_neg[:, :], accum_out=top_sum[:, :]).then_inc(s["e_exp"], 1)

            act.preload_act_table(ACT.Sigmoid)
            act.wait_ge(s["tab_made"], 1)

            def read_x(b, done):
                act.wait_ge(s_xps[b], done * 2 + 1)
                act.activation(xT[:, 0:4, P * b:P * b + P], ps[:, 4, :].rearrange("p (k t) -> p k t", t=P), ACT.Copy)\
                    .then_inc(s_xact[b], 1)

            def read_y(b, it, alone):
                act.wait_ge(s_yps[b], it * 2 + 1)
                act.wait_ge(s["idx_moved"], it + 1)
                act.wait_ge(s_scatter[b], it * 16)
                act.activation(y_rows[:, b, 0:512], ps[:, y_bank(b, alone), :], ACT.Copy, scale=idx_last[:, b, 1:2]).then_inc(s_yact[b], 1)

            def read_rows(it, size_last, size_next):
                for b in range(BLOCKS):
                    if size_next is not None:
                        with act.If(size_next > P * b + 1):
                            read_x(b, it + 1)
                        with act.Else():
                            act.sem_inc(s_xact[b], 1)
                    with act.If(size_last > P * b + 1):
                        read_y(b, it, size_next is None)
                    with act.Else():
                        act.sem_inc(s_yact[b], 1)

            def gate_sigmoids(it, n):
                for j in range(KD):
                    act.wait_ge(s["gate_read"], it * 8 + 1 + (j + 1))
                    act.wait_ge(s["act_ready"], it * 8 + 1 + max(j - 1, 0))
                    act.activation(sig_b[:, j % 2, 0:n], gate_b[:, j % 2, 0:n], ACT.Sigmoid, scale=ALPHA).then_inc(s["sig_ready"], 1)

            def down_part(it, n):
                act.wait_ge(s["bias_now"], it * 2 + 2)
                for m in range(0, KD, 2):
                    act.wait_ge(s["down_ready"], it * 8 + (m + 1))
                    act.activation(yT[:, m, 0:n], ps[:, m % 4, 0:n], ACT.Identity, bias=b_now[:, 16 + m:17 + m]).then_inc(s["yT_act"], 1)

            for b in range(BLOCKS):
                read_x(b, 0)
            act.sem_inc(s["sig_ready"], 1)
            act.sem_inc(s["yT_act"], 2)
            with act.Fori(0, MAX_ITEMS + 1) as it:
                kind_now = act.value_load(table[3:4, bass.ds(it + 1, 1)], min_val=0, max_val=len(SIZES) + 1)
                with act.If(kind_now > 0):
                    size_last = act.value_load(table[2:3, bass.ds(it, 1)], min_val=0, max_val=CAP + 1)
                    size_next = act.value_load(table[2:3, bass.ds(it + 2, 1)], min_val=0, max_val=CAP + 1)

                    def item(n):
                        if n > 0:
                            gate_sigmoids(it, n)
                            read_rows(it, size_last, size_next)
                            down_part(it, n)
                        else:
                            read_rows(it, size_last, None)

                    for_size(act, kind_now, item)
            for t in range(NT):
                act.wait_ge(s_final[t % 4], 16 * (t // 4 + 1))
                act.activation(wk[:, 4, :], wk[:, t % 4, :], ACT.Square, accum_out=e_ssq[:, t:t + 1]).then_inc(s["act_chain"], 1)
                act.wait_ge(s["act_chain"], 18 + t + 1)
                act.activation(e_std[:, t:t + 1], e_ssq[:, t:t + 1], ACT.Sqrt, scale=1.0 / D, bias=eps[:, :]).then_inc(s_fsq, 1)

        @block.vector
        def _(dve):
            chain = [0]

            def link(ins):
                chain[0] += 1
                ins.then_inc(s["dve_chain"], 1)
                dve.wait_ge(s["dve_chain"], chain[0])

            dve.wait_ge(s["vecT_ps"], 1)
            dve.tensor_copy(vecT[:, :], ps[:, 0, 0:22]).then_inc(s["vecT_made"], 1)
            def low_part(u):
                dve.wait_ge(s["w_high"], u + 1)
                whole = slot(u % PHASE1_SLOTS).rearrange("p k c -> p (k c)")
                dve.tensor_tensor(w_lo(u), whole, w_hi(u).bitcast(f32), ALU.subtract).then_inc(s["w_split"], 1)

            dve.wait_ge(s["vecT_made"], 1)
            for t in range(10):
                dve.wait_ge(s["x_std"], t + 1)
                link(dve.reciprocal(rstd[:, t:t + 1], std[:, t:t + 1]))
                dve.tensor_scalar(x_tile(t), x_tile(t), rstd[:, t:t + 1], None, ALU.mult).then_inc(s["x_normed"], 1)
                if t == 7:
                    low_part(0)
                if t in (3, 7):
                    dve.wait_ge(s["x_turned"], t + 1)
                    cols = slice(HALF * (t // 4), HALF * (t // 4) + HALF)
                    for k in range(KD):
                        dve.wait_ge(s["h_act"], KD * (t // 4) + k + 1)
                        dve.scalar_tensor_tensor(out=hT_lo(k)[:, cols], in0=ps[:, k, :], scalar=attn_g[:, k:k + 1],
                                                 in1=hT_hi[:, k, cols].bitcast(f32), op0=ALU.mult, op1=ALU.subtract).then_inc(s["h_dve"], 1)
                if t == 7:
                    low_part(1)
            dve.wait_ge(s["small_in"], 80)
            lv = lam_in.rearrange("p (a d) -> p a d", a=4)
            link(dve.tensor_tensor(lv[:, 0, :], lv[:, 0, :], lv[:, 1, :], ALU.mult))
            link(dve.tensor_tensor(lv[:, 2, :], lv[:, 2, :], lv[:, 3, :], ALU.mult))
            link(dve.reduce_sum(lam[:, 0:1], lv[:, 0, :], axis=AX.X))
            link(dve.reduce_sum(lam[:, 1:2], lv[:, 2, :], axis=AX.X))
            link(dve.tensor_scalar(sub_g[:, :], sub_g[:, :], 1.0 - LAM_INIT, None, ALU.mult))
            assert chain[0] == DOT_LINKS + 1
            for g in range(1, NG, 2):
                if g >= 3 and g - 2 in last_of[0:8]:
                    low_part(last_of.index(g - 2) + 2)
                dve.wait_ge(s["proj_done"], g + 1)
                if groups[g][1] == "line":
                    dve.wait_ge(s["lists_blank"], 64)
                if groups[g][1] == "mem":
                    k = groups[g][2]
                    dve.tensor_tensor(group_dest(g), group_source(g), mem_g[:, k:k + 2].unsqueeze(2).broadcast_to((P, 2, MEM)), ALU.mult)\
                        .then_inc(s["proj_dve"], 1)
                elif groups[g][1] == "line":
                    dve.tensor_scalar(group_dest(g), group_source(g), 1.0 / SCALE, None, ALU.mult).then_inc(s["proj_dve"], 1)
                else:
                    dve.tensor_copy(group_dest(g), group_source(g)).then_inc(s["proj_dve"], 1)
                if g == conv_ready + 2:
                    dve.wait_ge(s["proj_act"], 6)
                    dve.wait_ge(s["proj_dve"], 6)
                    for c in range(2):
                        link(dve.tensor_tensor(conv_u[:, c, :], conv_u[:, c, :], conv_c[:, c, :], ALU.mult))
                        link(dve.tensor_scalar(conv_c[:, c, :], conv_u[:, c, :], taps[:, 4 + c:5 + c], None, ALU.mult))
                        for tap in range(2):
                            late = 2 - tap
                            link(dve.scalar_tensor_tensor(out=conv_c[:, c, late:S], in0=conv_u[:, c, 0:S - late],
                                                          scalar=taps[:, 2 * tap + c:2 * tap + c + 1],
                                                          in1=conv_c[:, c, late:S], op0=ALU.mult, op1=ALU.add))
                        link(dve.tensor_tensor(conv_b[:, c, :], conv_b[:, c, :], conv_c[:, c, :], ALU.mult))
                    assert chain[0] == CONV_LINKS
            dve.wait_ge(s["proj_act"], NG // 2)
            link(dve.tensor_scalar(bguT[:, :, 8:16], bguT[:, :, 8:16], 1.0, None, ALU.add))

            for i in range(NT + 2):
                if i < NT:
                    dve.wait_ge(s["ms_done"], i + 1)
                    link(dve.tensor_reduce(m_max[:, i % 2, :], ps[:, 2 * (i % 2):2 * (i % 2) + 2, :].rearrange("p b (a n) -> p (b a) n", a=2),
                                           axis=AX.X, op=ALU.max))
                    if i >= 2:
                        dve.wait_ge(s["ms_exp"], 4 * (i - 1))
                    dve.tensor_scalar(m_neg[:, i % 2, :], m_max[:, i % 2, :], -SCALE, None, ALU.mult).then_inc(s["ms_max"], 1)
                    dve.wait_ge(s["ms_exp"], 4 * (i + 1))
                    link(dve.reciprocal(m_inv[:, i % 2, :], m_sum[:, i % 2, :]))
                    pv = wk[:, i % 2, :].rearrange("p (h n) -> p h n", h=HEADS)
                    dve.tensor_tensor(pv, pv, m_inv[:, i % 2, :].unsqueeze(2).broadcast_to((P, HEADS, MEM)), ALU.mult).then_inc(s["ms_prob"], 1)
                if 1 <= i <= NT:
                    j = i - 1
                    dve.wait_ge(s["ms_turned"], j + 1)
                    if j >= 2:
                        dve.wait_ge(s["ms_av"], j - 1)
                    dve.tensor_copy(wk[:, 2 + j % 2, 512:1024], ps[:, 5, :]).then_inc(s["ms_t_dve"], 1)
                if i >= 2:
                    j = i - 2
                    dve.wait_ge(s["ms_av"], j + 1)
                    dve.tensor_copy(mixT[:, 6:8, P * j:P * j + P], ps[:, 6 + j % 2, 0:256].rearrange("p (c t) -> p c t", c=2)).then_inc(s["ms_out"], 1)

            dve.wait_ge(s["lam_exp"], 1)
            link(dve.tensor_tensor(lam[:, 4:5], lam[:, 3:4], lam[:, 2:3], ALU.subtract))
            link(dve.tensor_scalar(lam[:, 5:6], lam[:, 4:5], -LAM_INIT, None, ALU.add))
            NU = NT * HEADS
            dve.wait_ge(s["ms_av"], NT)
            def scores_read(j, c):
                i, h = divmod(j, HEADS)
                kv = P * (i + 1)
                dve.wait_ge(s["ds_done"], 2 * j + c + 1)
                if j >= 2:
                    dve.wait_ge(s["ds_turned"], j - 1)
                sc = wk[:, 2 * (j % 2) + c, 0:kv]
                raw = ps[:, 2 * c:2 * c + 2, :].rearrange("p b n -> p (b n)")[:, 0:kv]
                dve.tensor_tensor_reduce(sc, raw, master[:, h, S - kv:S], scale=-SCALE, scalar=3e38, op0=ALU.add, op1=ALU.min,
                                         accum_out=d_neg[:, j % 2, c:c + 1]).then_inc(s["ds_read"], 1)

            def difference(n):
                kv = P * (n // HEADS + 1)
                dve.wait_ge(s["ds_exp"], 2 * n + 2)
                if n >= 3:
                    dve.wait_ge(s["ds_out"], n - 2)
                link(dve.reciprocal(d_inv[:, n % 3, :], d_sum[:, n % 2, :]))
                link(dve.scalar_tensor_tensor(out=d_lam[:, n % 2:n % 2 + 1], in0=d_sum[:, n % 2, 0:1], scalar=lam[:, 5:6],
                                              in1=d_inv[:, n % 3, 1:2], op0=ALU.mult, op1=ALU.mult))
                p0, p1 = wk[:, 2 * (n % 2), 0:kv], wk[:, 2 * (n % 2) + 1, 0:kv]
                dve.scalar_tensor_tensor(out=p0, in0=p1, scalar=d_lam[:, n % 2:n % 2 + 1], in1=p0, op0=ALU.mult, op1=ALU.add)\
                    .then_inc(s["ds_diff"], 1)

            for j in range(NU + 1):
                if j < NU:
                    scores_read(j, 0)
                if j >= 1:
                    difference(j - 1)
                if j < NU:
                    scores_read(j, 1)
                if NU - 15 <= j <= NU:
                    q, part = divmod(j - (NU - 15), 4)
                    cols = slice(HALF * part, HALF * part + HALF)
                    dve.wait_ge(s["wo_high"], j - (NU - 15) + 1)
                    dve.tensor_tensor(w_lo_r[:, q, cols], ring[:, q, cols], w_out_hi(q)[:, cols].bitcast(f32), ALU.subtract)\
                        .then_inc(s["wo_split"], 1)

            dve.wait_ge(s["ds_sq"], NU + 1)
            link(dve.reciprocal(o_rs[:, :], o_std[:, :]))

            def norm_heads(i):
                ov = o_all[:, i, :].rearrange("p (h n) -> p h n", h=HEADS)
                link(dve.tensor_tensor(ov, ov, o_rs[:, HEADS * i:HEADS * i + HEADS].unsqueeze(2).broadcast_to((P, HEADS, VD)), ALU.mult))
                dve.tensor_tensor(ov, ov, sub_g[:, :].unsqueeze(1).broadcast_to((P, HEADS, VD)), ALU.mult).then_inc(s["e_y"], 1)

            def ranks_read(j):
                dve.wait_ge(s["e_rank"], j + 1)
                dve.tensor_copy(place[:, :], ps[:, 5, 0:EXPERTS]).then_inc(s["e_rank_read"], 1)
                dve.wait_ge(s["e_rank_read"], j + 1)

            def mix_low(i):
                dve.wait_ge(s["e_high"], i + 1)
                high, low = mix_parts(i)
                high = high.bitcast(f32)
                dve.tensor_tensor(low[:, 2:6, :], ps[:, 4, :].rearrange("p (h t) -> p h t", h=HEADS), high[:, 2:6, :], ALU.subtract)
                dve.tensor_tensor(low[:, 0:2, :], conv_b[:, :, P * i:P * i + P], high[:, 0:2, :], ALU.subtract)
                dve.tensor_tensor(low[:, 6:8, :], mixT[:, 6:8, P * i:P * i + P], high[:, 6:8, :], ALU.subtract).then_inc(s["e_split"], 1)

            norm_heads(0)
            mix_low(0)
            norm_heads(1)
            mix_low(1)
            norm_heads(2)
            dve.wait_ge(s["consts_made"], 1)
            for i in range(NT + 2):
                if i < NT:
                    if i + 3 < NT:
                        norm_heads(i + 3)
                    dve.wait_ge(s_x[i % 2], 16 * (1 + i // 2 + 1))
                    for half in range(2):
                        dve.wait_ge(s["e_mix"], 2 * i + half + 1)
                        x_half = wk[:, i % 2, HALF * half:HALF * half + HALF]
                        dve.tensor_tensor(x_half, ps[:, 2 * (i % 2) + half, :], x_half, ALU.add).then_inc(s["e_x2"], 1)
                    dve.wait_ge(s["e_x2_sq"], i + 1)
                    link(dve.reciprocal(e_rstd[:, i:i + 1], e_std[:, i:i + 1]))
                    if i >= 2:
                        dve.wait_ge(s[f"xn_out{i % 2}"], 16 * (i // 2))
                        dve.wait_ge(s["e_hT"], i - 1)
                    dve.wait_ge(s["e_x2"], 2 * i + 2)
                    if i == 0:
                        dve.wait_ge(s["gain_in"], 16)
                    dve.scalar_tensor_tensor(out=wk[:, 2 + i % 2, :], in0=wk[:, i % 2, :], scalar=e_rstd[:, i:i + 1], in1=ffn_g,
                                             op0=ALU.mult, op1=ALU.mult).then_inc(s["e_xn"], 1)
                    if i == 0:
                        mix_low(2)
                    j = i
                    dve.wait_ge(s["e_hT"], j + 1)
                    if j >= 1:
                        dve.wait_ge(s["e_log"], j)
                    dve.tensor_copy(h2T[:, 4:8, :], ps[:, 6, :].rearrange("p (k t) -> p k t", t=P)).then_inc(s["e_hT_dve"], 1)
                    if i + 3 < NT:
                        mix_low(i + 3)
                    dve.wait_ge(s["e_log"], j + 1)
                    dve.tensor_tensor(logits[:, :], ps[:, 7, 0:EXPERTS], router_b[:, :], ALU.add).then_inc(s["e_log_read"], 1)
                    dve.wait_ge(s["e_log_read"], j + 1)
                    link(dve.max(top8[:, :], logits[:, :]))
                    link(dve.tensor_scalar(top_neg[:, :], top8[:, 0:1], -1.0, None, ALU.mult))
                    link(dve.max_index(top8i[:, :], top8[:, :], logits[:, :]))
                    link(dve.tensor_copy(top_e[:, j, :], top8i[:, 0:TOPK]))
                    link(dve.tensor_scalar(chosen[:, :], iota_e[:, :], top_e[:, j, 0:1], None, ALU.is_equal))
                    for c in range(1, TOPK):
                        to = chosen_b[:, j, :] if c == TOPK - 1 else chosen[:, :]
                        ins = dve.scalar_tensor_tensor(out=to, in0=iota_e[:, :], scalar=top_e[:, j, c:c + 1], in1=chosen[:, :],
                                                       op0=ALU.is_equal, op1=ALU.add)
                        if c < TOPK - 1:
                            link(ins)
                        else:
                            ins.then_inc(s["e_chosen"], 1)
                    dve.wait_ge(s["e_exp"], j + 1)
                    link(dve.reciprocal(top_inv[:, :], top_sum[:, :]))
                    link(dve.tensor_scalar(pay[:, j, :, 1], top_exp[:, :], top_inv[:, :], None, ALU.mult))
                if 1 <= i <= NT:
                    j = i - 1
                    ranks_read(j)
                    link(dve.scalar_tensor_tensor(out=place[:, :], in0=iota_e[:, :], scalar=float(S), in1=place[:, :], op0=ALU.mult, op1=ALU.add))
                    for c in range(TOPK):
                        ins = dve.scalar_tensor_tensor(out=dest_j[:, c, :], in0=iota_e[:, :], scalar=top_e[:, j, c:c + 1], in1=place[:, :],
                                                       op0=ALU.is_equal, op1=ALU.mult)
                    link(ins)
                    link(dve.reduce_sum(dest_f[:, j, :], dest_j[:, :, :], axis=AX.X))
                    dve.tensor_copy(dest_i[:, j, :], dest_f[:, j, :]).then_inc(s["e_dest"], 1)

            ranks_read(NT)
            cnt, nch, end, start, tmp, oh = (t32[:, n, :] for n in range(6))
            e0 = place[0:64, :]
            jj = iota_p[0:64, :]
            link(dve.tensor_copy(cnt, e0))
            link(dve.tensor_scalar(nch, cnt, float(CAP), 1.0, ALU.is_gt, ALU.add))
            link(dve.scalar_tensor_tensor(out=nch, in0=cnt, scalar=float(2 * CAP), in1=nch, op0=ALU.is_gt, op1=ALU.add))
            link(dve.memset(tmp, 1.0))
            link(dve.tensor_tensor_scan(end, tmp, nch, 0.0, ALU.mult, ALU.add))
            link(dve.tensor_tensor(start, end, nch, ALU.subtract))
            link(dve.tensor_scalar(tmp, end, jj, None, ALU.is_le))
            link(dve.reduce_sum(t1[:, 0:1], tmp, axis=AX.X))
            link(dve.scalar_tensor_tensor(out=tmp, in0=start, scalar=jj, in1=start, op0=ALU.is_le, op1=ALU.mult))
            link(dve.tensor_reduce(t1[:, 1:2], tmp, axis=AX.X, op=ALU.max))
            link(dve.scalar_tensor_tensor(out=oh, in0=iota_e[0:64, :], scalar=t1[:, 0:1], in1=cnt, op0=ALU.is_equal, op1=ALU.mult))
            link(dve.reduce_sum(t1[:, 2:3], oh, axis=AX.X))
            link(dve.tensor_tensor(t1[:, 3:4], jj, t1[:, 1:2], ALU.subtract))
            link(dve.scalar_tensor_tensor(out=t1[:, 4:5], in0=t1[:, 3:4], scalar=-float(CAP), in1=t1[:, 2:3], op0=ALU.mult, op1=ALU.add))
            link(dve.tensor_scalar(t1[:, 4:5], t1[:, 4:5], float(CAP), None, ALU.min))
            link(dve.tensor_scalar(t1[:, 5:6], t1[:, 0:1], float(EXPERTS), None, ALU.is_lt))
            link(dve.scalar_tensor_tensor(out=t1[:, 5:6], in0=jj, scalar=0.0, in1=t1[:, 5:6], op0=ALU.is_ge, op1=ALU.mult))
            link(dve.tensor_tensor(table_f[:, 0:1], t1[:, 0:1], t1[:, 5:6], ALU.mult))
            link(dve.tensor_scalar(t1[:, 6:7], t1[:, 3:4], float(CAP), None, ALU.mult))
            link(dve.scalar_tensor_tensor(out=t1[:, 6:7], in0=t1[:, 0:1], scalar=float(S), in1=t1[:, 6:7], op0=ALU.mult, op1=ALU.add))
            link(dve.tensor_tensor(table_f[:, 1:2], t1[:, 6:7], t1[:, 5:6], ALU.mult))
            link(dve.scalar_tensor_tensor(out=table_f[:, 2:3], in0=t1[:, 4:5], scalar=1.0, in1=t1[:, 5:6], op0=ALU.add, op1=ALU.mult))
            link(dve.tensor_scalar(t1[:, 7:8], t1[:, 4:5], float(SIZES[0]), 1.0, ALU.is_gt, ALU.add))
            for n in SIZES[1:-1]:
                link(dve.scalar_tensor_tensor(out=t1[:, 7:8], in0=t1[:, 4:5], scalar=float(n), in1=t1[:, 7:8], op0=ALU.is_gt, op1=ALU.add))
            link(dve.tensor_tensor(t1[:, 8:9], t1[:, 7:8], t1[:, 5:6], ALU.mult))
            link(dve.tensor_scalar(t1[:, 9:10], end[:, EXPERTS - 1:EXPERTS], jj, float(len(SIZES) + 1), ALU.is_equal, ALU.mult))
            dve.tensor_tensor(table_f[:, 3:4], t1[:, 8:9], t1[:, 9:10], ALU.add).then_inc(s["tab_f"], 1)
            dve.wait_ge(s["tab_ps"], 1)
            dve.tensor_copy(table[:, :], ps[0:4, 4, 0:64]).then_inc(s["tab_made"], 1)
            dve.wait_ge(s["tab_made"], 1)

            def read_x(b, done):
                dve.wait_ge(s_xps[b], done * 2 + 2)
                dve.tensor_copy(xT[:, 4:8, P * b:P * b + P], ps[:, 5, :].rearrange("p (k t) -> p k t", t=P)).then_inc(s_xdve[b], 1)

            def read_y(b, it, alone):
                dve.wait_ge(s_yps[b], it * 2 + 2)
                dve.wait_ge(s["idx_moved"], it + 1)
                dve.wait_ge(s_scatter[b], it * 16)
                dve.tensor_scalar(y_rows[:, b, 512:1024], ps[:, y_bank(b, alone) + 1, :], idx_last[:, b, 1:2], None, ALU.mult).then_inc(s_ydve[b], 1)

            def read_rows(it, size_last, size_next):
                for b in range(BLOCKS):
                    if size_next is not None:
                        with dve.If(size_next > P * b + 1):
                            read_x(b, it + 1)
                        with dve.Else():
                            dve.sem_inc(s_xdve[b], 1)
                    with dve.If(size_last > P * b + 1):
                        read_y(b, it, size_next is None)
                    with dve.Else():
                        dve.sem_inc(s_ydve[b], 1)

            def activations(it, n):
                dve.wait_ge(s["bias_now"], it * 2 + 2)
                for j in range(KD + 1):
                    if j < KD:
                        g, u = gate_b[:, j % 2, 0:n], up_b[:, j % 2, 0:n]
                        dve.wait_ge(s["gate_ready"], it * 8 + (j + 1))
                        dve.wait_ge(s["sig_ready"], it * 8 + 1 + max(j - 1, 0))
                        dve.wait_ge(s["act_ready"], it * 8 + 1 + max(j - 1, 0))
                        dve.tensor_scalar(g, ps[:, j % 2, 0:n], b_now[:, j:j + 1], LIMIT, ALU.add, ALU.min).then_inc(s["gate_read"], 1)
                        dve.wait_ge(s["up_ready"], it * 8 + (j + 1))
                        dve.tensor_scalar(u, ps[:, 2 + j % 2, 0:n], b_now[:, 8 + j:9 + j], LIMIT + 1.0, ALU.add, ALU.min).then_inc(s["up_read"], 1)
                    if j >= 1:
                        m = j - 1
                        g, u, sg = gate_b[:, m % 2, 0:n], up_b[:, m % 2, 0:n], sig_b[:, m % 2, 0:n]
                        dve.wait_ge(s["sig_ready"], it * 8 + 1 + j)
                        dve.wait_ge(s["up_read"], it * 8 + 1 + j)
                        dve.tensor_tensor(sg, g, sg, ALU.mult).then_inc(s["silu"], 1)
                        dve.wait_ge(s["silu"], it * 8 + j)
                        dve.scalar_tensor_tensor(out=actT[:, m, 0:n], in0=u, scalar=1.0 - LIMIT, in1=sg, op0=ALU.max, op1=ALU.mult)\
                            .then_inc(s["act_ready"], 1)

            def down_part(it, n):
                for m in range(1, KD, 2):
                    dve.wait_ge(s["down_ready"], it * 8 + (m + 1))
                    dve.tensor_scalar(yT[:, m, 0:n], ps[:, m % 4, 0:n], b_now[:, 16 + m:17 + m], None, ALU.add).then_inc(s["yT_dve"], 1)

            for b in range(BLOCKS):
                read_x(b, 0)
            for name in ("gate_read", "up_read", "act_ready"):
                dve.sem_inc(s[name], 1)
            dve.sem_inc(s["yT_dve"], 2)
            with dve.Fori(0, MAX_ITEMS + 1) as it:
                kind_now = dve.value_load(table[3:4, bass.ds(it + 1, 1)], min_val=0, max_val=len(SIZES) + 1)
                with dve.If(kind_now > 0):
                    e = dve.value_load(table[0:1, bass.ds(it + 1, 1)], min_val=0, max_val=EXPERTS - 1)
                    size_last = dve.value_load(table[2:3, bass.ds(it, 1)], min_val=0, max_val=CAP + 1)
                    size_next = dve.value_load(table[2:3, bass.ds(it + 2, 1)], min_val=0, max_val=CAP + 1)
                    dve.wait_ge(s["yT_act"], it * 4 + 2)
                    dve.wait_ge(s["yT_dve"], it * 4 + 2)
                    dve.tensor_copy(b_now[:, 0:16], bguT[:, bass.ds(e, 1), :].rearrange("p e m -> p (e m)")).then_inc(s["bias_now"], 1)
                    dve.tensor_copy(b_now[:, 16:24], bdnT[:, bass.ds(e, 1), :].rearrange("p e m -> p (e m)")).then_inc(s["bias_now"], 1)

                    def item(n):
                        if n > 0:
                            activations(it, n)
                            read_rows(it, size_last, size_next)
                            down_part(it, n)
                        else:
                            read_rows(it, size_last, None)

                    for_size(dve, kind_now, item)
            dve.wait_ge(s_gf, 16)
            for t in range(NT):
                dve.wait_ge(s_fsq, t + 1)
                link(dve.reciprocal(e_rstd[:, t:t + 1], e_std[:, t:t + 1]))
                dve.scalar_tensor_tensor(out=wk[:, t % 4, :], in0=wk[:, t % 4, :], scalar=e_rstd[:, t:t + 1], in1=wk[:, 5, :],
                                         op0=ALU.mult, op1=ALU.mult).then_inc(s_fdone, 1)


_INS = ["x", "mem", "rel_bias", "attn_norm_g", "w_mix_in", "conv_w", "lambda_qk", "diff_subln_g", "mem_norm_g",
        "w_mem_kv", "w_mix_out", "ffn_norm_g", "router_w", "router_b", "w_gate_up", "b_gate_up", "w_down", "b_down",
        "final_norm_g"]


def kernel(**inputs):
    import concourse.bacc as _bacc
    from concourse.bass_utils import run_bass_kernel_spmd as _run

    nc = _bacc.Bacc("TRN2", target_bir_lowering=False, num_devices=1)
    arrays, aps = {}, {}
    for name in _INS:
        arrays[f"in_{name}"] = np.ascontiguousarray(inputs[name])
    arrays["in_distance_one_hot"] = distance_one_hot()
    for key, value in arrays.items():
        aps[key[3:]] = nc.dram_tensor(key, value.shape, mybir.dt.from_np(value.dtype), kind="ExternalInput").ap()
    out = nc.dram_tensor("out_rows", (1, S, D), f32, kind="ExternalOutput").ap()
    hymba_kernel(nc, aps, out)
    r = _run(nc, [arrays], core_ids=[0])
    return r.results[0]["out_rows"]
```
